# Optimizing a Trainium2 kernel written in Bass

```python
import jax, jax.numpy as jnp
from jax import lax
import numpy as np

D_MODEL = 1024
BATCH = 1
SEQ = 512
DEPTH = 2

CHUNK = 64
N_META = 16
D_FF = 4 * D_MODEL
EPS = 1e-5

CONV_DIM = D_MODEL // 2
CONV_WIDTH = 31
POOL_DIM = D_MODEL // 2
POOL_WINDOWS = (2, 4, 8, 16)
POOL_GROUP = POOL_DIM // len(POOL_WINDOWS)
EVEN_IN = 2 * CONV_DIM + POOL_DIM
EVEN_MIX = CONV_DIM + POOL_DIM

GLA_HEADS = 4
GLA_DK = D_MODEL // 2
GLA_DV = D_MODEL
GLA_HK = GLA_DK // GLA_HEADS
GLA_HV = GLA_DV // GLA_HEADS
GLA_GATE_RANK = 16
GLA_GATE_NORM = 16.0
ODD_IN = 2 * GLA_DK + 2 * GLA_DV + GLA_GATE_RANK

N_EVEN = (DEPTH + 1) // 2
N_ODD = DEPTH // 2

kernel_name = "hybrid_conv_pool_gla_trunk"

def rms_norm(x, g):
    xf = x.astype(jnp.float32)
    y = xf * lax.rsqrt(jnp.mean(xf * xf, axis=-1, keepdims=True) + EPS)
    return (y * g.astype(jnp.float32)).astype(x.dtype)

def layer_norm(x, g, b):
    xf = x.astype(jnp.float32)
    mu = jnp.mean(xf, axis=-1, keepdims=True)
    xc = xf - mu
    y = xc * lax.rsqrt(jnp.mean(xc * xc, axis=-1, keepdims=True) + EPS)
    return (y * g.astype(jnp.float32) + b.astype(jnp.float32)).astype(x.dtype)

def causal_depthwise_conv(u, w, b):
    c = u.shape[-1]
    lhs = jnp.pad(u, ((0, 0), (CONV_WIDTH - 1, 0), (0, 0)))
    out = lax.conv_general_dilated(
        lhs, w[:, None, :].astype(u.dtype), window_strides=(1,), padding="VALID",
        dimension_numbers=("NWC", "WIO", "NWC"), feature_group_count=c)
    return out + b.astype(u.dtype)

def trailing_mean_minus_self(u, window):
    L = u.shape[1]
    uf = u.astype(jnp.float32)
    csum = jnp.cumsum(uf, axis=1)
    cpad = jnp.pad(csum, ((0, 0), (1, 0), (0, 0)))
    lower = jnp.pad(cpad[:, :L - window + 1], ((0, 0), (window - 1, 0), (0, 0)))
    count = jnp.minimum(jnp.arange(L) + 1, window).astype(jnp.float32)[None, :, None]
    return ((csum - lower) / count - uf).astype(u.dtype)

def conv_pool_mixer(h, w_in, conv_w, conv_b, ln_g, ln_b, pool_w, pool_scale, w_out):
    bsz, L, _ = h.shape
    z = h @ w_in
    a_in, p_in = z[..., :2 * CONV_DIM], z[..., 2 * CONV_DIM:]
    a = a_in[..., :CONV_DIM] * jax.nn.sigmoid(a_in[..., CONV_DIM:])
    a = causal_depthwise_conv(a, conv_w, conv_b)
    a = jax.nn.silu(layer_norm(a, ln_g, ln_b))
    groups = [trailing_mean_minus_self(p_in[..., i * POOL_GROUP:(i + 1) * POOL_GROUP], w)
              for i, w in enumerate(POOL_WINDOWS)]
    p = jnp.stack(groups, axis=2)
    p = jnp.einsum("blgc,gcd->blgd", p, pool_w).reshape(bsz, L, POOL_DIM) * pool_scale
    return jnp.concatenate([a, p], axis=-1) @ w_out

def gla_mixer(h, w_in, gate_w2, gate_b, head_g, w_out):
    bsz, L, _ = h.shape
    z = h @ w_in
    split_at = np.cumsum([GLA_DK, GLA_DK, GLA_DV, GLA_DV]).tolist()
    q, k, v, g, r = jnp.split(z, split_at, axis=-1)
    log_a = jax.nn.log_sigmoid((r @ gate_w2 + gate_b).astype(jnp.float32)) / GLA_GATE_NORM
    pad = (-L) % CHUNK
    n_chunks = (L + pad) // CHUNK

    def to_chunks(t, hd):
        t = jnp.pad(t.astype(jnp.float32), ((0, 0), (pad, 0), (0, 0)))
        return t.reshape(bsz, n_chunks, CHUNK, GLA_HEADS, hd).transpose(1, 0, 3, 2, 4)

    qc = to_chunks(q * (GLA_HK ** -0.5), GLA_HK)
    kc = to_chunks(k, GLA_HK)
    vc = to_chunks(v, GLA_HV)
    lac = to_chunks(log_a, GLA_HK)
    cum = jnp.cumsum(lac, axis=3)
    total = cum[:, :, :, -1]
    k_dec = kc * jnp.exp(total[:, :, :, None, :] - cum)

    def step(state, inp):
        q_i, k_i, v_i, tot_i = inp
        state = jnp.exp(tot_i)[..., None] * state + jnp.einsum("bhck,bhcv->bhkv", k_i, v_i)
        o_i = jnp.einsum("bhck,bhkv->bhcv", q_i, state)
        return state, o_i

    s0 = jnp.zeros((bsz, GLA_HEADS, GLA_HK, GLA_HV), jnp.float32)
    _, o = lax.scan(step, s0, (qc, k_dec, vc, total))
    o = o.transpose(1, 0, 3, 2, 4).reshape(bsz, n_chunks * CHUNK, GLA_HEADS, GLA_HV)[:, pad:]
    o = rms_norm(o, head_g).reshape(bsz, L, GLA_DV)
    o = o * jax.nn.silu(g.astype(jnp.float32))
    return o.astype(h.dtype) @ w_out

def squared_relu_mlp(u, w1, w2):
    a = jax.nn.relu(u @ w1)
    return (a * a) @ w2

def setup_inputs(seed: int = 0) -> dict:
    key = jax.random.key(seed)
    ks = jax.random.split(key, 21)
    f32 = jnp.float32
    nrm = lambda k, shape, scale: jax.random.normal(k, shape, f32) * scale
    return {
        "x": nrm(ks[0], (BATCH, SEQ, D_MODEL), 1.0),
        "meta_tokens": nrm(ks[1], (N_META, D_MODEL), 1.0),
        "mix_norm_g": 1.0 + nrm(ks[2], (DEPTH, D_MODEL), 0.02),
        "ffn_norm_g": 1.0 + nrm(ks[3], (DEPTH, D_MODEL), 0.02),
        "ffn_w1": nrm(ks[4], (DEPTH, D_MODEL, D_FF), D_MODEL ** -0.5),
        "ffn_w2": nrm(ks[5], (DEPTH, D_FF, D_MODEL), D_FF ** -0.5),
        "cp_w_in": nrm(ks[6], (N_EVEN, D_MODEL, EVEN_IN), D_MODEL ** -0.5),
        "cp_conv_w": nrm(ks[7], (N_EVEN, CONV_WIDTH, CONV_DIM), CONV_WIDTH ** -0.5),
        "cp_conv_b": nrm(ks[8], (N_EVEN, CONV_DIM), 0.02),
        "cp_ln_g": 1.0 + nrm(ks[9], (N_EVEN, CONV_DIM), 0.02),
        "cp_ln_b": nrm(ks[10], (N_EVEN, CONV_DIM), 0.02),
        "cp_pool_w": nrm(ks[11], (N_EVEN, len(POOL_WINDOWS), POOL_GROUP, POOL_GROUP), POOL_GROUP ** -0.5),
        "cp_pool_scale": 1.0 + nrm(ks[12], (N_EVEN, POOL_DIM), 0.02),
        "cp_w_out": nrm(ks[13], (N_EVEN, EVEN_MIX, D_MODEL), EVEN_MIX ** -0.5),
        "gla_w_in": nrm(ks[14], (N_ODD, D_MODEL, ODD_IN), D_MODEL ** -0.5),
        "gla_gate_w2": nrm(ks[15], (N_ODD, GLA_GATE_RANK, GLA_DK), GLA_GATE_RANK ** -0.5),
        "gla_gate_b": nrm(ks[16], (N_ODD, GLA_DK), 0.02),
        "gla_head_g": 1.0 + nrm(ks[17], (N_ODD, GLA_HV), 0.02),
        "gla_w_out": nrm(ks[18], (N_ODD, GLA_DV, D_MODEL), GLA_DV ** -0.5),
        "final_norm_g": 1.0 + nrm(ks[19], (D_MODEL,), 0.02),
    }

def reference(x, meta_tokens, mix_norm_g, ffn_norm_g, ffn_w1, ffn_w2, cp_w_in, cp_conv_w,
              cp_conv_b, cp_ln_g, cp_ln_b, cp_pool_w, cp_pool_scale, cp_w_out, gla_w_in,
              gla_gate_w2, gla_gate_b, gla_head_g, gla_w_out, final_norm_g):
    bsz = x.shape[0]
    meta = jnp.broadcast_to(meta_tokens[None].astype(x.dtype), (bsz, N_META, D_MODEL))
    h = jnp.concatenate([meta, x], axis=1)
    for i in range(DEPTH):
        j = i // 2
        u = rms_norm(h, mix_norm_g[i])
        if i % 2 == 0:
            h = h + conv_pool_mixer(u, cp_w_in[j], cp_conv_w[j], cp_conv_b[j], cp_ln_g[j],
                                    cp_ln_b[j], cp_pool_w[j], cp_pool_scale[j], cp_w_out[j])
        else:
            h = h + gla_mixer(u, gla_w_in[j], gla_gate_w2[j], gla_gate_b[j], gla_head_g[j],
                              gla_w_out[j])
        u = rms_norm(h, ffn_norm_g[i])
        h = h + squared_relu_mlp(u, ffn_w1[i], ffn_w2[i])
    return rms_norm(h[:, N_META:], final_norm_g)


_drawn_inputs = setup_inputs


def setup_inputs(seed=0):
    import zlib

    import numpy as np

    out = dict(_drawn_inputs(seed))
    spreads = {}
    factors = {'cp_conv_b': 3.287,
     'cp_ln_g': 5.285,
     'cp_ln_b': 5.55,
     'cp_pool_scale': 4.45,
     'gla_gate_b': 8.0,
     'gla_head_g': 31.512,
     'final_norm_g': 8.083,
     'ffn_norm_g': 4.63}
    for name, (base, spread) in spreads.items():
        noise = np.random.default_rng([zlib.crc32(name.encode()), seed]).standard_normal(out[name].shape)
        drawn = base * np.exp(spread * noise) if base else spread * noise
        out[name] = __import__('jax').numpy.asarray(drawn.astype(out[name].dtype))
    for name, factor in factors.items():
        out[name] = (out[name] * factor).astype(out[name].dtype)
    return out
```

```python
from contextlib import ExitStack

import concourse.bass as bass
from concourse import mybir

F32 = mybir.dt.float32
F32R = mybir.dt.float32r
ALU = mybir.AluOpType
ACT = mybir.ActivationFunctionType

P = 128
EPS = 1e-5
META = 16
SEQ = 512
TOK = META + SEQ
D = 1024
KD = D // P
FF = 4 * D
FBLK = FF // D
CONV = 512
CT = CONV // P
TAPS = 31
PG = 4
WMAX = 16
HEADS = 4
DK = 512
HK = DK // HEADS
DV = 1024
HV = DV // HEADS
RANK = 16
GATE_NORM = 16.0
CHUNK = 64
NCH = SEQ // CHUNK + 1
TT = SEQ // P
NS = 4
BANK = 512
SPLIT = META + 2 * P
C0 = BANK - SPLIT
V_MIX, V_FFN, V_FIN = 0, 2 * KD, 4 * KD
V_CB = V_FIN + KD
V_LG, V_LB, V_PS, V_GB = V_CB + CT, V_CB + 2 * CT, V_CB + 3 * CT, V_CB + 4 * CT
V_HG = V_GB + DK // P
NV = V_HG + HV // P
B_GLU, B_POOL = 0, CT
B_OUTP = B_POOL + 2
B_OUTC = B_OUTP + 2
B_F0 = B_OUTC + 2
B_V = B_F0 + 8 * FBLK
B_K, B_Q, B_G = B_V + 4, B_V + 6, B_V + 8
B_OUT1 = B_G + 4
B_F1 = B_OUT1 + 4
NB = B_F1 + 8 * FBLK


def plan_slots():
    order = [("vec",)] + [("x", k) for k in range(KD)]
    order += [("glu", 0), ("stat", 0)] + [("glu", n) for n in range(1, 2 * CT)]
    order += [("p", g) for g in range(PG)] + [("mix", g) for g in range(PG)]
    order += [("outp", k) for k in range(KD)] + [("mean",), ("var",)]
    order += [("outc", k) for k in range(KD)]
    slot = {}

    def add(names):
        for n in names:
            slot[n] = len(slot)

    def ffn(layer, norm):
        for fb in range(FBLK):
            for i in range(2 * KD):
                yield ("ffn", layer, fb, i)
                if fb == 0 and i == 0:
                    yield ("stat", norm)
                if layer == 1 and fb == FBLK - 1 and i > KD:
                    yield ("y", i - KD - 1)
        if layer == 1:
            yield ("tstat", 4)
            yield ("y", KD - 1)

    add(order)
    add(ffn(0, 1))
    add([("r",), ("stat", 2), ("tstat", 2)])
    for b in range(4):
        add(("v", b, t) for t in range(TT + 1))
        if b == 0:
            add(("gate", n) for n in range(HEADS))
    for h in range(HEADS):
        add([("k", h)] + ([("kt", h - 1)] if h else []))
    add([("q", 0), ("kt", HEADS - 1), ("q", 1), ("q", 2), ("kv", 0), ("q", 3), ("kv", 1)])
    for i in range(KD):
        add([("g", i), ("o", i + 1)] + ([("kv", i + 2)] if i + 2 < NCH else []))
        if i >= 2 and i % 2 == 0:
            add([("hn", i // 2 - 1)])
    add([("hn", TT - 1)])
    add(("out1", k) for k in range(KD))
    add(ffn(1, 3))
    return slot


SLOT = plan_slots()


def half_reader(n):
    b, j = divmod(n, 2)
    if b < B_POOL:
        return SLOT["glu", n]
    if b < B_OUTP:
        return SLOT["p", n - 2 * B_POOL]
    if b < B_OUTC:
        return SLOT["outp", 2 * (n - 2 * B_OUTP) + 1]
    if b < B_F0:
        return SLOT["outc", 2 * (n - 2 * B_OUTC) + 1]
    if b < B_V:
        return SLOT["ffn", 0, (b - B_F0) // 8, (n - 2 * B_F0) % 16]
    if b < B_K:
        return SLOT["v", b - B_V, TT]
    if b < B_Q:
        return SLOT["k", n - 2 * B_K]
    if b < B_G:
        return SLOT["q", n - 2 * B_Q]
    if b < B_OUT1:
        return SLOT["g", n - 2 * B_G]
    if b < B_F1:
        return SLOT["out1", n - 2 * B_OUT1]
    return SLOT["ffn", 1, (b - B_F1) // 8, (n - 2 * B_F1) % 16]


def raw_count(b):
    return 16 * (b // 2 + 1 + min(b // 2 + 1, B_POOL // 2))


def half_reader(n):
    b, j = divmod(n, 2)
    if b < B_POOL:
        return SLOT["glu", n]
    if b < B_OUTP:
        return SLOT["p", n - 2 * B_POOL]
    if b < B_OUTC:
        return SLOT["outp", 2 * (n - 2 * B_OUTP) + 1]
    if b < B_F0:
        return SLOT["outc", 2 * (n - 2 * B_OUTC) + 1]
    if b < B_V:
        return SLOT["ffn", 0, (b - B_F0) // 8, (n - 2 * B_F0) % 16]
    if b < B_K:
        return SLOT["v", b - B_V, TT]
    if b < B_Q:
        return SLOT["k", n - 2 * B_K]
    if b < B_G:
        return SLOT["q", n - 2 * B_Q]
    if b < B_OUT1:
        return SLOT["g", n - 2 * B_G]
    if b < B_F1:
        return SLOT["out1", n - 2 * B_OUT1]
    return SLOT["ffn", 1, (b - B_F1) // 8, (n - 2 * B_F1) % 16]


def raw_count(b):
    return 16 * (b // 2 + 1 + min(b // 2 + 1, B_POOL // 2))


def half_reader(n):
    b, j = divmod(n, 2)
    if b < B_POOL:
        return SLOT["glu", n]
    if b < B_OUTP:
        return SLOT["p", n - 2 * B_POOL]
    if b < B_OUTC:
        return SLOT["outp", 2 * (n - 2 * B_OUTP) + 1]
    if b < B_F0:
        return SLOT["outc", 2 * (n - 2 * B_OUTC) + 1]
    if b < B_V:
        return SLOT["ffn", 0, (b - B_F0) // 8, (n - 2 * B_F0) % 16]
    if b < B_K:
        return SLOT["v", b - B_V, TT]
    if b < B_Q:
        return SLOT["k", n - 2 * B_K]
    if b < B_G:
        return SLOT["q", n - 2 * B_Q]
    if b < B_OUT1:
        return SLOT["g", n - 2 * B_G]
    if b < B_F1:
        return SLOT["out1", n - 2 * B_OUT1]
    return SLOT["ffn", 1, (b - B_F1) // 8, (n - 2 * B_F1) % 16]


def raw_count(b):
    return 16 * (b // 2 + 1 + min(b // 2 + 1, B_POOL // 2))


def half_reader(n):
    b, j = divmod(n, 2)
    if b < B_POOL:
        return SLOT["glu", n]
    if b < B_OUTP:
        return SLOT["p", n - 2 * B_POOL]
    if b < B_OUTC:
        return SLOT["outp", 2 * (n - 2 * B_OUTP) + 1]
    if b < B_F0:
        return SLOT["outc", 2 * (n - 2 * B_OUTC) + 1]
    if b < B_V:
        return SLOT["ffn", 0, (b - B_F0) // 8, (n - 2 * B_F0) % 16]
    if b < B_K:
        return SLOT["v", b - B_V, TT]
    if b < B_Q:
        return SLOT["k", n - 2 * B_K]
    if b < B_G:
        return SLOT["q", n - 2 * B_Q]
    if b < B_OUT1:
        return SLOT["g", n - 2 * B_G]
    if b < B_F1:
        return SLOT["out1", n - 2 * B_OUT1]
    return SLOT["ffn", 1, (b - B_F1) // 8, (n - 2 * B_F1) % 16]


def half_freed(n):
    changed = n // 2 in (B_OUTP, B_OUTP + 1, B_F0, B_F0 + 1)
    return half_reader(n - 4 + (1 - n % 2 if changed else 0))


def raw_count(b):
    return 16 * (b // 2 + 1 + min(b // 2 + 1, B_POOL // 2))


def half_reader(n):
    b, j = divmod(n, 2)
    if b < B_POOL:
        return SLOT["glu", n]
    if b < B_OUTP:
        return SLOT["p", n - 2 * B_POOL]
    if b < B_OUTC:
        return SLOT["outp", 2 * (n - 2 * B_OUTP) + 1]
    if b < B_F0:
        return SLOT["outc", 2 * (n - 2 * B_OUTC) + 1]
    if b < B_V:
        return SLOT["ffn", 0, (b - B_F0) // 8, (n - 2 * B_F0) % 16]
    if b < B_K:
        return SLOT["v", b - B_V, TT]
    if b < B_Q:
        return SLOT["k", n - 2 * B_K]
    if b < B_G:
        return SLOT["q", n - 2 * B_Q]
    if b < B_OUT1:
        return SLOT["g", n - 2 * B_G]
    if b < B_F1:
        return SLOT["out1", n - 2 * B_OUT1]
    return SLOT["ffn", 1, (b - B_F1) // 8, (n - 2 * B_F1) % 16]


def half_freed(n):
    changed = n // 2 in (B_OUTP, B_OUTP + 1, B_F0, B_F0 + 1)
    return half_reader(n - 4 + (1 - n % 2 if changed else 0))


def raw_count(b):
    return 16 * (b // 2 + 1 + min(b // 2 + 1, B_POOL // 2))


def half_reader(n):
    b, j = divmod(n, 2)
    if b < B_POOL:
        return SLOT["glu", n]
    if b < B_OUTP:
        return SLOT["p", n - 2 * B_POOL]
    if b < B_OUTC:
        return SLOT["outp", 2 * (n - 2 * B_OUTP) + 1]
    if b < B_F0:
        return SLOT["outc", 2 * (n - 2 * B_OUTC) + 1]
    if b < B_V:
        return SLOT["ffn", 0, (b - B_F0) // 8, (n - 2 * B_F0) % 16]
    if b < B_K:
        return SLOT["v", b - B_V, TT]
    if b < B_Q:
        return SLOT["k", n - 2 * B_K]
    if b < B_G:
        return SLOT["q", n - 2 * B_Q]
    if b < B_OUT1:
        return SLOT["g", n - 2 * B_G]
    if b < B_F1:
        return SLOT["out1", n - 2 * B_OUT1]
    return SLOT["ffn", 1, (b - B_F1) // 8, (n - 2 * B_F1) % 16]


def half_freed(n):
    changed = n // 2 in (B_OUTP, B_OUTP + 1, B_F0, B_F0 + 1)
    return half_reader(n - 4 + (1 - n % 2 if changed else 0))


def raw_count(b):
    return 16 * (b // 2 + 1 + min(b // 2 + 1, B_POOL // 2))


def half_reader(n):
    b, j = divmod(n, 2)
    if b < B_POOL:
        return SLOT["glu", n]
    if b < B_OUTP:
        return SLOT["p", n - 2 * B_POOL]
    if b < B_OUTC:
        return SLOT["outp", 2 * (n - 2 * B_OUTP) + 1]
    if b < B_F0:
        return SLOT["outc", 2 * (n - 2 * B_OUTC) + 1]
    if b < B_V:
        return SLOT["ffn", 0, (b - B_F0) // 8, (n - 2 * B_F0) % 16]
    if b < B_K:
        return SLOT["v", b - B_V, TT]
    if b < B_Q:
        return SLOT["k", n - 2 * B_K]
    if b < B_G:
        return SLOT["q", n - 2 * B_Q]
    if b < B_OUT1:
        return SLOT["g", n - 2 * B_G]
    if b < B_F1:
        return SLOT["out1", n - 2 * B_OUT1]
    return SLOT["ffn", 1, (b - B_F1) // 8, (n - 2 * B_F1) % 16]


def half_freed(n):
    changed = n // 2 in (B_OUTP, B_OUTP + 1, B_F0, B_F0 + 1)
    return half_reader(n - 4 + (1 - n % 2 if changed else 0))


def raw_count(b):
    return 16 * (b // 2 + 1 + min(b // 2 + 1, B_POOL // 2))


def build_trunk(nc, x, meta_tokens, mix_norm_g, ffn_norm_g, ffn_w1, ffn_w2, cp_w_in, cp_conv_w,
                cp_conv_b, cp_ln_g, cp_ln_b, cp_pool_w, cp_pool_scale, cp_w_out, gla_w_in,
                gla_gate_w2, gla_gate_b, gla_head_g, gla_w_out, final_norm_g, out):
    with ExitStack() as ctx:
        def sb(name, shape, dt=F32, stack=ctx):
            return stack.enter_context(nc.sbuf_tensor(name, shape, dt))

        def sem(name):
            return ctx.enter_context(nc.semaphore(name))

        ps = ctx.enter_context(nc.psum_tensor("ps", [P, NS, 2 * BANK], F32))

        h = sb("h", [P, KD, TOK])
        u_hi = sb("u_hi", [P, KD, TOK], F32R)
        u_lo = sb("u_lo", [P, KD, TOK], F32R)
        h_sq = sb("h_sq", [P, 2, TOK])
        sq_sum = sb("sq_sum", [P, TOK])
        std = sb("std", [P, TOK])
        rstd = sb("rstd", [P, TOK])
        std_tok = sb("std_tok", [P, TT + 1])
        rstd_tok = sb("rstd_tok", [P, TT + 1])
        raw = sb("raw", [P, 2, 2 * KD * P])
        w_hi = sb("w_hi", [P, 2, 2 * KD * P], F32R)
        w_lo = sb("w_lo", [P, 2, 2 * KD * P], F32R)
        ident = sb("ident", [P, P])
        ones_d = sb("ones_d", [P, P])
        ones_c = sb("ones_c", [P, P])
        ones_v = sb("ones_v", [P, P])
        eps = sb("eps", [P, 1])
        vec_rows = sb("vec_rows", [NV, P])
        cw_rows = sb("cw_rows", [TAPS * CT, P])
        vec = sb("vec", [P, NV])
        cw = sb("cw", [P, TAPS * CT])
        gw2 = sb("gw2", [RANK, DK])
        rw = sb("rw", [P, KD * RANK])
        rw_hi = sb("rw_hi", [P, (KD - 1) * RANK + P], F32R)
        rw_lo = sb("rw_lo", [P, (KD - 1) * RANK + P], F32R)
        relu = sb("relu", [P, 2, TOK])
        act2 = sb("act2", [P, 2, TOK])

        with ExitStack() as part:
            a_hi = sb("a_hi", [P, KD, TOK], F32R, part)
            a_lo = sb("a_lo", [P, KD, TOK], F32R, part)
            with ExitStack() as mixer0:
                pin = sb("pin", [P, WMAX + TOK], F32, mixer0)
                win = sb("win", [P, 2, WMAX + TOK], F32, mixer0)
                rcount = sb("rcount", [P, WMAX], F32, mixer0)
                pw = sb("pw", [P, PG, P], F32, mixer0)
                pw_hi = sb("pw_hi", [P, PG, P], F32R, mixer0)
                pw_lo = sb("pw_lo", [P, PG, P], F32R, mixer0)
                pd = sb("pd", [P, TOK], F32, mixer0)
                with ExitStack() as start:
                    xin = sb("xin", [P, TT, D], F32, start)
                    xmeta = sb("xmeta", [META, D], F32, start)
                with ExitStack() as rest:
                    conv_in = sb("conv_in", [P, CT, TAPS - 1 + TOK], F32, rest)
                    conv = sb("conv", [P, CT, TOK], F32, rest)
            with ExitStack() as last:
                y_tok = sb("y_tok", [P, TT, D], F32, last)
        with ExitStack() as gla:
            v_tok = sb("v_tok", [P, TT, DV], F32, gla)
            v_meta = sb("v_meta", [META, DV], F32, gla)
            k_tok = sb("k_tok", [P, TT, DK], F32, gla)
            k_meta = sb("k_meta", [META, DK], F32, gla)
            decay = sb("decay", [P, HEADS, TOK], F32, gla)
            gate = sb("gate", [P, KD, SEQ], F32, gla)
            o = sb("o", [P, KD, SEQ], F32, gla)
            state = sb("state", [P, 2, HEADS, HV], F32, gla)
            etot = sb("etot", [P, HEADS, NCH], F32, gla)
        q = decay[:, :, META:]
        mask = state[:, 0, :, :].rearrange("p h v -> p (h v)")[:, 0:TOK]
        logd = o[:, :, :].rearrange("p k t -> p (k t)")[:, 0:HEADS * TOK].rearrange(
            "p (h t) -> p h t", h=HEADS)
        o_sq = relu[:, :, :].rearrange("p a t -> p (a t)")[:, 0:KD * P].rearrange(
            "p (m h t) -> p m h t", m=HV // P, h=HEADS)
        r_sb = relu[0:RANK, 0, :]

        x_loaded = [sem(f"x_loaded{i}") for i in range(4)]
        meta_loaded = sem("meta_loaded")
        vec_loaded = sem("vec_loaded")
        small_loaded = sem("small_loaded")
        raw_loaded = [sem(f"raw_loaded{i}") for i in range(2)]
        consts = sem("consts")
        filled_n = sem("filled")
        evac = [sem(f"evac{i}") for i in range(NS)]
        w_hi_ready = sem("w_hi_ready")
        w_lo_ready = sem("w_lo_ready")
        small_hi = sem("small_hi")
        small_lo = sem("small_lo")
        h_sq_ready = sem("h_sq_ready")
        u_hi_ready = sem("u_hi_ready")
        u_lo_ready = sem("u_lo_ready")
        sq_sum_ready = sem("sq_sum_ready")
        rstd_ready = sem("rstd_ready")
        rstd_tok_ready = sem("rstd_tok_ready")
        sig_ready = sem("sig_ready")
        glu_ready = sem("glu_ready")
        tap_done = sem("tap_done")
        dve_step = sem("dve_step")
        pd_ready = sem("pd_ready")
        pd_hi_ready = sem("pd_hi_ready")
        pd_lo_ready = sem("pd_lo_ready")
        mix_hi_ready = sem("mix_hi_ready")
        centred = sem("centred")
        ln_sq_ready = sem("ln_sq_ready")
        normed = sem("normed")
        silu_ready = sem("silu_ready")
        sq_ready = sem("sq_ready")
        a_hi_ready = sem("a_hi_ready")
        a_lo_ready = sem("a_lo_ready")
        c_hi_ready = sem("c_hi_ready")
        c_lo_ready = sem("c_lo_ready")
        abs_ready = sem("abs_ready")
        gexp_ready = sem("gexp_ready")
        softplus_ready = sem("softplus_ready")
        suffix_ready = sem("suffix_ready")
        decay_ready = sem("decay_ready")
        kscale_ready = sem("kscale_ready")
        gate_ready = sem("gate_ready")
        o_sq_ready = sem("o_sq_ready")
        head_normed = sem("head_normed")
        gated = sem("gated")
        o_hi_ready = sem("o_hi_ready")
        o_lo_ready = sem("o_lo_ready")
        hg_ready = sem("hg_ready")
        act_out = sem("act_out")
        dve_out = sem("dve_out")
        stored = sem("stored")
        N_CONST = 14

        def filled(eng, n, it=0):
            eng.wait_ge(filled_n, n + 1 + 16 * it)

        def evacuated(eng, n, it=0):
            eng.wait_ge(evac[n % NS], n // NS + 1 + 4 * it)

        FULL = (0, TOK)
        FRAMES = (META, TOK)

        def pcols(tokens):
            return (C0, C0 + TOK) if tokens == FULL else (0, SEQ)

        def slot_ap(n, tokens=FULL, rows=P):
            a, b = pcols(tokens)
            return ps[0:rows, n % NS, a:b]

        def half_view(t, n):
            b, j = divmod(n, 2)
            if B_OUTP <= b < B_F0:
                return t[:, b % 2, :].rearrange("p (k n) -> p k n", k=KD // 2)[:, :, 2 * P * j:2 * P * (j + 1)]
            return t[:, b % 2, :].rearrange("p (k n) -> p k n", k=KD)[:, :, P * j:P * (j + 1)]

        def split_hi(n, it=0):
            act = nc.scalar
            act.wait_ge(raw_loaded[n // 2 % 2], raw_count(n // 2) + 64 * it)
            if n >= 4:
                filled(act, half_freed(n), it)
            act.activation(half_view(w_hi, n), half_view(raw, n), ACT.Copy).then_inc(w_hi_ready, 1)

        def split_lo(n, it=0):
            dve = nc.vector
            if n >= 4:
                filled(dve, half_freed(n), it)
            dve.wait_ge(w_hi_ready, n + 1 + 16 * it)
            dve.tensor_tensor(half_view(w_lo, n), half_view(raw, n), half_view(w_hi, n).bitcast(F32),
                              ALU.subtract).then_inc(w_lo_ready, 1)

        block = ctx.enter_context(nc.Block())

        @block.sync
        def _(sp):
            x_v = x[0].rearrange("(j p) d -> p j d", p=P)

            def load_x(c):
                sp.dma_start(xin[:, :, 256 * c:256 * (c + 1)], x_v[:, :, 256 * c:256 * (c + 1)])\
                  .then_inc(x_loaded[c], 16)

            def reusable(b, fb=0):
                if b >= 2:
                    sp.wait_ge(w_lo_ready, 2 * (b - 1) + 16 * fb)

            def load(b, src, fb=0):
                reusable(b, fb)
                sp.dma_start(raw[:, b % 2, :].rearrange("p (k n) -> p k n", n=src.shape[2]), src)\
                  .then_inc(raw_loaded[b % 2], 16)

            cp_in = cp_w_in[0].rearrange("(k p) n -> p k n", p=P)
            cp_out = cp_w_out[0].rearrange("(k p) n -> p k n", p=P)
            gla_in = gla_w_in[0].rearrange("(k p) n -> p k n", p=P)
            gla_out = gla_w_out[0].rearrange("(k p) n -> p k n", p=P)

            def load_glu(c):
                reusable(B_GLU + c)
                for j in range(2):
                    n = 2 * (B_GLU + c) + j
                    sp.dma_start(half_view(raw, n), cp_in[:, :, CONV * j + P * c:CONV * j + P * (c + 1)])\
                      .then_inc(raw_loaded[c % 2], 16)

            def load_ffn(layer, first):
                w1 = ffn_w1[layer].rearrange("(k p) n -> p k n", p=P)
                w2 = ffn_w2[layer].rearrange("(k p) n -> p k n", p=P)
                with sp.Fori(0, FBLK) as fb:
                    for j in range(4):
                        load(first + j, w1[:, :, bass.ds(fb * D + 256 * j, 256)], fb)
                    for j in range(4):
                        load(first + 4 + j, w2[:, bass.ds(fb * KD, KD), 256 * j:256 * (j + 1)], fb)

            load_x(0)
            sp.dma_start(xmeta[:, :], meta_tokens).then_inc(meta_loaded, 16)
            load_x(1)
            load_glu(0)
            load_x(2)
            load_x(3)
            for c in range(1, CT):
                load_glu(c)
            for j in range(2):
                load(B_POOL + j, cp_in[:, :, 2 * CONV + 256 * j:2 * CONV + 256 * (j + 1)])
            for j in range(2):
                load(B_OUTP + j, cp_out[:, KD // 2:, 512 * j:512 * (j + 1)])
            for j in range(2):
                load(B_OUTC + j, cp_out[:, :KD // 2, 512 * j:512 * (j + 1)])
            load_ffn(0, B_F0)
            for b, at, n in ((B_V, 2 * DK, 4), (B_K, DK, 2), (B_Q, 0, 2), (B_G, 2 * DK + DV, 4)):
                for j in range(n):
                    load(b + j, gla_in[:, :, at + 256 * j:at + 256 * (j + 1)])
            for j in range(4):
                load(B_OUT1 + j, gla_out[:, :, 256 * j:256 * (j + 1)])
            load_ffn(1, B_F1)
            out_v = out[0].rearrange("(j p) d -> j p d", p=P)
            for j in range(TT):
                sp.wait_ge((act_out, dve_out)[j % 2], j // 2 + 1)
                sp.dma_start(out_v[j], y_tok[:, j, :]).then_inc(stored, 16)
            sp.wait_ge(stored, 16 * TT)

        @block.gpsimd
        def _(pool):
            pool.memset(ident[:, :], 0.0).then_inc(consts, 1)
            pool.wait_ge(consts, 1)
            pool.affine_select(out=ident[:, :], in_=ident[:, :], compare_op=ALU.not_equal, fill=1.0,
                               base=0, pattern=[[-1, P]], channel_multiplier=1).then_inc(consts, 1)
            pool.memset(ones_d[:, :], 1.0 / D).then_inc(consts, 1)
            pool.memset(ones_c[:, :], 1.0 / CONV).then_inc(consts, 1)
            pool.memset(ones_v[:, :], 1.0 / HV).then_inc(consts, 1)
            pool.memset(eps[:, :], EPS).then_inc(consts, 1)
            pool.memset(pin[:, 0:WMAX], 0.0).then_inc(consts, 1)
            pool.memset(win[:, 0, 0:WMAX], 0.0).then_inc(consts, 1)
            pool.memset(win[:, 1, 0:WMAX], 0.0).then_inc(consts, 1)
            pool.memset(rw_hi[:, KD * RANK:].bitcast(F32), 0.0).then_inc(consts, 1)
            pool.memset(rw_lo[:, KD * RANK:].bitcast(F32), 0.0).then_inc(consts, 1)
            for t in range(WMAX - 1):
                last = pool.memset(rcount[:, t:t + 1], 1.0 / (t + 1))
            last.then_inc(consts, 3)

        @block.scalar
        def _(act):
            at = 0
            for v in (mix_norm_g, ffn_norm_g):
                act.dma_start(vec_rows[at:at + 2 * KD, :], v.rearrange("l (k p) -> (l k) p", p=P))\
                   .then_inc(vec_loaded, 16)
                at += 2 * KD
            act.dma_start(vec_rows[V_FIN:V_FIN + KD, :], final_norm_g.rearrange("(k p) -> k p", p=P))\
               .then_inc(vec_loaded, 16)
            for v, row in ((cp_conv_b, V_CB), (cp_ln_g, V_LG), (cp_ln_b, V_LB), (cp_pool_scale, V_PS),
                           (gla_gate_b, V_GB), (gla_head_g, V_HG)):
                n = v.shape[1] // P
                act.dma_start(vec_rows[row:row + n, :], v[0].rearrange("(k p) -> k p", p=P))\
                   .then_inc(vec_loaded, 16)
            act.dma_start(cw_rows[:, :], cp_conv_w[0].rearrange("t (c p) -> (t c) p", p=P))\
               .then_inc(vec_loaded, 16)
            act.dma_start(pw[:, :, :], cp_pool_w[0].rearrange("g c d -> c g d")).then_inc(small_loaded, 16)
            act.dma_start(rw[:, :].rearrange("p (k r) -> p k r", r=RANK),
                          gla_w_in[0].rearrange("(k p) n -> p k n", p=P)[:, :, 2 * DK + 2 * DV:])\
               .then_inc(small_loaded, 16)
            act.dma_start(gw2[:, :], gla_gate_w2[0]).then_inc(small_loaded, 16)

            def prep(norm, k, n, tokens):
                a, b = tokens
                evacuated(act, n)
                if k >= 2 or norm:
                    act.wait_ge(sq_sum_ready, KD * norm + k - 1)
                act.activation(h_sq[:, k % 2, a:b], h[:, k, a:b], ACT.Square).then_inc(h_sq_ready, 1)
                if norm < 4:
                    g = (V_MIX, V_FFN, V_MIX + KD, V_FFN + KD)[norm] + k
                    act.activation(u_hi[:, k, a:b], h[:, k, a:b], ACT.Copy, scale=vec[:, g:g + 1])\
                       .then_inc(u_hi_ready, 1)

            def stat(norm, tokens):
                n = SLOT["stat", norm]
                filled(act, n)
                act.activation(std[:, tokens[0]:tokens[1]], slot_ap(n, tokens), ACT.Sqrt,
                               bias=eps[:, :]).then_inc(evac[n % NS], 1)

            def tstat(norm):
                n = SLOT["tstat", norm]
                filled(act, n)
                last = act.activation(std_tok[:, 0:TT], ps[:, n % NS, 0:TT], ACT.Sqrt, bias=eps[:, :])
                if norm == 2:
                    last = act.activation(std_tok[0:META, TT:TT + 1], ps[0:META, n % NS, TT:TT + 1],
                                          ACT.Sqrt, bias=eps[0:META, :])
                last.then_inc(evac[n % NS], 1)

            act.wait_ge(consts, N_CONST)
            n = SLOT["vec",]
            filled(act, n)
            act.activation(vec[:, :], ps[:, n % NS, 0:NV], ACT.Copy)
            act.activation(cw[:, :], ps[:, n % NS, BANK:BANK + TAPS * CT], ACT.Copy)\
               .then_inc(evac[n % NS], 1)
            evacuated(act, n)
            for k in range(KD):
                n = SLOT["x", k]
                filled(act, n)
                act.activation(h[:, k, :], slot_ap(n), ACT.Copy).then_inc(evac[n % NS], 1)
                prep(0, k, n, FULL)
                if k % 2:
                    split_hi(k // 2)
            act.wait_ge(small_loaded, 48)
            act.activation(pw_hi[:, :, :], pw[:, :, :], ACT.Copy).then_inc(small_hi, 1)
            act.activation(rw_hi[:, 0:KD * RANK], rw[:, :], ACT.Copy).then_inc(small_hi, 1)
            stat(0, FULL)
            for n in range(2 * CT):
                split_hi(n + 4)
                if n % 2:
                    c = n // 2
                    evacuated(act, SLOT["glu", n])
                    act.activation(act2[:, c % 2, :], relu[:, c % 2, :], ACT.Sigmoid).then_inc(sig_ready, 1)
            for g in range(PG):
                split_hi(2 * B_POOL + g + 4)
                act.wait_ge(pd_ready, g + 1)
                act.activation(a_hi[:, g, :], pd[:, :], ACT.Copy).then_inc(pd_hi_ready, 1)
            for g in range(PG):
                n = SLOT["mix", g]
                filled(act, n)
                act.activation(a_hi[:, PG + g, :], slot_ap(n), ACT.Copy,
                               scale=vec[:, V_PS + g:V_PS + g + 1]).then_inc(mix_hi_ready, 1)
            for n in range(4):
                split_hi(2 * B_OUTC + n)
            ln_work = [relu[:, 0, :], relu[:, 1, :], act2[:, 0, :], act2[:, 1, :]]
            for c in range(CT):
                if c < CT - 1:
                    act.wait_ge(centred, c + 1)
                else:
                    evacuated(act, SLOT["mean",])
                act.activation(ln_work[c], conv[:, c, :], ACT.Square).then_inc(ln_sq_ready, 1)
            n = SLOT["var",]
            filled(act, n)
            act.activation(std[:, :], slot_ap(n), ACT.Sqrt, bias=eps[:, :]).then_inc(evac[n % NS], 1)
            for c in range(CT):
                act.wait_ge(normed, c + 1)
                act.activation(ln_work[c], conv[:, c, :], ACT.Silu, bias=vec[:, V_LB + c:V_LB + c + 1],
                               scale=vec[:, V_LG + c:V_LG + c + 1]).then_inc(silu_ready, 1)
                act.wait_ge(silu_ready, c + 1)
                act.activation(a_hi[:, c, :], ln_work[c], ACT.Copy).then_inc(c_hi_ready, 1)
            for k in range(KD):
                n = SLOT["outc", k]
                if k % 2:
                    split_hi(2 * B_F0 + k // 2)
                prep(1, k, n, FULL)

            def ffn(layer, fb, tokens, it=0):
                a, b = tokens
                for i in range(2 * KD):
                    n = SLOT["ffn", layer, fb, i]
                    w = 2 * (B_F1 if layer else B_F0) + 16 * fb + i + 4
                    if fb == 0 and i == 0:
                        stat(2 * layer + 1, tokens)
                    if i < KD:
                        t = KD * FBLK * layer + KD * fb + i
                        evacuated(act, n, it)
                        if t >= 2:
                            act.wait_ge(a_lo_ready, t - 1 + 8 * it)
                        act.activation(act2[:, i % 2, a:b], relu[:, i % 2, a:b], ACT.Square)\
                           .then_inc(sq_ready, 1)
                        act.wait_ge(sq_ready, t + 1 + 8 * it)
                        act.activation(a_hi[:, i, a:b], act2[:, i % 2, a:b], ACT.Copy)\
                           .then_inc(a_hi_ready, 1)
                    if w < 2 * NB:
                        split_hi(w, it)
                    if i >= KD and fb == FBLK - 1:
                        k = i - KD
                        if layer == 0:
                            prep(2, k, n, FULL)
                            continue
                        prep(4, k, n, FRAMES)
                        if k >= 2:
                            filled(act, SLOT["y", k - 2])
                        act.activation(relu[:, k % 2, a:b], h[:, k, a:b], ACT.Copy,
                                       scale=vec[:, V_FIN + k:V_FIN + k + 1]).then_inc(hg_ready, 1)

            def ffn_all(layer, tokens):
                ffn(layer, 0, tokens)
                with act.Fori(0, FBLK - 2) as it:
                    ffn(layer, 1, tokens, it)
                ffn(layer, FBLK - 1, tokens)

            ffn_all(0, FULL)

            def evac_v(b):
                cols = slice(256 * b, 256 * (b + 1))
                for t in range(TT + 1):
                    n = SLOT["v", b, t]
                    filled(act, n)
                    if t < TT:
                        dst, src, r = v_tok[:, t, cols], ps[:, n % NS, 0:256], rstd_tok[:, t:t + 1]
                    else:
                        dst, src, r = v_meta[:, cols], ps[0:META, n % NS, 0:256], rstd_tok[0:META, TT:TT + 1]
                    act.activation(dst, src, ACT.Copy, scale=r).then_inc(evac[n % NS], 1)
                for j in range(2):
                    split_hi(2 * (B_V + b) + 4 + j)

            stat(2, FULL)
            tstat(2)
            act.wait_ge(rstd_tok_ready, 1)
            evac_v(0)
            for hd in range(HEADS):
                n = SLOT["gate", hd]
                filled(act, n)
                act.activation(decay[:, hd, :], slot_ap(n), ACT.Abs,
                               bias=vec[:, V_GB + hd:V_GB + hd + 1]).then_inc(abs_ready, 1)
            act.wait_ge(abs_ready, HEADS)
            act.activation(decay[:, :, :], decay[:, :, :], ACT.Exp, scale=-1.0).then_inc(gexp_ready, 1)
            act.wait_ge(gexp_ready, 1)
            act.activation(decay[:, :, :], decay[:, :, :], ACT.Ln, bias=1.0).then_inc(softplus_ready, 1)
            evac_v(1)
            evac_v(2)
            for hd in range(HEADS):
                act.wait_ge(suffix_ready, hd + 1)
                act.activation(etot[:, hd, :], decay[:, hd, META - 1::CHUNK], ACT.Exp, scale=1.0 / GATE_NORM)
                act.activation(logd[:, hd, :], logd[:, hd, :], ACT.Exp, scale=1.0 / GATE_NORM)\
                   .then_inc(decay_ready, 1)
            evac_v(3)

            def evac_kt(hd):
                n = SLOT["kt", hd]
                filled(act, n)
                cols = slice(HK * hd, HK * (hd + 1))
                act.activation(k_tok[:, :, cols], ps[:, n % NS, 0:SEQ].rearrange("p (j d) -> p j d", d=HK),
                               ACT.Copy)
                act.activation(k_meta[:, cols], ps[0:META, n % NS, BANK:BANK + HK], ACT.Copy)\
                   .then_inc(evac[n % NS], 1)

            for hd in range(HEADS):
                split_hi(2 * B_K + hd + 4)
                if hd:
                    evac_kt(hd - 1)
            evac_kt(HEADS - 1)
            for hd in range(HEADS):
                split_hi(2 * B_Q + hd + 4)

            def evac_o(c):
                n = SLOT["o", c]
                filled(act, n)
                act.activation(o[:, :, CHUNK * (c - 1):CHUNK * c],
                               ps[:, n % NS, 0:KD * CHUNK].rearrange("p (k t) -> p k t", t=CHUNK),
                               ACT.Copy).then_inc(evac[n % NS], 1)

            def square_o(j):
                evacuated(act, SLOT["o", 2 * j + 2])
                evacuated(act, SLOT["o", 2 * j + 1])
                if j:
                    filled(act, SLOT["hn", j - 1])
                act.activation(o_sq, o[:, :, P * j:P * (j + 1)].rearrange("p (h m) t -> p m h t", m=HV // P),
                               ACT.Square).then_inc(o_sq_ready, 1)

            def head_std(j):
                n = SLOT["hn", j]
                filled(act, n)
                if j:
                    act.wait_ge(head_normed, j)
                act.activation(act2[:, 0, 0:SEQ], ps[:, n % NS, 0:SEQ], ACT.Sqrt, bias=eps[:, :])\
                   .then_inc(evac[n % NS], 1)

            for i in range(KD):
                evacuated(act, SLOT["g", i])
                act.activation(gate[:, i, :], gate[:, i, :], ACT.Silu).then_inc(gate_ready, 1)
                split_hi(2 * B_G + i + 4)
                evac_o(i + 1)
                if i % 2:
                    square_o(i // 2)
                elif i:
                    head_std(i // 2 - 1)
            head_std(TT - 1)
            for k in range(KD):
                act.wait_ge(gated, k + 1)
                act.activation(a_hi[:, k, META:], gate[:, k, :], ACT.Copy).then_inc(o_hi_ready, 1)
            for k in range(KD):
                split_hi(2 * B_OUT1 + k + 4)
                prep(3, k, SLOT["out1", k], FRAMES)
            ffn_all(1, FRAMES)
            tstat(4)
            act.wait_ge(rstd_tok_ready, 2)
            for k in range(KD):
                evacuated(act, SLOT["y", k])
            for j in range(0, TT, 2):
                act.activation(y_tok[:, j, :], y_tok[:, j, :], ACT.Copy, scale=rstd_tok[:, j:j + 1])\
                   .then_inc(act_out, 1)

        @block.vector
        def _(dve):
            V = nc.vector
            steps = [0]

            def step(ins):
                ins.then_inc(dve_step, 1)
                steps[0] += 1
                dve.wait_ge(dve_step, steps[0])

            def prep(norm, k, tokens):
                a, b = tokens
                t = KD * norm + k + 1
                if norm < 4:
                    g = (V_MIX, V_FFN, V_MIX + KD, V_FFN + KD)[norm] + k
                    dve.wait_ge(u_hi_ready, t)
                    V.scalar_tensor_tensor(out=u_lo[:, k, a:b], in0=h[:, k, a:b], scalar=vec[:, g:g + 1],
                                           in1=u_hi[:, k, a:b].bitcast(F32), op0=ALU.mult,
                                           op1=ALU.subtract).then_inc(u_lo_ready, 1)
                dve.wait_ge(h_sq_ready, t)
                if k == 0:
                    V.tensor_copy(sq_sum[:, a:b], h_sq[:, 0, a:b]).then_inc(sq_sum_ready, 1)
                else:
                    dve.wait_ge(sq_sum_ready, t - 1)
                    V.tensor_tensor(sq_sum[:, a:b], sq_sum[:, a:b], h_sq[:, k % 2, a:b], ALU.add)\
                     .then_inc(sq_sum_ready, 1)

            uses = [0]

            def recip(n, tokens):
                evacuated(dve, n)
                V.reciprocal(rstd[:, tokens[0]:tokens[1]], std[:, tokens[0]:tokens[1]])\
                 .then_inc(rstd_ready, 1)
                uses[0] += 1
                dve.wait_ge(rstd_ready, uses[0])

            def recip_tok(norm):
                evacuated(dve, SLOT["tstat", norm])
                last = V.reciprocal(rstd_tok[:, 0:TT], std_tok[:, 0:TT])
                if norm == 2:
                    last = V.reciprocal(rstd_tok[0:META, TT:TT + 1], std_tok[0:META, TT:TT + 1])
                last.then_inc(rstd_tok_ready, 1)

            def scale_out(dst, n, tokens=FULL, rows=P):
                filled(dve, n)
                V.tensor_tensor(dst, slot_ap(n, tokens, rows), rstd[0:rows, tokens[0]:tokens[1]], ALU.mult)\
                 .then_inc(evac[n % NS], 1)

            def add_to_h(k, n, tokens, it=0):
                a, b = tokens
                filled(dve, n, it)
                V.tensor_tensor(h[:, k, a:b], h[:, k, a:b], slot_ap(n, tokens), ALU.add)\
                 .then_inc(evac[n % NS], 1)

            dve.wait_ge(consts, N_CONST)
            for k in range(KD):
                prep(0, k, FULL)
                if k % 2:
                    split_lo(k // 2)
            dve.wait_ge(small_hi, 2)
            V.tensor_tensor(pw_lo[:, :, :], pw[:, :, :], pw_hi[:, :, :].bitcast(F32), ALU.subtract)\
             .then_inc(small_lo, 1)
            V.tensor_tensor(rw_lo[:, 0:KD * RANK], rw[:, :], rw_hi[:, 0:KD * RANK].bitcast(F32),
                            ALU.subtract).then_inc(small_lo, 1)
            filled(dve, SLOT["x", KD - 1])
            V.memset(conv_in[:, :, 0:TAPS - 1], 0.0)
            recip(SLOT["stat", 0], FULL)

            taps = [(c, t) for c in range(CT) for t in range(TAPS)]

            def run_taps(count, tiles):
                while count and taps and taps[0][0] < tiles:
                    c, t = taps.pop(0)
                    count -= 1
                    src, wt = conv_in[:, c, t:t + TOK], cw[:, t * CT + c:t * CT + c + 1]
                    if t == 0:
                        dve.wait_ge(glu_ready, c + 1)
                        V.tensor_scalar(conv[:, c, :], src, wt, vec[:, V_CB + c:V_CB + c + 1],
                                        ALU.mult, ALU.add).then_inc(tap_done, 1)
                    else:
                        dve.wait_ge(tap_done, TAPS * c + t)
                        V.scalar_tensor_tensor(out=conv[:, c, :], in0=src, scalar=wt, in1=conv[:, c, :],
                                               op0=ALU.mult, op1=ALU.add).then_inc(tap_done, 1)

            for c in range(CT):
                n = SLOT["glu", 2 * c]
                scale_out(conv_in[:, c, TAPS - 1:], n)
                split_lo(2 * c + 4)
                run_taps(7, c)
                scale_out(relu[:, c % 2, :], SLOT["glu", 2 * c + 1])
                split_lo(2 * c + 5)
                dve.wait_ge(sig_ready, c + 1)
                evacuated(dve, n)
                V.tensor_tensor(conv_in[:, c, TAPS - 1:], conv_in[:, c, TAPS - 1:], act2[:, c % 2, :],
                                ALU.mult).then_inc(glu_ready, 1)
                run_taps(7, c)
            for g in range(PG):
                n = SLOT["p", g]
                scale_out(pin[:, WMAX:], n)
                split_lo(2 * B_POOL + g + 4)
                evacuated(dve, n)
                src = pin[:, :]
                for j in range(g + 1):
                    back = 1 << j
                    step(V.tensor_tensor(win[:, j % 2, WMAX:], src[:, WMAX:], src[:, WMAX - back:-back],
                                         ALU.add))
                    src = win[:, j % 2, :]
                short = (2 << g) - 1
                step(V.tensor_tensor(pd[:, 0:short], src[:, WMAX:WMAX + short], rcount[:, 0:short], ALU.mult))
                V.tensor_tensor(pd[:, 0:short], pd[:, 0:short], pin[:, WMAX:WMAX + short], ALU.subtract)
                V.scalar_tensor_tensor(out=pd[:, short:], in0=src[:, WMAX + short:], scalar=1.0 / (short + 1),
                                       in1=pin[:, WMAX + short:], op0=ALU.mult, op1=ALU.subtract)\
                 .then_inc(pd_ready, 1)
                run_taps(4, CT)
                dve.wait_ge(pd_hi_ready, g + 1)
                V.tensor_tensor(a_lo[:, g, :], pd[:, :], a_hi[:, g, :].bitcast(F32), ALU.subtract)\
                 .then_inc(pd_lo_ready, 1)
                run_taps(2, CT)
            for g in range(PG):
                n = SLOT["mix", g]
                dve.wait_ge(mix_hi_ready, g + 1)
                V.scalar_tensor_tensor(out=a_lo[:, PG + g, :], in0=slot_ap(n),
                                       scalar=vec[:, V_PS + g:V_PS + g + 1],
                                       in1=a_hi[:, PG + g, :].bitcast(F32), op0=ALU.mult,
                                       op1=ALU.subtract).then_inc(evac[n % NS], 1)
            for k in range(KD):
                add_to_h(k, SLOT["outp", k], FULL)
                if k % 2:
                    split_lo(2 * B_OUTC + k // 2)
                run_taps(8, CT)
            run_taps(len(taps), CT)
            n = SLOT["mean",]
            filled(dve, n)
            for c in range(CT):
                V.tensor_tensor(conv[:, c, :], conv[:, c, :], slot_ap(n), ALU.subtract)\
                 .then_inc(centred if c < CT - 1 else evac[n % NS], 1)
            recip(SLOT["var",], FULL)
            for c in range(CT):
                V.tensor_tensor(conv[:, c, :], conv[:, c, :], rstd[:, :], ALU.mult).then_inc(normed, 1)
            ln_work = [relu[:, 0, :], relu[:, 1, :], act2[:, 0, :], act2[:, 1, :]]
            for c in range(CT):
                dve.wait_ge(c_hi_ready, c + 1)
                V.tensor_tensor(a_lo[:, c, :], ln_work[c], a_hi[:, c, :].bitcast(F32), ALU.subtract)\
                 .then_inc(c_lo_ready, 1)
            for k in range(KD):
                add_to_h(k, SLOT["outc", k], FULL)
                if k % 2:
                    split_lo(2 * B_F0 + k // 2)
                prep(1, k, FULL)

            def ffn(layer, fb, tokens, it=0):
                a, b = tokens
                for i in range(2 * KD):
                    n = SLOT["ffn", layer, fb, i]
                    w = 2 * (B_F1 if layer else B_F0) + 16 * fb + i + 4
                    if fb == 0 and i == 0:
                        recip(SLOT["stat", 2 * layer + 1], tokens)
                    if i < KD:
                        t = KD * FBLK * layer + KD * fb + i
                        filled(dve, n, it)
                        if t >= 2:
                            dve.wait_ge(sq_ready, t - 1 + 8 * it)
                        V.scalar_tensor_tensor(out=relu[:, i % 2, a:b], in0=slot_ap(n, tokens), scalar=0.0,
                                               in1=rstd[:, a:b], op0=ALU.max, op1=ALU.mult)\
                         .then_inc(evac[n % NS], 1)
                        dve.wait_ge(a_hi_ready, t + 1 + 8 * it)
                        V.tensor_tensor(a_lo[:, i, a:b], act2[:, i % 2, a:b], a_hi[:, i, a:b].bitcast(F32),
                                        ALU.subtract).then_inc(a_lo_ready, 1)
                    else:
                        add_to_h(i - KD, n, tokens, it)
                    if w < 2 * NB:
                        split_lo(w, it)
                    if i >= KD and fb == FBLK - 1:
                        k = i - KD
                        prep(2 if layer == 0 else 4, k, tokens)
                        if layer and k:
                            copy_y(k - 1)

            def ffn_all(layer, tokens):
                ffn(layer, 0, tokens)
                with dve.Fori(0, FBLK - 2) as it:
                    ffn(layer, 1, tokens, it)
                ffn(layer, FBLK - 1, tokens)

            def copy_y(k):
                n = SLOT["y", k]
                filled(dve, n)
                V.tensor_copy(y_tok[:, :, P * k:P * (k + 1)],
                              ps[:, n % NS, 0:SEQ].rearrange("p (j d) -> p j d", d=P)).then_inc(evac[n % NS], 1)

            ffn_all(0, FULL)
            recip(SLOT["stat", 2], FULL)
            recip_tok(2)
            scale_out(r_sb, SLOT["r",], FULL, RANK)
            step(V.memset(mask, 1.0))
            V.memset(mask[:, META::CHUNK], 0.0).then_inc(dve_step, 1)
            steps[0] += 1

            def split_v(b):
                for j in range(2):
                    split_lo(2 * (B_V + b) + 4 + j)

            split_v(0)
            for hd in range(HEADS):
                n = SLOT["gate", hd]
                dve.wait_ge(abs_ready, hd + 1)
                V.tensor_scalar(logd[:, hd, :], slot_ap(n), vec[:, V_GB + hd:V_GB + hd + 1], 0.0,
                                ALU.add, ALU.min).then_inc(evac[n % NS], 1)
            split_v(1)
            dve.wait_ge(softplus_ready, 1)
            dve.wait_ge(dve_step, steps[0])
            for hd in range(HEADS):
                evacuated(dve, SLOT["gate", hd])
                ld, cum = logd[:, hd, :], decay[:, hd, :]
                step(V.tensor_tensor(ld, ld, cum, ALU.subtract))
                step(V.tensor_tensor_scan(cum, mask, ld, 0.0, ALU.mult, ALU.add))
                V.tensor_tensor(ld[:, 0:META], cum[:, META - 1:META].to_broadcast([P, META]),
                                cum[:, 0:META], ALU.subtract)
                cf = cum[:, META:].rearrange("p (c t) -> p c t", t=CHUNK)
                V.tensor_tensor(ld[:, META:].rearrange("p (c t) -> p c t", t=CHUNK),
                                cf[:, :, CHUNK - 1:CHUNK].to_broadcast([P, NCH - 1, CHUNK]), cf,
                                ALU.subtract).then_inc(suffix_ready, 1)
            split_v(2)
            for hd in range(HEADS):
                dve.wait_ge(decay_ready, hd + 1)
                V.tensor_tensor(decay[:, hd, :], logd[:, hd, :], rstd[:, :], ALU.mult).then_inc(kscale_ready, 1)
            split_v(3)
            dve.wait_ge(kscale_ready, HEADS)
            for hd in range(HEADS):
                n = SLOT["k", hd]
                filled(dve, n)
                if hd >= 2:
                    filled(dve, SLOT["kt", hd - 2])
                V.tensor_tensor(relu[:, hd % 2, :], slot_ap(n), decay[:, hd, :], ALU.mult)\
                 .then_inc(evac[n % NS], 1)
                split_lo(2 * B_K + hd + 4)

            def update_state(c):
                n = SLOT["kv", c]
                filled(dve, n)
                kv = ps[:, n % NS, :].rearrange("p (h v) -> p h v", h=HEADS)
                if c == 0:
                    V.tensor_copy(state[:, 0, :, :], kv).then_inc(evac[n % NS], 1)
                    return
                evacuated(dve, SLOT["kv", c - 1])
                for hd in range(HEADS):
                    last = V.scalar_tensor_tensor(out=state[:, c % 2, hd, :], in0=state[:, (c - 1) % 2, hd, :],
                                                  scalar=etot[:, hd, c:c + 1], in1=kv[:, hd, :],
                                                  op0=ALU.mult, op1=ALU.add)
                last.then_inc(evac[n % NS], 1)

            for hd in range(HEADS):
                n = SLOT["q", hd]
                filled(dve, n)
                V.scalar_tensor_tensor(out=q[:, hd, :], in0=slot_ap(n, FRAMES), scalar=HK ** -0.5,
                                       in1=rstd[:, META:], op0=ALU.mult, op1=ALU.mult)\
                 .then_inc(evac[n % NS], 1)
                split_lo(2 * B_Q + hd + 4)
                if hd >= 2:
                    update_state(hd - 2)

            def head_norm(j):
                evacuated(dve, SLOT["hn", j])
                step(V.reciprocal(act2[:, 1, 0:SEQ], act2[:, 0, 0:SEQ]))
                r = act2[:, 1, 0:SEQ].rearrange("p (h t) -> p h t", h=HEADS)
                for m in range(HV // P):
                    part = o[:, m::HV // P, P * j:P * (j + 1)]
                    last = V.scalar_tensor_tensor(out=part, in0=part, scalar=vec[:, V_HG + m:V_HG + m + 1],
                                                  in1=r, op0=ALU.mult, op1=ALU.mult)
                last.then_inc(head_normed, 1)

            for i in range(KD):
                scale_out(gate[:, i, :], SLOT["g", i], FRAMES)
                split_lo(2 * B_G + i + 4)
                if i + 2 < NCH:
                    update_state(i + 2)
                if i >= 2 and i % 2 == 0:
                    head_norm(i // 2 - 1)
            head_norm(TT - 1)
            dve.wait_ge(head_normed, TT)

            def rest_of_o(k):
                dve.wait_ge(o_hi_ready, k + 1)
                V.tensor_tensor(a_lo[:, k, META:], gate[:, k, :], a_hi[:, k, META:].bitcast(F32),
                                ALU.subtract).then_inc(o_lo_ready, 1)

            for k in range(KD):
                dve.wait_ge(gate_ready, k + 1)
                V.tensor_tensor(gate[:, k, :], gate[:, k, :], o[:, k, :], ALU.mult).then_inc(gated, 1)
                if k:
                    rest_of_o(k - 1)
            rest_of_o(KD - 1)
            for k in range(KD):
                add_to_h(k, SLOT["out1", k], FRAMES)
                split_lo(2 * B_OUT1 + k + 4)
                prep(3, k, FRAMES)
            ffn_all(1, FRAMES)
            recip_tok(4)
            copy_y(KD - 1)
            dve.wait_ge(rstd_tok_ready, 2)
            for k in range(KD):
                evacuated(dve, SLOT["y", k])
            for j in range(1, TT, 2):
                V.tensor_scalar(y_tok[:, j, :], y_tok[:, j, :], rstd_tok[:, j:j + 1], None, ALU.mult)\
                 .then_inc(dve_out, 1)

        @block.tensor
        def _(pe):
            mm = nc.tensor.matmul

            def start_slot(n, it=0):
                if n >= NS:
                    evacuated(pe, n - NS, it)

            def parts(tokens):
                if tokens == FULL:
                    return ((C0, 0, SPLIT), (BANK, SPLIT, TOK))
                return ((0, META, TOK),)

            def exact(n, lhs, rhs, count, tokens, before=None, it=0):
                start_slot(n, it)
                for k in range(count):
                    if before:
                        before(k)
                    (l_hi, l_lo), (r_hi, r_lo) = lhs(k), rhs(k)
                    for i, (l, r) in enumerate(((l_hi, r_lo), (l_hi, r_hi), (l_lo, r_hi))):
                        for c, a, b in parts(tokens):
                            last = mm(ps[:, n % NS, c:c + b - a], l, r[:, a:b],
                                      start=(k == 0 and i == 0), stop=(k == count - 1 and i == 2))
                last.then_inc(filled_n, 1)

            def plain(n, pairs, tokens):
                for i, (l, r) in enumerate(pairs):
                    for c, a, b in parts(tokens):
                        last = mm(ps[:, n % NS, c:c + b - a], l, r[:, a:b], start=(i == 0),
                                  stop=(i == len(pairs) - 1))
                last.then_inc(filled_n, 1)

            def whalf(w):
                hi, lo = half_view(w_hi, w), half_view(w_lo, w)
                return lambda k: (hi[:, k, 0:P], lo[:, k, 0:P])

            def u(k):
                return u_hi[:, k, :], u_lo[:, k, :]

            def acts(k):
                return a_hi[:, k, :], a_lo[:, k, :]

            def u_wait(norm):
                return lambda k: pe.wait_ge(u_lo_ready, KD * norm + k + 1)

            def project(n, w, tokens, before=None):
                pe.wait_ge(w_lo_ready, w + 1)
                exact(n, whalf(w), u, KD, tokens, before)

            def stat(norm, tokens):
                n = SLOT["stat", norm]
                start_slot(n)
                pe.wait_ge(sq_sum_ready, KD * (norm + 1))
                plain(n, [(ones_d[:, :], sq_sum)], tokens)

            def tstat(norm):
                n = SLOT["tstat", norm]
                start_slot(n)
                pe.wait_ge(sq_sum_ready, KD * (norm + 1))
                for t in range(TT):
                    last = mm(ps[:, n % NS, t:t + 1], sq_sum[:, META + P * t:META + P * (t + 1)],
                              ones_d[:, 0:1], start=True, stop=True)
                if norm == 2:
                    last = mm(ps[0:META, n % NS, TT:TT + 1], sq_sum[:, 0:META], ones_d[:, 0:1],
                              start=True, stop=True)
                last.then_inc(filled_n, 1)

            def flip(dst, src, rows=P):
                return nc.tensor.transpose(dst, src, ident[0:rows, 0:rows])

            pe.wait_ge(consts, N_CONST)
            pe.wait_ge(vec_loaded, 160)
            n = SLOT["vec",]
            flip(ps[:, n % NS, 0:NV], vec_rows[:, :], NV)
            flip(ps[:, n % NS, BANK:BANK + TAPS * CT], cw_rows[:, :], TAPS * CT).then_inc(filled_n, 1)
            pe.wait_ge(meta_loaded, 16)
            for k in range(KD):
                n = SLOT["x", k]
                start_slot(n)
                pe.wait_ge(x_loaded[k // 2], 16)
                flip(ps[:, n % NS, C0:C0 + META], xmeta[:, P * k:P * (k + 1)], META)
                for j in range(TT):
                    c = C0 + META + P * j
                    last = flip(ps[:, n % NS, c:c + P], xin[:, j, P * k:P * (k + 1)])
                last.then_inc(filled_n, 1)
            for n in range(2 * CT):
                project(SLOT["glu", n], 2 * B_GLU + n, FULL, u_wait(0) if n == 0 else None)
                if n == 0:
                    stat(0, FULL)
            for g in range(PG):
                project(SLOT["p", g], 2 * B_POOL + g, FULL)
            pe.wait_ge(small_lo, 1)
            for g in range(PG):
                exact(SLOT["mix", g], lambda k: (pw_hi[:, g, :], pw_lo[:, g, :]),
                      lambda k: (a_hi[:, g, :], a_lo[:, g, :]), 1, FULL,
                      lambda k: pe.wait_ge(pd_lo_ready, g + 1))

            def project_out0(stage, b, k, first, before):
                w = 2 * b + k // 2
                pe.wait_ge(w_lo_ready, w + 1)
                hi, lo = half_view(w_hi, w), half_view(w_lo, w)
                cols = slice(P * (k % 2), P * (k % 2 + 1))
                exact(SLOT[stage, k], lambda j: (hi[:, j, cols], lo[:, j, cols]),
                      lambda j: (a_hi[:, first + j, :], a_lo[:, first + j, :]), KD // 2, FULL,
                      before if k == 0 else None)

            for k in range(KD):
                project_out0("outp", B_OUTP, k, PG, lambda j: evacuated(pe, SLOT["mix", j]))
            n = SLOT["mean",]
            start_slot(n)
            for c in range(CT):
                pe.wait_ge(tap_done, TAPS * (c + 1))
                for col, a, b in parts(FULL):
                    last = mm(ps[:, n % NS, col:col + b - a], ones_c[:, :], conv[:, c, a:b], start=(c == 0),
                              stop=(c == CT - 1))
            last.then_inc(filled_n, 1)
            n = SLOT["var",]
            ln_work = [relu[:, 0, :], relu[:, 1, :], act2[:, 0, :], act2[:, 1, :]]
            start_slot(n)
            for c in range(CT):
                pe.wait_ge(ln_sq_ready, c + 1)
                for col, a, b in parts(FULL):
                    last = mm(ps[:, n % NS, col:col + b - a], ones_c[:, :], ln_work[c][:, a:b],
                              start=(c == 0), stop=(c == CT - 1))
            last.then_inc(filled_n, 1)
            for k in range(KD):
                project_out0("outc", B_OUTC, k, 0, lambda j: pe.wait_ge(c_lo_ready, j + 1))

            def ffn(layer, fb, tokens, it=0):
                for i in range(2 * KD):
                    n = SLOT["ffn", layer, fb, i]
                    w = 2 * (B_F1 if layer else B_F0) + 16 * fb + i
                    t = KD * FBLK * layer + KD * fb
                    pe.wait_ge(w_lo_ready, w + 1 + 16 * it)
                    if i < KD:
                        exact(n, whalf(w), u, KD, tokens, u_wait(2 * layer + 1) if fb == i == 0 else None, it)
                    else:
                        exact(n, whalf(w), acts, KD, tokens,
                              (lambda k: pe.wait_ge(a_lo_ready, t + k + 1 + 8 * it)) if i == KD else None, it)
                    if fb == 0 and i == 0:
                        stat(2 * layer + 1, tokens)
                    if layer == 1 and fb == FBLK - 1 and i > KD:
                        flip_y(i - KD - 1)

            def ffn_all(layer, tokens):
                ffn(layer, 0, tokens)
                with pe.Fori(0, FBLK - 2) as it:
                    ffn(layer, 1, tokens, it)
                ffn(layer, FBLK - 1, tokens)

            def flip_y(k):
                n = SLOT["y", k]
                start_slot(n)
                pe.wait_ge(hg_ready, k + 1)
                for j in range(TT):
                    last = flip(ps[:, n % NS, P * j:P * (j + 1)], relu[:, k % 2, META + P * j:META + P * (j + 1)])
                last.then_inc(filled_n, 1)

            ffn_all(0, FULL)
            pe.wait_ge(small_lo, 2)
            exact(SLOT["r",], lambda k: (rw_hi[:, RANK * k:RANK * k + P], rw_lo[:, RANK * k:RANK * k + P]),
                  u, KD, FULL, u_wait(2))
            stat(2, FULL)
            tstat(2)

            def project_v(b):
                pe.wait_ge(w_lo_ready, 2 * (B_V + b) + 2)
                whole = [t[:, (B_V + b) % 2, :].rearrange("p (k n) -> p k n", k=KD) for t in (w_hi, w_lo)]
                for t in range(TT + 1):
                    n = SLOT["v", b, t]
                    a = META + P * t if t < TT else 0
                    start_slot(n)
                    for k in range(KD):
                        hi, lo = u_hi[:, k, a:a + P], u_lo[:, k, a:a + P]
                        for i, (l, r) in enumerate(((hi, whole[1]), (hi, whole[0]), (lo, whole[0]))):
                            last = mm(ps[:, n % NS, 0:256], l, r[:, k, :], start=(k == 0 and i == 0),
                                      stop=(k == KD - 1 and i == 2))
                    last.then_inc(filled_n, 1)

            project_v(0)
            evacuated(pe, SLOT["r",])
            pe.wait_ge(small_loaded, 48)
            for hd in range(HEADS):
                start_slot(SLOT["gate", hd])
                plain(SLOT["gate", hd], [(gw2[:, HK * hd:HK * (hd + 1)], r_sb)], FULL)
            for b in range(1, 4):
                project_v(b)

            def flip_k(hd):
                n = SLOT["kt", hd]
                start_slot(n)
                evacuated(pe, SLOT["k", hd])
                kd = relu[:, hd % 2, :]
                for j in range(TT):
                    flip(ps[:, n % NS, P * j:P * (j + 1)], kd[:, META + P * j:META + P * (j + 1)])
                flip(ps[:, n % NS, BANK:BANK + P], kd[:, 0:P]).then_inc(filled_n, 1)

            def project_k(hd):
                project(SLOT["k", hd], 2 * B_K + hd, FULL)

            def project_q(hd):
                project(SLOT["q", hd], 2 * B_Q + hd, FRAMES)

            def chunk_kv(c):
                n = SLOT["kv", c]
                start_slot(n)
                if c == 0:
                    for hd in range(HEADS):
                        evacuated(pe, SLOT["kt", hd])
                    for t in range(TT + 1):
                        evacuated(pe, SLOT["v", 3, t])
                    kc, vc = k_meta[:, :], v_meta[:, :]
                else:
                    j, r = (c - 1) // 2, CHUNK * ((c - 1) % 2)
                    kc, vc = k_tok[r:r + CHUNK, j, :], v_tok[r:r + CHUNK, j, :]
                for hd in range(HEADS):
                    last = mm(ps[:, n % NS, HV * hd:HV * (hd + 1)], kc[:, HK * hd:HK * (hd + 1)],
                              vc[:, HV * hd:HV * (hd + 1)], start=True, stop=True)
                last.then_inc(filled_n, 1)

            def chunk_o(c):
                n = SLOT["o", c]
                start_slot(n)
                evacuated(pe, SLOT["kv", c])
                if c == 1:
                    for hd in range(HEADS):
                        evacuated(pe, SLOT["q", hd])
                for hd in range(HEADS):
                    for m in range(HV // P):
                        k = hd * (HV // P) + m
                        last = mm(ps[:, n % NS, CHUNK * k:CHUNK * (k + 1)],
                                  state[:, c % 2, hd, P * m:P * (m + 1)],
                                  q[:, hd, CHUNK * (c - 1):CHUNK * c], start=True, stop=True)
                last.then_inc(filled_n, 1)

            def head_square_sum(j):
                n = SLOT["hn", j]
                start_slot(n)
                pe.wait_ge(o_sq_ready, j + 1)
                for m in range(HV // P):
                    last = mm(ps[:, n % NS, 0:SEQ], ones_v[:, :], o_sq[:, m, :, :].rearrange("p h t -> p (h t)"),
                              start=(m == 0), stop=(m == HV // P - 1))
                last.then_inc(filled_n, 1)

            for hd in range(HEADS):
                project_k(hd)
                if hd:
                    flip_k(hd - 1)
            project_q(0)
            flip_k(HEADS - 1)
            project_q(1)
            project_q(2)
            chunk_kv(0)
            project_q(3)
            chunk_kv(1)
            for i in range(KD):
                project(SLOT["g", i], 2 * B_G + i, FRAMES)
                chunk_o(i + 1)
                if i + 2 < NCH:
                    chunk_kv(i + 2)
                if i >= 2 and i % 2 == 0:
                    head_square_sum(i // 2 - 1)
            head_square_sum(TT - 1)
            for k in range(KD):
                w = 2 * B_OUT1 + k
                pe.wait_ge(w_lo_ready, w + 1)
                exact(SLOT["out1", k], whalf(w), acts, KD, FRAMES,
                      (lambda j: pe.wait_ge(o_lo_ready, j + 1)) if k == 0 else None)
            ffn_all(1, FRAMES)
            tstat(4)
            flip_y(KD - 1)


_INS = ["x", "meta_tokens", "mix_norm_g", "ffn_norm_g", "ffn_w1", "ffn_w2", "cp_w_in", "cp_conv_w",
        "cp_conv_b", "cp_ln_g", "cp_ln_b", "cp_pool_w", "cp_pool_scale", "cp_w_out", "gla_w_in",
        "gla_gate_w2", "gla_gate_b", "gla_head_g", "gla_w_out", "final_norm_g"]


def kernel(**inputs):
    import numpy as _np
    import concourse.bacc as _bacc
    from concourse import mybir as _mybir
    from concourse.bass_utils import run_bass_kernel_spmd as _run

    nc = _bacc.Bacc("TRN2", target_bir_lowering=False, num_devices=1)
    arrays, args = {}, []
    for name in _INS:
        a = _np.ascontiguousarray(inputs[name])
        arrays[f"in_{name}_dram"] = a
        args.append(nc.dram_tensor(f"in_{name}_dram", a.shape, _mybir.dt.from_np(a.dtype),
                                   kind="ExternalInput").ap())
    shape = inputs["x"].shape
    args.append(nc.dram_tensor("out_dram", shape, _mybir.dt.float32, kind="ExternalOutput").ap())
    build_trunk(nc, *args)
    r = _run(nc, [arrays], core_ids=[0])
    return r.results[0]["out_dram"]
```

```python
from contextlib import ExitStack

import concourse.bass as bass
from concourse import mybir

F32 = mybir.dt.float32
F32R = mybir.dt.float32r
ALU = mybir.AluOpType
ACT = mybir.ActivationFunctionType

P = 128
EPS = 1e-5
META = 16
SEQ = 512
TOK = META + SEQ
D = 1024
KD = D // P
FF = 4 * D
FBLK = FF // D
CONV = 512
CT = CONV // P
TAPS = 31
PG = 4
WMAX = 16
HEADS = 4
DK = 512
HK = DK // HEADS
DV = 1024
HV = DV // HEADS
RANK = 16
GATE_NORM = 16.0
CHUNK = 64
NCH = SEQ // CHUNK + 1
TT = SEQ // P
NS = 4
BANK = 512
SPLIT = META + 2 * P
C0 = BANK - SPLIT
PE_TAPS = [(2, t) for t in range(12)] + [(3, t) for t in range(31)]
DIAGS = 8
OUT_MEAN, OUT_VAR = 4, 5
CONV_STEP, POOL_STEP, PD_STEP, MIX_STEP, OUT_STEP = 20, 2, 2, 1, 4
V_MIX, V_FFN, V_FIN = 0, 2 * KD, 4 * KD
V_CB = V_FIN + KD
V_LG, V_LB, V_PS, V_GB = V_CB + CT, V_CB + 2 * CT, V_CB + 3 * CT, V_CB + 4 * CT
V_HG = V_GB + DK // P
NV = V_HG + HV // P
B_GLU, B_POOL = 0, CT
B_OUTP = B_POOL + 2
B_OUTC = B_OUTP + 2
B_F0 = B_OUTC + 2
B_V = B_F0 + 8 * FBLK
B_K, B_Q, B_G = B_V + 4, B_V + 6, B_V + 8
B_OUT1 = B_G + 4
B_F1 = B_OUT1 + 4
NB = B_F1 + 8 * FBLK


def plan_slots():
    order = [("gain",), ("xm",)] + [("x", i) for i in range(KD // 2)]
    for c in range(CT):
        order += [("glu", 2 * c)] + [("vec",)] * (c == 0)
        order += [("glu", 2 * c + 1), ("h", 2 * c), ("h", 2 * c + 1)]
    order += [("conv", 2)] + [("p", g) for g in range(PG)] + [("conv", 3)]
    order += [("mix", g) for g in range(PG)]
    order += [("outp", k) for k in range(OUT_MEAN)] + [("mean",)]
    order += [("outp", k) for k in range(OUT_MEAN, OUT_VAR)] + [("var",)]
    order += [("outp", k) for k in range(OUT_VAR, KD)] + [("outc", k) for k in range(KD)]
    slot = {}

    def add(names):
        for n in names:
            slot[n] = len(slot)

    def ffn(layer, norm):
        for fb in range(FBLK):
            for i in range(2 * KD):
                yield ("ffn", layer, fb, i)
                if fb == 0 and i == 0:
                    yield ("stat", norm)
                if layer == 1 and fb == FBLK - 1 and i > KD:
                    yield ("y", i - KD - 1)
        if layer == 1:
            yield ("tstat", 4)
            yield ("y", KD - 1)

    add(order)
    add(ffn(0, 1))
    add([("r",), ("tstat", 2), ("stat", 2)])
    for b in range(4):
        add(("v", b, t) for t in range(TT + 1))
        if b == 0:
            add(("gate", n) for n in range(HEADS))
    for h in range(HEADS):
        add([("k", h)] + ([("kt", h - 1)] if h else []))
    add([("q", 0), ("kt", HEADS - 1), ("q", 1), ("kv", 0), ("q", 2), ("kv", 1), ("q", 3), ("kv", 2),
         ("o", 1)])
    for i in range(KD - 2):
        add([("hn", i // 2)] * (i % 2) + [("g", i), ("o", i + 2), ("kv", i + 3)] + [("hb", i // 2)] * (i % 2))
    add([("o", NCH - 1), ("g", KD - 2), ("hn", TT - 1), ("hb", TT - 1), ("g", KD - 1)])
    add(("out1", k) for k in range(KD))
    add(ffn(1, 3))
    return slot


SLOT = plan_slots()


def half_reader(n):
    b, j = divmod(n, 2)
    if b < B_POOL:
        return SLOT["glu", n]
    if b < B_OUTP:
        return SLOT["p", n - 2 * B_POOL]
    if b < B_OUTC:
        return SLOT["outp", 2 * (n - 2 * B_OUTP) + 1]
    if b < B_F0:
        return SLOT["outc", 2 * (n - 2 * B_OUTC) + 1]
    if b < B_V:
        return SLOT["ffn", 0, (b - B_F0) // 8, (n - 2 * B_F0) % 16]
    if b < B_K:
        return SLOT["v", b - B_V, TT]
    if b < B_Q:
        return SLOT["k", n - 2 * B_K]
    if b < B_G:
        return SLOT["q", n - 2 * B_Q]
    if b < B_OUT1:
        return SLOT["g", n - 2 * B_G]
    if b < B_F1:
        return SLOT["out1", n - 2 * B_OUT1]
    return SLOT["ffn", 1, (b - B_F1) // 8, (n - 2 * B_F1) % 16]


def half_freed(n):
    changed = n // 2 in (B_OUTP, B_OUTP + 1, B_F0, B_F0 + 1)
    return half_reader(n - 4 + (1 - n % 2 if changed else 0))


def raw_count(b):
    return 16 * (b // 2 + 1 + min(b // 2 + 1, B_POOL // 2))


def build_trunk(nc, x, meta_tokens, mix_norm_g, ffn_norm_g, ffn_w1, ffn_w2, cp_w_in, cp_conv_w,
                cp_conv_b, cp_ln_g, cp_ln_b, cp_pool_w, cp_pool_scale, cp_w_out, gla_w_in,
                gla_gate_w2, gla_gate_b, gla_head_g, gla_w_out, final_norm_g, out):
    with ExitStack() as ctx:
        def sb(name, shape, dt=F32, stack=ctx):
            return stack.enter_context(nc.sbuf_tensor(name, shape, dt))

        def sem(name):
            return ctx.enter_context(nc.semaphore(name))

        ps = ctx.enter_context(nc.psum_tensor("ps", [P, NS, 2 * BANK], F32))

        h = sb("h", [P, KD, TOK])
        u_hi = sb("u_hi", [P, KD, TOK], F32R)
        u_lo = sb("u_lo", [P, KD, TOK], F32R)
        h_sq = sb("h_sq", [P, 2, TOK])
        sq_sum = sb("sq_sum", [P, TOK])
        std = sb("std", [P, TOK])
        rstd = sb("rstd", [P, TOK])
        ms_tok = sb("ms_tok", [P, TT + 1])
        std_tok = sb("std_tok", [P, TT + 1])
        rstd_tok = sb("rstd_tok", [P, TT + 1])
        std_head = sb("std_head", [P, HEADS])
        rstd_head = sb("rstd_head", [P, HEADS])
        raw = sb("raw", [P, 2, 2 * KD * P])
        w_hi = sb("w_hi", [P, 2, 2 * KD * P], F32R)
        w_lo = sb("w_lo", [P, 2, 2 * KD * P], F32R)
        ident = sb("ident", [P, P])
        ones_d = sb("ones_d", [P, P])
        ones_c = sb("ones_c", [P, P])
        ones_v = sb("ones_v", [P, P])
        ones_1 = sb("ones_1", [P, P])
        eps = sb("eps", [P, 1])
        gain_rows = sb("gain_rows", [2 * KD, P])
        vec_rows = sb("vec_rows", [NV - 2 * KD, P])
        cw_rows = sb("cw_rows", [TAPS * CT, P])
        vec = sb("vec", [P, NV])
        cw = sb("cw", [P, TAPS * CT])
        gw2 = sb("gw2", [RANK, DK])
        rw = sb("rw", [P, KD * RANK])
        rw_hi = sb("rw_hi", [P, (KD - 1) * RANK + P], F32R)
        rw_lo = sb("rw_lo", [P, (KD - 1) * RANK + P], F32R)
        relu = sb("relu", [P, 2, TOK])
        act2 = sb("act2", [P, 2, TOK])

        with ExitStack() as part:
            with ExitStack() as start:
                xin = sb("xin", [P, TT, D], F32, start)
                xmeta = sb("xmeta", [META, D], F32, start)
            a_hi = sb("a_hi", [P, KD, TOK], F32R, part)
            with ExitStack() as early:
                sb("below_pin", [P, PG, TOK], F32, early)
                pin = sb("pin", [P, PG, WMAX + TOK], F32, early)
            a_lo = sb("a_lo", [P, KD, TOK], F32R, part)
            sb("pin_end", [P, PG, WMAX], F32, part)
            with ExitStack() as mixer0:
                win = sb("win", [P, 2, WMAX + TOK], F32, mixer0)
                rcount = sb("rcount", [P, WMAX], F32, mixer0)
                pw = sb("pw", [P, PG, P], F32, mixer0)
                pw_hi = sb("pw_hi", [P, PG, P], F32R, mixer0)
                pw_lo = sb("pw_lo", [P, PG, P], F32R, mixer0)
                conv_in = sb("conv_in", [P, CT, TAPS - 1 + TOK], F32, mixer0)
                conv = sb("conv", [P, CT, TOK], F32, mixer0)
                ci_hi = sb("ci_hi", [P, 2, TAPS - 1 + TOK], F32R, mixer0)
                ci_lo = sb("ci_lo", [P, 2, TAPS - 1 + TOK], F32R, mixer0)
                cw_hi = sb("cw_hi", [P, TAPS * CT], F32R, mixer0)
                cw_lo = sb("cw_lo", [P, TAPS * CT], F32, mixer0)
                diag_hi = sb("diag_hi", [P, DIAGS, P], F32R, mixer0)
                diag_lo = sb("diag_lo", [P, DIAGS, P], F32R, mixer0)
            with ExitStack() as last:
                y_tok = sb("y_tok", [P, TT, D], F32, last)
        with ExitStack() as gla:
            v_tok = sb("v_tok", [P, TT, DV], F32, gla)
            v_meta = sb("v_meta", [META, DV], F32, gla)
            k_tok = sb("k_tok", [P, TT, DK], F32, gla)
            k_meta = sb("k_meta", [META, DK], F32, gla)
            decay = sb("decay", [P, HEADS, TOK], F32, gla)
            with ExitStack() as gated_parts:
                gated_lo = sb("gated_lo", [P, KD, SEQ], F32R, gated_parts)
                gated_hi = sb("gated_hi", [P, KD, SEQ], F32R, gated_parts)
            gate = sb("gate", [P, KD, SEQ], F32, gla)
            o = sb("o", [P, KD, SEQ], F32, gla)
            state = sb("state", [P, 2, HEADS, HV], F32, gla)
            etot = sb("etot", [P, HEADS, NCH], F32, gla)
        q = decay[:, :, META:]
        mask = state[:, 0, :, :].rearrange("p h v -> p (h v)")[:, 0:TOK]
        logd = o[:, :, :].rearrange("p k t -> p (k t)")[:, 0:HEADS * TOK].rearrange(
            "p (h t) -> p h t", h=HEADS)
        o_sq = relu[:, :, :].rearrange("p a t -> p (a t)")[:, 0:KD * P].rearrange(
            "p (m h t) -> p m h t", m=HV // P, h=HEADS)
        r_sb = relu[0:RANK, 0, :]
        work = [relu[:, 0, :], relu[:, 1, :], act2[:, 0, :], act2[:, 1, :]]
        x_normed = h[:, :, :].rearrange("p k t -> p (k t)")[:, 0:TT * D].rearrange(
            "p (j d) -> p j d", d=D)
        meta_normed = relu[0:META, :, :].rearrange("p a t -> p (a t)")[:, 0:D]
        squares = conv[:, :, :].rearrange("p c t -> p (c t)")[:, 0:D]
        u_meta = sq_sum[:, 0:KD * META].rearrange("p (k t) -> p k t", t=META)
        head_diag = act2[:, 0, 0:SEQ].rearrange("p (h t) -> p h t", h=HEADS)

        x_loaded = [sem(f"x_loaded{i}") for i in range(TT)]
        x_squared = sem("x_squared")
        x_std = sem("x_std")
        x_normed_ready = sem("x_normed_ready")
        u_meta_ready = sem("u_meta_ready")
        u_meta_hi_ready = sem("u_meta_hi_ready")
        gain_loaded = sem("gain_loaded")
        meta_loaded = sem("meta_loaded")
        vec_loaded = sem("vec_loaded")
        small_loaded = sem("small_loaded")
        raw_loaded = [sem(f"raw_loaded{i}") for i in range(2)]
        consts = sem("consts")
        filled_n = sem("filled")
        evac = [sem(f"evac{i}") for i in range(NS)]
        w_hi_ready = sem("w_hi_ready")
        w_lo_ready = sem("w_lo_ready")
        small_hi = sem("small_hi")
        small_lo = sem("small_lo")
        h_sq_ready = sem("h_sq_ready")
        u_hi_ready = sem("u_hi_ready")
        u_lo_ready = sem("u_lo_ready")
        sq_sum_ready = sem("sq_sum_ready")
        rstd_ready = sem("rstd_ready")
        rstd_tok_ready = sem("rstd_tok_ready")
        tap_done = [sem(f"tap_done{c}") for c in range(CT)]
        ci_hi_ready = sem("ci_hi_ready")
        ci_lo_ready = sem("ci_lo_ready")
        diag_ready = sem("diag_ready")
        diag_used = sem("diag_used")
        dve_step = sem("dve_step")
        pin_zeroed = sem("pin_zeroed")
        pd_ready = sem("pd_ready")
        pd_hi_ready = sem("pd_hi_ready")
        pd_lo_ready = sem("pd_lo_ready")
        mix_hi_ready = sem("mix_hi_ready")
        centred = sem("centred")
        ln_sq_ready = sem("ln_sq_ready")
        normed = sem("normed")
        silu_ready = sem("silu_ready")
        sq_ready = sem("sq_ready")
        a_hi_ready = sem("a_hi_ready")
        a_lo_ready = sem("a_lo_ready")
        c_hi_ready = sem("c_hi_ready")
        c_lo_ready = sem("c_lo_ready")
        abs_ready = sem("abs_ready")
        gexp_ready = sem("gexp_ready")
        softplus_ready = sem("softplus_ready")
        suffix_ready = sem("suffix_ready")
        decay_ready = sem("decay_ready")
        kscale_ready = sem("kscale_ready")
        gate_ready = sem("gate_ready")
        o_sq_ready = sem("o_sq_ready")
        diag_set = sem("diag_set")
        gated = sem("gated")
        o_hi_ready = sem("o_hi_ready")
        o_lo_ready = sem("o_lo_ready")
        hg_ready = sem("hg_ready")
        act_out = sem("act_out")
        dve_out = sem("dve_out")
        stored = sem("stored")
        N_CONST = 14

        def filled(eng, n, it=0):
            eng.wait_ge(filled_n, n + 1 + 16 * it)

        def evacuated(eng, n, it=0):
            eng.wait_ge(evac[n % NS], n // NS + 1 + 4 * it)

        GATE_PARTS = [(0, 2, 0, P), (2, 4, 0, P), (0, 4, P, 2 * P), (4, 6, 0, 2 * P), (0, 6, 2 * P, 3 * P),
                      (6, 7, 0, 3 * P), (0, 4, 3 * P, SEQ), (4, 7, 3 * P, SEQ), (7, 8, 0, SEQ)]
        GATE_AT = {2: (0,), 4: (1, 2), 6: (3, 4), 7: (5, 6, 7)}

        def diag_free(eng, i):
            c = PE_TAPS[i][0]
            if i + 1 == len(PE_TAPS) or PE_TAPS[i + 1][0] != c:
                filled(eng, SLOT["conv", c])
            else:
                eng.wait_ge(diag_used, i + 1 - (c - 2))

        FULL = (0, TOK)
        FRAMES = (META, TOK)

        def pcols(tokens):
            return (C0, C0 + TOK) if tokens == FULL else (0, SEQ)

        def slot_ap(n, tokens=FULL, rows=P):
            a, b = pcols(tokens)
            return ps[0:rows, n % NS, a:b]

        def half_view(t, n):
            b, j = divmod(n, 2)
            if B_OUTP <= b < B_F0:
                return t[:, b % 2, :].rearrange("p (k n) -> p k n", k=KD // 2)[:, :, 2 * P * j:2 * P * (j + 1)]
            return t[:, b % 2, :].rearrange("p (k n) -> p k n", k=KD)[:, :, P * j:P * (j + 1)]

        def split_hi(n, it=0):
            act = nc.scalar
            act.wait_ge(raw_loaded[n // 2 % 2], raw_count(n // 2) + 64 * it)
            if n >= 4:
                filled(act, half_freed(n), it)
            act.activation(half_view(w_hi, n), half_view(raw, n), ACT.Copy).then_inc(w_hi_ready, 1)

        def split_lo(n, it=0):
            dve = nc.vector
            if n >= 4:
                filled(dve, half_freed(n), it)
            dve.wait_ge(w_hi_ready, n + 1 + 16 * it)
            dve.tensor_tensor(half_view(w_lo, n), half_view(raw, n), half_view(w_hi, n).bitcast(F32),
                              ALU.subtract).then_inc(w_lo_ready, 1)

        block = ctx.enter_context(nc.Block())

        @block.sync
        def _(sp):
            x_v = x[0].rearrange("(j p) d -> p j d", p=P)

            def load_x(j):
                sp.dma_start(xin[:, j, :], x_v[:, j, :]).then_inc(x_loaded[j], 16)

            def reusable(b, fb=0):
                if b >= 2:
                    sp.wait_ge(w_lo_ready, 2 * (b - 1) + 16 * fb)

            def load(b, src, fb=0):
                reusable(b, fb)
                sp.dma_start(raw[:, b % 2, :].rearrange("p (k n) -> p k n", n=src.shape[2]), src)\
                  .then_inc(raw_loaded[b % 2], 16)

            cp_in = cp_w_in[0].rearrange("(k p) n -> p k n", p=P)
            cp_out = cp_w_out[0].rearrange("(k p) n -> p k n", p=P)
            gla_in = gla_w_in[0].rearrange("(k p) n -> p k n", p=P)
            gla_out = gla_w_out[0].rearrange("(k p) n -> p k n", p=P)

            def load_glu(c):
                reusable(B_GLU + c)
                for j in range(2):
                    n = 2 * (B_GLU + c) + j
                    at = CONV * (1 - j) + P * c
                    sp.dma_start(half_view(raw, n), cp_in[:, :, at:at + P])\
                      .then_inc(raw_loaded[c % 2], 16)

            def load_ffn(layer, first):
                w1 = ffn_w1[layer].rearrange("(k p) n -> p k n", p=P)
                w2 = ffn_w2[layer].rearrange("(k p) n -> p k n", p=P)
                with sp.Fori(0, FBLK) as fb:
                    for j in range(4):
                        load(first + j, w1[:, :, bass.ds(fb * D + 256 * j, 256)], fb)
                    for j in range(4):
                        load(first + 4 + j, w2[:, bass.ds(fb * KD, KD), 256 * j:256 * (j + 1)], fb)

            load_x(0)
            sp.dma_start(gain_rows[:, :], mix_norm_g.rearrange("l (k p) -> (l k) p", p=P))\
               .then_inc(gain_loaded, 16)
            sp.dma_start(xmeta[:, :], meta_tokens).then_inc(meta_loaded, 16)
            for j in range(1, TT):
                load_x(j)
            load_glu(0)
            sp.dma_start(vec_rows[0:2 * KD, :], ffn_norm_g.rearrange("l (k p) -> (l k) p", p=P))\
               .then_inc(vec_loaded, 16)
            at = V_FIN - 2 * KD
            sp.dma_start(vec_rows[at:at + KD, :], final_norm_g.rearrange("(k p) -> k p", p=P))\
               .then_inc(vec_loaded, 16)
            for v, row in ((cp_conv_b, V_CB), (cp_ln_g, V_LG), (cp_ln_b, V_LB), (cp_pool_scale, V_PS),
                           (gla_gate_b, V_GB), (gla_head_g, V_HG)):
                n, row = v.shape[1] // P, row - 2 * KD
                sp.dma_start(vec_rows[row:row + n, :], v[0].rearrange("(k p) -> k p", p=P))\
                   .then_inc(vec_loaded, 16)
            sp.dma_start(cw_rows[:, :], cp_conv_w[0].rearrange("t (c p) -> (t c) p", p=P))\
               .then_inc(vec_loaded, 16)
            sp.dma_start(pw[:, :, :], cp_pool_w[0].rearrange("g c d -> c g d")).then_inc(small_loaded, 16)
            sp.dma_start(rw[:, :].rearrange("p (k r) -> p k r", r=RANK),
                          gla_w_in[0].rearrange("(k p) n -> p k n", p=P)[:, :, 2 * DK + 2 * DV:])\
               .then_inc(small_loaded, 16)
            sp.dma_start(gw2[:, :], gla_gate_w2[0]).then_inc(small_loaded, 16)
            for c in range(1, CT):
                load_glu(c)
            for j in range(2):
                load(B_POOL + j, cp_in[:, :, 2 * CONV + 256 * j:2 * CONV + 256 * (j + 1)])
            for j in range(2):
                load(B_OUTP + j, cp_out[:, KD // 2:, 512 * j:512 * (j + 1)])
            for j in range(2):
                load(B_OUTC + j, cp_out[:, :KD // 2, 512 * j:512 * (j + 1)])
            load_ffn(0, B_F0)
            for b, at, n in ((B_V, 2 * DK, 4), (B_K, DK, 2), (B_Q, 0, 2), (B_G, 2 * DK + DV, 4)):
                for j in range(n):
                    load(b + j, gla_in[:, :, at + 256 * j:at + 256 * (j + 1)])
            for j in range(4):
                load(B_OUT1 + j, gla_out[:, :, 256 * j:256 * (j + 1)])
            load_ffn(1, B_F1)
            out_v = out[0].rearrange("(j p) d -> j p d", p=P)
            for j in range(TT):
                sp.wait_ge((act_out, dve_out)[j % 2], j // 2 + 1)
                sp.dma_start(out_v[j], y_tok[:, j, :]).then_inc(stored, 16)
            sp.wait_ge(stored, 16 * TT)

        @block.gpsimd
        def _(pool):
            pool.memset(ident[:, :], 0.0).then_inc(consts, 1)
            pool.wait_ge(consts, 1)
            pool.affine_select(out=ident[:, :], in_=ident[:, :], compare_op=ALU.not_equal, fill=1.0,
                               base=0, pattern=[[-1, P]], channel_multiplier=1).then_inc(consts, 1)
            pool.memset(ones_d[:, :], 1.0 / D).then_inc(consts, 1)
            pool.memset(ones_c[:, :], 1.0 / CONV).then_inc(consts, 1)
            pool.memset(ones_v[:, :], 1.0 / HV).then_inc(consts, 1)
            pool.memset(ones_1[:, :], 1.0).then_inc(consts, 1)
            pool.memset(eps[:, :], EPS).then_inc(consts, 1)
            pool.memset(conv_in[:, :, 0:TAPS - 1], 0.0).then_inc(consts, 1)
            pool.memset(win[:, :, 0:WMAX], 0.0).then_inc(consts, 1)
            pool.memset(rw_hi[:, KD * RANK:].bitcast(F32), 0.0).then_inc(consts, 1)
            pool.memset(rw_lo[:, KD * RANK:].bitcast(F32), 0.0).then_inc(consts, 1)
            for t in range(WMAX - 1):
                last = pool.memset(rcount[:, t:t + 1], 1.0 / (t + 1))
            last.then_inc(consts, 3)

        @block.scalar
        def _(act):
            def prep(norm, k, n, tokens):
                a, b = tokens
                evacuated(act, n)
                if norm < 4:
                    g = (V_MIX, V_FFN, V_MIX + KD, V_FFN + KD)[norm] + k
                    act.activation(u_hi[:, k, a:b], h[:, k, a:b], ACT.Copy, scale=vec[:, g:g + 1])\
                       .then_inc(u_hi_ready, 1)
                t = KD * (norm - 1) + k
                if t >= 2:
                    act.wait_ge(sq_sum_ready, t - 1)
                act.activation(h_sq[:, k % 2, a:b], h[:, k, a:b], ACT.Square).then_inc(h_sq_ready, 1)

            def stat(norm, tokens):
                n = SLOT["stat", norm]
                filled(act, n)
                act.activation(std[:, tokens[0]:tokens[1]], slot_ap(n, tokens), ACT.Sqrt,
                               bias=eps[:, :]).then_inc(evac[n % NS], 1)

            def tstat(norm):
                n = SLOT["tstat", norm]
                filled(act, n)
                last = act.activation(std_tok[:, 0:TT], ps[:, n % NS, 0:TT], ACT.Sqrt, bias=eps[:, :])
                if norm == 2:
                    last = act.activation(std_tok[0:META, TT:TT + 1], ps[0:META, n % NS, TT:TT + 1],
                                          ACT.Sqrt, bias=eps[0:META, :])
                last.then_inc(evac[n % NS], 1)

            act.wait_ge(consts, N_CONST)
            act.activation(std_head[:, 0:1], eps[:, :], ACT.Sqrt)
            for j in range(TT):
                act.wait_ge(x_loaded[j], 16)
                act.activation(squares, xin[:, j, :], ACT.Square, accum_out=ms_tok[:, j:j + 1])\
                   .then_inc(x_squared, 1)
                if j == 0:
                    act.wait_ge(meta_loaded, 16)
                    act.activation(meta_normed, xmeta[:, :], ACT.Square,
                                   accum_out=ms_tok[0:META, TT:TT + 1]).then_inc(x_squared, 1)
                    act.wait_ge(x_squared, 2)
                    act.activation(std_tok[0:META, TT:TT + 1], ms_tok[0:META, TT:TT + 1], ACT.Sqrt,
                                   bias=eps[0:META, :], scale=1.0 / D).then_inc(x_std, 1)
                act.wait_ge(x_squared, j + 2)
                act.activation(std_tok[:, j:j + 1], ms_tok[:, j:j + 1], ACT.Sqrt, bias=eps[:, :],
                               scale=1.0 / D).then_inc(x_std, 1)
                if j == 1:
                    n = SLOT["gain",]
                    filled(act, n)
                    act.activation(vec[:, 0:2 * KD], ps[:, n % NS, 0:2 * KD], ACT.Copy)\
                       .then_inc(evac[n % NS], 1)
                if j == 2:
                    act.wait_ge(u_meta_ready, 1)
                    act.activation(u_hi[:, :, 0:META], u_meta, ACT.Copy).then_inc(u_meta_hi_ready, 1)
            evacuated(act, SLOT["gain",])

            def x_bank(k):
                return ps[:, SLOT["x", k // 2] % NS, BANK * (k % 2):BANK * (k % 2) + SEQ]

            split_hi(0)
            for k in range(KD):
                filled(act, SLOT["x", k // 2])
                act.activation(u_hi[:, k, META:], x_bank(k), ACT.Copy, scale=vec[:, V_MIX + k:V_MIX + k + 1])\
                   .then_inc(u_hi_ready, 1)
            split_hi(1)
            n = SLOT["vec",]
            filled(act, n)
            act.activation(vec[:, 2 * KD:], ps[:, n % NS, 0:NV - 2 * KD], ACT.Copy)
            act.activation(cw[:, :], ps[:, n % NS, BANK:BANK + TAPS * CT], ACT.Copy)\
               .then_inc(evac[n % NS], 1)
            split_hi(2)
            evacuated(act, n)
            act.activation(cw_hi[:, :], cw[:, :], ACT.Copy).then_inc(small_hi, 1)
            act.wait_ge(small_loaded, 48)
            act.activation(pw_hi[:, :, :], pw[:, :, :], ACT.Copy).then_inc(small_hi, 1)
            act.activation(rw_hi[:, 0:KD * RANK], rw[:, :], ACT.Copy).then_inc(small_hi, 1)
            split_hi(3)
            built = [0]

            def build_diags(count):
                for i in range(built[0], min(built[0] + count, len(PE_TAPS))):
                    c, t = PE_TAPS[i]
                    col = t * CT + c
                    if i >= DIAGS:
                        diag_free(act, i - DIAGS)
                    act.activation(diag_hi[:, i % DIAGS, :], ident[:, :], ACT.Copy,
                                   scale=cw_hi[:, col:col + 1].bitcast(F32))
                    act.activation(diag_lo[:, i % DIAGS, :], ident[:, :], ACT.Copy,
                                   scale=cw_lo[:, col:col + 1]).then_inc(diag_ready, 1)
                    built[0] = i + 1

            def copy_h(k):
                n = SLOT["h", k]
                filled(act, n)
                act.activation(h[:, k, :], slot_ap(n), ACT.Copy).then_inc(evac[n % NS], 1)

            act.wait_ge(small_hi, 1)
            act.wait_ge(small_lo, 1)
            for c in range(CT):
                n = SLOT["glu", 2 * c]
                filled(act, n)
                if c >= 2:
                    evacuated(act, SLOT["glu", 2 * (c - 2) + 1])
                act.activation(act2[:, c % 2, :], slot_ap(n), ACT.Sigmoid).then_inc(evac[n % NS], 1)
                split_hi(4 * c // 2 + 4)
                build_diags(2)
                split_hi(4 * c // 2 + 5)
                copy_h(2 * c)
                copy_h(2 * c + 1)
                if c >= 2:
                    evacuated(act, SLOT["glu", 2 * c + 1])
                    act.activation(ci_hi[:, c - 2, :], conv_in[:, c, :], ACT.Copy).then_inc(ci_hi_ready, 1)

            def evac_conv(c):
                n = SLOT["conv", c]
                filled(act, n)
                act.activation(conv[:, c, :], slot_ap(n), ACT.Identity,
                               bias=vec[:, V_CB + c:V_CB + c + 1]).then_inc(evac[n % NS], 1)

            build_diags(sum(c == 2 for c, _ in PE_TAPS) - built[0])
            evac_conv(2)
            for g in range(PG):
                n = SLOT["p", g]
                filled(act, n)
                act.activation(pin[:, g, WMAX:], slot_ap(n), ACT.Copy).then_inc(evac[n % NS], 1)
                split_hi(2 * B_POOL + g + 4)
                build_diags(2)
            for g in range(PG):
                build_diags(5)
                act.wait_ge(pd_ready, g + 1)
                act.activation(a_hi[:, g, :], work[g], ACT.Copy).then_inc(pd_hi_ready, 1)
            build_diags(len(PE_TAPS))
            evac_conv(3)
            for g in range(PG):
                n = SLOT["mix", g]
                filled(act, n)
                act.activation(a_hi[:, PG + g, :], slot_ap(n), ACT.Copy,
                               scale=vec[:, V_PS + g:V_PS + g + 1]).then_inc(mix_hi_ready, 1)
            for k in range(1, OUT_MEAN, 2):
                split_hi(2 * B_OUTC + k // 2)
            for c in range(CT):
                if c < CT - 1:
                    act.wait_ge(centred, c + 1)
                else:
                    evacuated(act, SLOT["mean",])
                act.activation(work[c], conv[:, c, :], ACT.Square).then_inc(ln_sq_ready, 1)
            n = SLOT["var",]
            filled(act, n)
            act.activation(std[:, :], slot_ap(n), ACT.Sqrt, bias=eps[:, :]).then_inc(evac[n % NS], 1)
            for c in range(CT):
                if c == 0:
                    for k in range(OUT_MEAN, KD):
                        if k % 2 and k < OUT_VAR:
                            split_hi(2 * B_OUTC + k // 2)
                act.wait_ge(normed, c + 1)
                act.activation(work[c], conv[:, c, :], ACT.Silu, bias=vec[:, V_LB + c:V_LB + c + 1],
                               scale=vec[:, V_LG + c:V_LG + c + 1]).then_inc(silu_ready, 1)
                act.wait_ge(silu_ready, c + 1)
                act.activation(a_hi[:, c, :], work[c], ACT.Copy).then_inc(c_hi_ready, 1)
            for k in range(OUT_VAR, KD):
                if k % 2:
                    split_hi(2 * B_OUTC + k // 2)
            for k in range(KD):
                n = SLOT["outc", k]
                if k % 2:
                    split_hi(2 * B_F0 + k // 2)
                prep(1, k, n, FULL)

            def ffn(layer, fb, tokens, it=0):
                a, b = tokens
                for i in range(2 * KD):
                    n = SLOT["ffn", layer, fb, i]
                    w = 2 * (B_F1 if layer else B_F0) + 16 * fb + i + 4
                    if fb == 0 and i == 0:
                        stat(2 * layer + 1, tokens)
                    if i < KD:
                        t = KD * FBLK * layer + KD * fb + i
                        evacuated(act, n, it)
                        if t >= 2:
                            act.wait_ge(a_lo_ready, t - 1 + 8 * it)
                        act.activation(act2[:, i % 2, a:b], relu[:, i % 2, a:b], ACT.Square)\
                           .then_inc(sq_ready, 1)
                        act.wait_ge(sq_ready, t + 1 + 8 * it)
                        act.activation(a_hi[:, i, a:b], act2[:, i % 2, a:b], ACT.Copy)\
                           .then_inc(a_hi_ready, 1)
                    if w < 2 * NB:
                        split_hi(w, it)
                    if i >= KD and fb == FBLK - 1:
                        k = i - KD
                        if layer == 0:
                            prep(2, k, n, FULL)
                            continue
                        prep(4, k, n, FRAMES)
                        if k >= 2:
                            filled(act, SLOT["y", k - 2])
                        act.activation(relu[:, k % 2, a:b], h[:, k, a:b], ACT.Copy,
                                       scale=vec[:, V_FIN + k:V_FIN + k + 1]).then_inc(hg_ready, 1)

            def ffn_all(layer, tokens):
                ffn(layer, 0, tokens)
                with act.Fori(0, FBLK - 2) as it:
                    ffn(layer, 1, tokens, it)
                ffn(layer, FBLK - 1, tokens)

            ffn_all(0, FULL)

            def evac_v(b):
                cols = slice(256 * b, 256 * (b + 1))
                for t in range(TT + 1):
                    n = SLOT["v", b, t]
                    filled(act, n)
                    if t < TT:
                        dst, src, r = v_tok[:, t, cols], ps[:, n % NS, 0:256], rstd_tok[:, t:t + 1]
                    else:
                        dst, src, r = v_meta[:, cols], ps[0:META, n % NS, 0:256], rstd_tok[0:META, TT:TT + 1]
                    act.activation(dst, src, ACT.Copy, scale=r).then_inc(evac[n % NS], 1)

            def split_v(b):
                for j in range(2):
                    split_hi(2 * (B_V + b) + 4 + j)

            tstat(2)
            stat(2, FULL)
            act.wait_ge(rstd_tok_ready, TT + 2)
            evac_v(0)
            for hd in range(HEADS):
                n = SLOT["gate", hd]
                filled(act, n)
                act.activation(decay[:, hd, :], slot_ap(n), ACT.Abs,
                               bias=vec[:, V_GB + hd:V_GB + hd + 1]).then_inc(abs_ready, 1)
            split_v(0)
            act.wait_ge(abs_ready, HEADS)
            act.activation(decay[:, :, :], decay[:, :, :], ACT.Exp, scale=-1.0).then_inc(gexp_ready, 1)
            act.wait_ge(gexp_ready, 1)
            act.activation(decay[:, :, :], decay[:, :, :], ACT.Ln, bias=1.0).then_inc(softplus_ready, 1)
            evac_v(1)
            split_v(1)
            evac_v(2)
            split_v(2)
            for hd in range(HEADS):
                act.wait_ge(suffix_ready, hd + 1)
                act.activation(etot[:, hd, :], decay[:, hd, META - 1::CHUNK], ACT.Exp, scale=1.0 / GATE_NORM)
                act.activation(logd[:, hd, :], logd[:, hd, :], ACT.Exp, scale=1.0 / GATE_NORM)\
                   .then_inc(decay_ready, 1)
            evac_v(3)
            split_v(3)

            def evac_kt(hd):
                n = SLOT["kt", hd]
                filled(act, n)
                cols = slice(HK * hd, HK * (hd + 1))
                act.activation(k_tok[:, :, cols], ps[:, n % NS, 0:SEQ].rearrange("p (j d) -> p j d", d=HK),
                               ACT.Copy)
                act.activation(k_meta[:, cols], ps[0:META, n % NS, BANK:BANK + HK], ACT.Copy)\
                   .then_inc(evac[n % NS], 1)

            for hd in range(HEADS):
                split_hi(2 * B_K + hd + 4)
                if hd:
                    evac_kt(hd - 1)
            evac_kt(HEADS - 1)
            for hd in range(HEADS):
                split_hi(2 * B_Q + hd + 4)

            def evac_o(c):
                n = SLOT["o", c]
                filled(act, n)
                act.activation(o[:, :, CHUNK * (c - 1):CHUNK * c],
                               ps[:, n % NS, 0:KD * CHUNK].rearrange("p (k t) -> p k t", t=CHUNK),
                               ACT.Copy).then_inc(evac[n % NS], 1)

            def square_o(j):
                evacuated(act, SLOT["o", 2 * j + 2])
                evacuated(act, SLOT["o", 2 * j + 1])
                if j:
                    filled(act, SLOT["hn", j - 1])
                act.activation(o_sq, o[:, :, P * j:P * (j + 1)].rearrange("p (h m) t -> p m h t", m=HV // P),
                               ACT.Square).then_inc(o_sq_ready, 1)

            def head_std(j):
                n = SLOT["hn", j]
                filled(act, n)
                act.activation(std_head[:, :], ps[:, n % NS, 0:HEADS], ACT.Sqrt, bias=eps[:, :])\
                   .then_inc(evac[n % NS], 1)

            def silu_gate(i):
                evacuated(act, SLOT["g", i])
                act.activation(gate[:, i, :], gate[:, i, :], ACT.Silu).then_inc(gate_ready, 1)

            def round_o(n):
                k0, k1, a, b = GATE_PARTS[n]
                act.wait_ge(gated, n + 1)
                act.activation(gated_hi[:, k0:k1, a:b], gate[:, k0:k1, a:b], ACT.Copy).then_inc(o_hi_ready, 1)

            evac_o(1)
            for i in range(KD - 2):
                if i % 2:
                    head_std(i // 2)
                silu_gate(i)
                split_hi(2 * B_G + i + 4)
                evac_o(i + 2)
                if i % 2 == 0:
                    square_o(i // 2)
                for n in GATE_AT.get(i, ()):
                    round_o(n)
            evac_o(NCH - 1)
            square_o(TT - 1)
            for n in GATE_AT[KD - 2]:
                round_o(n)
            silu_gate(KD - 2)
            head_std(TT - 1)
            split_hi(2 * B_G + KD - 2 + 4)
            for n in GATE_AT[KD - 1]:
                round_o(n)
            silu_gate(KD - 1)
            round_o(len(GATE_PARTS) - 1)
            split_hi(2 * B_G + KD - 1 + 4)
            for k in range(KD):
                split_hi(2 * B_OUT1 + k + 4)
                prep(3, k, SLOT["out1", k], FRAMES)
            ffn_all(1, FRAMES)
            tstat(4)
            act.wait_ge(rstd_tok_ready, TT + 3)
            for k in range(KD):
                evacuated(act, SLOT["y", k])
            for j in range(0, TT, 2):
                act.activation(y_tok[:, j, :], y_tok[:, j, :], ACT.Copy, scale=rstd_tok[:, j:j + 1])\
                   .then_inc(act_out, 1)

        @block.vector
        def _(dve):
            V = nc.vector
            steps = [0]

            def step(ins):
                ins.then_inc(dve_step, 1)
                steps[0] += 1
                dve.wait_ge(dve_step, steps[0])

            def rest_of_u(norm, k, tokens):
                a, b = tokens
                g = (V_MIX, V_FFN, V_MIX + KD, V_FFN + KD)[norm] + k
                dve.wait_ge(u_hi_ready, KD * norm + k + 1)
                V.scalar_tensor_tensor(out=u_lo[:, k, a:b], in0=h[:, k, a:b], scalar=vec[:, g:g + 1],
                                       in1=u_hi[:, k, a:b].bitcast(F32), op0=ALU.mult,
                                       op1=ALU.subtract).then_inc(u_lo_ready, 1)

            def add_squares(norm, k, tokens):
                a, b = tokens
                t = KD * (norm - 1) + k + 1
                dve.wait_ge(h_sq_ready, t)
                if k == 0:
                    V.tensor_copy(sq_sum[:, a:b], h_sq[:, 0, a:b]).then_inc(sq_sum_ready, 1)
                else:
                    dve.wait_ge(sq_sum_ready, t - 1)
                    V.tensor_tensor(sq_sum[:, a:b], sq_sum[:, a:b], h_sq[:, k % 2, a:b], ALU.add)\
                     .then_inc(sq_sum_ready, 1)

            def prep(norm, k, tokens):
                if norm < 4:
                    rest_of_u(norm, k, tokens)
                add_squares(norm, k, tokens)

            uses = [0]

            def recip(n, tokens):
                evacuated(dve, n)
                V.reciprocal(rstd[:, tokens[0]:tokens[1]], std[:, tokens[0]:tokens[1]])\
                 .then_inc(rstd_ready, 1)
                uses[0] += 1
                dve.wait_ge(rstd_ready, uses[0])

            def recip_tok(norm):
                evacuated(dve, SLOT["tstat", norm])
                last = V.reciprocal(rstd_tok[:, 0:TT], std_tok[:, 0:TT])
                if norm == 2:
                    last = V.reciprocal(rstd_tok[0:META, TT:TT + 1], std_tok[0:META, TT:TT + 1])
                last.then_inc(rstd_tok_ready, 1)

            def scale_out(dst, n, tokens=FULL, rows=P):
                filled(dve, n)
                V.tensor_tensor(dst, slot_ap(n, tokens, rows), rstd[0:rows, tokens[0]:tokens[1]], ALU.mult)\
                 .then_inc(evac[n % NS], 1)

            def add_to_h(k, n, tokens, it=0):
                a, b = tokens
                filled(dve, n, it)
                V.tensor_tensor(h[:, k, a:b], h[:, k, a:b], slot_ap(n, tokens), ALU.add)\
                 .then_inc(evac[n % NS], 1)

            dve.wait_ge(consts, N_CONST)
            V.memset(pin[:, :, 0:WMAX], 0.0).then_inc(pin_zeroed, 1)
            for i in range(TT + 1):
                rows, t = (META, TT) if i == 0 else (P, i - 1)
                dve.wait_ge(x_std, i + 1)
                V.reciprocal(rstd_tok[0:rows, t:t + 1], std_tok[0:rows, t:t + 1]).then_inc(rstd_tok_ready, 1)
                dve.wait_ge(rstd_tok_ready, i + 1)
                src, dst = (xmeta[:, :], meta_normed) if i == 0 else (xin[:, t, :], x_normed[:, t, :])
                V.tensor_scalar(dst, src, rstd_tok[0:rows, t:t + 1], None, ALU.mult).then_inc(x_normed_ready, 1)
                if i == 2:
                    n = SLOT["xm",]
                    evacuated(dve, SLOT["gain",])
                    filled(dve, n)
                    V.tensor_tensor(u_meta, ps[:, n % NS, 0:KD * META].rearrange("p (k t) -> p k t", t=META),
                                    vec[:, V_MIX:V_MIX + KD, None].to_broadcast([P, KD, META]), ALU.mult)\
                     .then_inc(u_meta_ready, 1)
            n = SLOT["xm",]
            dve.wait_ge(u_meta_ready, 1)
            dve.wait_ge(u_meta_hi_ready, 1)
            V.tensor_tensor(u_lo[:, :, 0:META], u_meta, u_hi[:, :, 0:META].bitcast(F32), ALU.subtract)\
             .then_inc(evac[n % NS], 1)
            split_lo(0)
            for k in range(KD):
                n = SLOT["x", k // 2]
                dve.wait_ge(u_hi_ready, k + 1)
                ins = V.scalar_tensor_tensor(out=u_lo[:, k, META:],
                                             in0=ps[:, n % NS, BANK * (k % 2):BANK * (k % 2) + SEQ],
                                             scalar=vec[:, V_MIX + k:V_MIX + k + 1],
                                             in1=u_hi[:, k, META:].bitcast(F32), op0=ALU.mult,
                                             op1=ALU.subtract)
                if k % 2:
                    ins.then_inc(evac[n % NS], 1)
            split_lo(1)
            split_lo(2)
            evacuated(dve, SLOT["vec",])
            dve.wait_ge(small_hi, 3)
            V.tensor_tensor(cw_lo[:, :], cw[:, :], cw_hi[:, :].bitcast(F32), ALU.subtract)\
             .then_inc(small_lo, 1)
            V.tensor_tensor(pw_lo[:, :, :], pw[:, :, :], pw_hi[:, :, :].bitcast(F32), ALU.subtract)\
             .then_inc(small_lo, 1)
            V.tensor_tensor(rw_lo[:, 0:KD * RANK], rw[:, :], rw_hi[:, 0:KD * RANK].bitcast(F32),
                            ALU.subtract).then_inc(small_lo, 1)
            split_lo(3)

            taps = {c: [t for t in range(TAPS) if (c, t) not in PE_TAPS] for c in range(CT)}
            last_tile = [0]

            def run_taps(count, tiles):
                while count and any(taps[c] for c in tiles):
                    live = [c for c in tiles if taps[c]][:2]
                    c = live[-1] if last_tile[0] == live[0] else live[0]
                    last_tile[0] = c
                    t = taps[c].pop(0)
                    count -= 1
                    src, wt = conv_in[:, c, t:t + TOK], cw[:, t * CT + c:t * CT + c + 1]
                    done = sum((c, i) not in PE_TAPS for i in range(t))
                    if t == 0:
                        evacuated(dve, SLOT["glu", 2 * c + 1])
                        V.tensor_scalar(conv[:, c, :], src, wt, vec[:, V_CB + c:V_CB + c + 1],
                                        ALU.mult, ALU.add).then_inc(tap_done[c], 1)
                        continue
                    if done:
                        dve.wait_ge(tap_done[c], done)
                    else:
                        evacuated(dve, SLOT["glu", 2 * c + 1])
                        evacuated(dve, SLOT["conv", c])
                    V.scalar_tensor_tensor(out=conv[:, c, :], in0=src, scalar=wt, in1=conv[:, c, :],
                                           op0=ALU.mult, op1=ALU.add).then_inc(tap_done[c], 1)

            for c in range(CT):
                n = SLOT["glu", 2 * c + 1]
                evacuated(dve, SLOT["glu", 2 * c])
                split_lo(2 * c + 4)
                run_taps(5, (0, 1)[:c])
                filled(dve, n)
                V.tensor_tensor(conv_in[:, c, TAPS - 1:], slot_ap(n), act2[:, c % 2, :], ALU.mult)\
                 .then_inc(evac[n % NS], 1)
                split_lo(2 * c + 5)
                if c >= 2:
                    dve.wait_ge(ci_hi_ready, c - 1)
                    V.tensor_tensor(ci_lo[:, c - 2, :], conv_in[:, c, :], ci_hi[:, c - 2, :].bitcast(F32),
                                    ALU.subtract).then_inc(ci_lo_ready, 1)
                run_taps(6, (0, 1)[:c + 1])
            run_taps(CONV_STEP, (0, 1))
            for g in range(PG):
                n = SLOT["p", g]
                run_taps(POOL_STEP, (0, 1))
                split_lo(2 * B_POOL + g + 4)
                evacuated(dve, n)
                src = p_in = pin[:, g, :]
                for j in range(g + 1):
                    back = 1 << j
                    V.tensor_tensor(win[:, j % 2, WMAX:], src[:, WMAX:], src[:, WMAX - back:-back],
                                    ALU.add).then_inc(dve_step, 1)
                    steps[0] += 1
                    run_taps(1, (0, 1))
                    dve.wait_ge(dve_step, steps[0])
                    src = win[:, j % 2, :]
                short, pd = (2 << g) - 1, work[g]
                V.scalar_tensor_tensor(out=pd[:, short:], in0=src[:, WMAX + short:], scalar=1.0 / (short + 1),
                                       in1=p_in[:, WMAX + short:], op0=ALU.mult, op1=ALU.subtract)
                step(V.tensor_tensor(pd[:, 0:short], src[:, WMAX:WMAX + short], rcount[:, 0:short], ALU.mult))
                V.tensor_tensor(pd[:, 0:short], pd[:, 0:short], p_in[:, WMAX:WMAX + short], ALU.subtract)\
                 .then_inc(pd_ready, 1)
            for g in range(PG):
                run_taps(PD_STEP, (0, 1, 2))
                dve.wait_ge(pd_hi_ready, g + 1)
                V.tensor_tensor(a_lo[:, g, :], work[g], a_hi[:, g, :].bitcast(F32), ALU.subtract)\
                 .then_inc(pd_lo_ready, 1)
            for g in range(PG):
                n = SLOT["mix", g]
                run_taps(MIX_STEP, (0, 1, 2))
                dve.wait_ge(mix_hi_ready, g + 1)
                V.scalar_tensor_tensor(out=a_lo[:, PG + g, :], in0=slot_ap(n),
                                       scalar=vec[:, V_PS + g:V_PS + g + 1],
                                       in1=a_hi[:, PG + g, :].bitcast(F32), op0=ALU.mult,
                                       op1=ALU.subtract).then_inc(evac[n % NS], 1)

            def out_pool(k):
                add_to_h(k, SLOT["outp", k], FULL)
                if k % 2:
                    split_lo(2 * B_OUTC + k // 2)

            for k in range(OUT_MEAN):
                out_pool(k)
                run_taps(OUT_STEP, (0, 1, 2))
            run_taps(len(PE_TAPS) + 2 * TAPS, (0, 1, 2))
            n = SLOT["mean",]
            filled(dve, n)
            for c in range(CT):
                V.tensor_tensor(conv[:, c, :], conv[:, c, :], slot_ap(n), ALU.subtract)\
                 .then_inc(centred if c < CT - 1 else evac[n % NS], 1)
            for k in range(OUT_MEAN, OUT_VAR):
                out_pool(k)
            recip(SLOT["var",], FULL)
            for c in range(CT):
                V.tensor_tensor(conv[:, c, :], conv[:, c, :], rstd[:, :], ALU.mult).then_inc(normed, 1)
            for c in range(CT):
                dve.wait_ge(c_hi_ready, c + 1)
                V.tensor_tensor(a_lo[:, c, :], work[c], a_hi[:, c, :].bitcast(F32), ALU.subtract)\
                 .then_inc(c_lo_ready, 1)
            for k in range(OUT_VAR, KD):
                out_pool(k)
            for k in range(KD):
                add_to_h(k, SLOT["outc", k], FULL)
                if k:
                    rest_of_u(1, k - 1, FULL)
                if k == KD - 1:
                    rest_of_u(1, k, FULL)
                if k:
                    add_squares(1, k - 1, FULL)
                if k % 2:
                    split_lo(2 * B_F0 + k // 2)
            add_squares(1, KD - 1, FULL)

            def ffn(layer, fb, tokens, it=0):
                a, b = tokens
                for i in range(2 * KD):
                    n = SLOT["ffn", layer, fb, i]
                    w = 2 * (B_F1 if layer else B_F0) + 16 * fb + i + 4
                    if fb == 0 and i == 0:
                        recip(SLOT["stat", 2 * layer + 1], tokens)
                    if i < KD:
                        t = KD * FBLK * layer + KD * fb + i
                        filled(dve, n, it)
                        if t >= 2:
                            dve.wait_ge(sq_ready, t - 1 + 8 * it)
                        V.scalar_tensor_tensor(out=relu[:, i % 2, a:b], in0=slot_ap(n, tokens), scalar=0.0,
                                               in1=rstd[:, a:b], op0=ALU.max, op1=ALU.mult)\
                         .then_inc(evac[n % NS], 1)
                        dve.wait_ge(a_hi_ready, t + 1 + 8 * it)
                        V.tensor_tensor(a_lo[:, i, a:b], act2[:, i % 2, a:b], a_hi[:, i, a:b].bitcast(F32),
                                        ALU.subtract).then_inc(a_lo_ready, 1)
                    else:
                        add_to_h(i - KD, n, tokens, it)
                    if w < 2 * NB:
                        split_lo(w, it)
                    if i >= KD and fb == FBLK - 1:
                        k = i - KD
                        prep(2 if layer == 0 else 4, k, tokens)
                        if layer and k:
                            copy_y(k - 1)

            def ffn_all(layer, tokens):
                ffn(layer, 0, tokens)
                with dve.Fori(0, FBLK - 2) as it:
                    ffn(layer, 1, tokens, it)
                ffn(layer, FBLK - 1, tokens)

            def copy_y(k):
                n = SLOT["y", k]
                filled(dve, n)
                V.tensor_copy(y_tok[:, :, P * k:P * (k + 1)],
                              ps[:, n % NS, 0:SEQ].rearrange("p (j d) -> p j d", d=P)).then_inc(evac[n % NS], 1)

            ffn_all(0, FULL)
            recip_tok(2)
            recip(SLOT["stat", 2], FULL)
            scale_out(r_sb, SLOT["r",], FULL, RANK)
            step(V.memset(mask, 1.0))
            V.memset(mask[:, META::CHUNK], 0.0).then_inc(dve_step, 1)
            steps[0] += 1

            def split_v(b):
                for j in range(2):
                    split_lo(2 * (B_V + b) + 4 + j)

            for hd in range(HEADS):
                n = SLOT["gate", hd]
                dve.wait_ge(abs_ready, hd + 1)
                V.tensor_scalar(logd[:, hd, :], slot_ap(n), vec[:, V_GB + hd:V_GB + hd + 1], 0.0,
                                ALU.add, ALU.min).then_inc(evac[n % NS], 1)
            split_v(0)
            split_v(1)
            dve.wait_ge(softplus_ready, 1)
            dve.wait_ge(dve_step, steps[0])
            for hd in range(HEADS):
                evacuated(dve, SLOT["gate", hd])
                ld, cum = logd[:, hd, :], decay[:, hd, :]
                step(V.tensor_tensor(ld, ld, cum, ALU.subtract))
                step(V.tensor_tensor_scan(cum, mask, ld, 0.0, ALU.mult, ALU.add))
                V.tensor_tensor(ld[:, 0:META], cum[:, META - 1:META].to_broadcast([P, META]),
                                cum[:, 0:META], ALU.subtract)
                cf = cum[:, META:].rearrange("p (c t) -> p c t", t=CHUNK)
                V.tensor_tensor(ld[:, META:].rearrange("p (c t) -> p c t", t=CHUNK),
                                cf[:, :, CHUNK - 1:CHUNK].to_broadcast([P, NCH - 1, CHUNK]), cf,
                                ALU.subtract).then_inc(suffix_ready, 1)
            split_v(2)
            for hd in range(HEADS):
                dve.wait_ge(decay_ready, hd + 1)
                V.tensor_tensor(decay[:, hd, :], logd[:, hd, :], rstd[:, :], ALU.mult).then_inc(kscale_ready, 1)
            split_v(3)
            dve.wait_ge(kscale_ready, HEADS)
            for hd in range(HEADS):
                n = SLOT["k", hd]
                filled(dve, n)
                if hd >= 2:
                    filled(dve, SLOT["kt", hd - 2])
                V.tensor_tensor(relu[:, hd % 2, :], slot_ap(n), decay[:, hd, :], ALU.mult)\
                 .then_inc(evac[n % NS], 1)
                split_lo(2 * B_K + hd + 4)

            def update_state(c):
                n = SLOT["kv", c]
                filled(dve, n)
                kv = ps[:, n % NS, :].rearrange("p (h v) -> p h v", h=HEADS)
                if c == 0:
                    V.tensor_copy(state[:, 0, :, :], kv).then_inc(evac[n % NS], 1)
                    return
                evacuated(dve, SLOT["kv", c - 1])
                for hd in range(HEADS):
                    last = V.scalar_tensor_tensor(out=state[:, c % 2, hd, :], in0=state[:, (c - 1) % 2, hd, :],
                                                  scalar=etot[:, hd, c:c + 1], in1=kv[:, hd, :],
                                                  op0=ALU.mult, op1=ALU.add)
                last.then_inc(evac[n % NS], 1)

            for hd in range(HEADS):
                n = SLOT["q", hd]
                filled(dve, n)
                V.scalar_tensor_tensor(out=q[:, hd, :], in0=slot_ap(n, FRAMES), scalar=HK ** -0.5,
                                       in1=rstd[:, META:], op0=ALU.mult, op1=ALU.mult)\
                 .then_inc(evac[n % NS], 1)
                split_lo(2 * B_Q + hd + 4)
                if hd:
                    update_state(hd - 1)

            def head_factors(j):
                evacuated(dve, SLOT["hn", j])
                step(V.reciprocal(rstd_head[:, :], std_head[:, :]))
                if j:
                    filled(dve, SLOT["hb", j - 1])
                V.tensor_tensor(head_diag, ident[:, None, :].to_broadcast([P, HEADS, P]),
                                rstd_head[:, :, None].to_broadcast([P, HEADS, P]), ALU.mult)\
                 .then_inc(diag_set, 1)

            def head_norm(j):
                n = SLOT["hb", j]
                filled(dve, n)
                r = ps[:, n % NS, 0:SEQ].rearrange("p (h t) -> p h t", h=HEADS)
                evacuated(dve, SLOT["o", 2 * j + 2])
                for m in range(HV // P):
                    part = o[:, m::HV // P, P * j:P * (j + 1)]
                    last = V.scalar_tensor_tensor(out=part, in0=part, scalar=vec[:, V_HG + m:V_HG + m + 1],
                                                  in1=r, op0=ALU.mult, op1=ALU.mult)
                last.then_inc(evac[n % NS], 1)

            def gate_o(n):
                k0, k1, a, b = GATE_PARTS[n]
                dve.wait_ge(gate_ready, k1)
                evacuated(dve, SLOT["hb", (b - 1) // P])
                V.tensor_tensor(gate[:, k0:k1, a:b], gate[:, k0:k1, a:b], o[:, k0:k1, a:b], ALU.mult)\
                 .then_inc(gated, 1)

            def rest_of_o(n):
                k0, k1, a, b = GATE_PARTS[n]
                dve.wait_ge(o_hi_ready, n + 1)
                V.tensor_tensor(gated_lo[:, k0:k1, a:b], gate[:, k0:k1, a:b],
                                gated_hi[:, k0:k1, a:b].bitcast(F32), ALU.subtract).then_inc(o_lo_ready, 1)

            for i in range(KD - 2):
                for n in GATE_AT.get(i, ()):
                    gate_o(n)
                if i % 2:
                    head_factors(i // 2)
                scale_out(gate[:, i, :], SLOT["g", i], FRAMES)
                split_lo(2 * B_G + i + 4)
                update_state(i + 3)
                if i % 2:
                    head_norm(i // 2)
                for n in GATE_AT.get(i, ()):
                    rest_of_o(n)
            for n in GATE_AT[KD - 2]:
                gate_o(n)
            scale_out(gate[:, KD - 2, :], SLOT["g", KD - 2], FRAMES)
            for n in GATE_AT[KD - 2]:
                rest_of_o(n)
            head_factors(TT - 1)
            split_lo(2 * B_G + KD - 2 + 4)
            gate_o(GATE_AT[KD - 1][0])
            head_norm(TT - 1)
            for n in GATE_AT[KD - 1][1:]:
                gate_o(n)
            for n in GATE_AT[KD - 1]:
                rest_of_o(n)
            scale_out(gate[:, KD - 1, :], SLOT["g", KD - 1], FRAMES)
            gate_o(len(GATE_PARTS) - 1)
            rest_of_o(len(GATE_PARTS) - 1)
            split_lo(2 * B_G + KD - 1 + 4)
            for k in range(KD):
                add_to_h(k, SLOT["out1", k], FRAMES)
                split_lo(2 * B_OUT1 + k + 4)
                prep(3, k, FRAMES)
            ffn_all(1, FRAMES)
            recip_tok(4)
            copy_y(KD - 1)
            dve.wait_ge(rstd_tok_ready, TT + 3)
            for k in range(KD):
                evacuated(dve, SLOT["y", k])
            for j in range(1, TT, 2):
                V.tensor_scalar(y_tok[:, j, :], y_tok[:, j, :], rstd_tok[:, j:j + 1], None, ALU.mult)\
                 .then_inc(dve_out, 1)

        @block.tensor
        def _(pe):
            mm = nc.tensor.matmul

            def start_slot(n, it=0):
                if n >= NS:
                    evacuated(pe, n - NS, it)

            def parts(tokens):
                if tokens == FULL:
                    return ((C0, 0, SPLIT), (BANK, SPLIT, TOK))
                return ((0, META, TOK),)

            def exact(n, lhs, rhs, count, tokens, before=None, it=0, middle=None, at=KD // 2, origin=0):
                start_slot(n, it)
                for k in range(count):
                    if middle and k == at:
                        middle()
                    if before:
                        before(k)
                    (l_hi, l_lo), (r_hi, r_lo) = lhs(k), rhs(k)
                    for i, (l, r) in enumerate(((l_hi, r_lo), (l_hi, r_hi), (l_lo, r_hi))):
                        for c, a, b in parts(tokens):
                            last = mm(ps[:, n % NS, c:c + b - a], l, r[:, a - origin:b - origin],
                                      start=(k == 0 and i == 0), stop=(k == count - 1 and i == 2))
                last.then_inc(filled_n, 1)

            def plain(n, pairs, tokens):
                for i, (l, r) in enumerate(pairs):
                    for c, a, b in parts(tokens):
                        last = mm(ps[:, n % NS, c:c + b - a], l, r[:, a:b], start=(i == 0),
                                  stop=(i == len(pairs) - 1))
                last.then_inc(filled_n, 1)

            def whalf(w):
                hi, lo = half_view(w_hi, w), half_view(w_lo, w)
                return lambda k: (hi[:, k, 0:P], lo[:, k, 0:P])

            def u(k):
                return u_hi[:, k, :], u_lo[:, k, :]

            def acts(k):
                return a_hi[:, k, :], a_lo[:, k, :]

            def u_wait(norm):
                return lambda k: pe.wait_ge(u_lo_ready, KD * (norm - 1) + k + 1)

            def project(n, w, tokens, before=None, middle=None, at=KD // 2):
                pe.wait_ge(w_lo_ready, w + 1)
                exact(n, whalf(w), u, KD, tokens, before, middle=middle, at=at)

            def stat(norm, tokens):
                n = SLOT["stat", norm]
                start_slot(n)
                pe.wait_ge(sq_sum_ready, KD * norm)
                plain(n, [(ones_d[:, :], sq_sum)], tokens)

            def tstat(norm):
                n = SLOT["tstat", norm]
                start_slot(n)
                pe.wait_ge(sq_sum_ready, KD * norm)
                for t in range(TT):
                    last = mm(ps[:, n % NS, t:t + 1], sq_sum[:, META + P * t:META + P * (t + 1)],
                              ones_d[:, 0:1], start=True, stop=True)
                if norm == 2:
                    last = mm(ps[0:META, n % NS, TT:TT + 1], sq_sum[:, 0:META], ones_d[:, 0:1],
                              start=True, stop=True)
                last.then_inc(filled_n, 1)

            def flip(dst, src, rows=P):
                return nc.tensor.transpose(dst, src, ident[0:rows, 0:rows])

            pe.wait_ge(consts, N_CONST)
            pe.wait_ge(gain_loaded, 16)
            n = SLOT["gain",]
            flip(ps[:, n % NS, 0:2 * KD], gain_rows[:, :], 2 * KD).then_inc(filled_n, 1)
            pe.wait_ge(x_normed_ready, 1)
            n = SLOT["xm",]
            for k in range(KD):
                last = flip(ps[:, n % NS, META * k:META * (k + 1)], meta_normed[:, P * k:P * (k + 1)], META)
            last.then_inc(filled_n, 1)
            for j in range(TT):
                pe.wait_ge(x_normed_ready, j + 2)
                for k in range(KD):
                    n = SLOT["x", k // 2]
                    if j == 0 and k % 2 == 0:
                        start_slot(n)
                    c = BANK * (k % 2) + P * j
                    last = flip(ps[:, n % NS, c:c + P], x_normed[:, j, P * k:P * (k + 1)])
                    if j == TT - 1 and k % 2:
                        last.then_inc(filled_n, 1)

            def flip_x(n, k):
                start_slot(n)
                flip(ps[:, n % NS, C0:C0 + META], xmeta[:, P * k:P * (k + 1)], META)
                for j in range(TT):
                    c = C0 + META + P * j
                    last = flip(ps[:, n % NS, c:c + P], xin[:, j, P * k:P * (k + 1)])
                last.then_inc(filled_n, 1)

            def input_wait(k):
                if k == 0:
                    evacuated(pe, SLOT["xm",])
                evacuated(pe, SLOT["x", k // 2])

            for c in range(CT):
                project(SLOT["glu", 2 * c], 2 * B_GLU + 2 * c, FULL,
                        input_wait if c == 0 else None)
                if c == 0:
                    n = SLOT["vec",]
                    start_slot(n)
                    pe.wait_ge(vec_loaded, 144)
                    flip(ps[:, n % NS, 0:NV - 2 * KD], vec_rows[:, :], NV - 2 * KD)
                    flip(ps[:, n % NS, BANK:BANK + TAPS * CT], cw_rows[:, :], TAPS * CT)\
                        .then_inc(filled_n, 1)
                project(SLOT["glu", 2 * c + 1], 2 * B_GLU + 2 * c + 1, FULL)
                flip_x(SLOT["h", 2 * c], 2 * c)
                flip_x(SLOT["h", 2 * c + 1], 2 * c + 1)

            def conv_taps(c):
                n = SLOT["conv", c]
                start_slot(n)
                pe.wait_ge(ci_lo_ready, c - 1)
                mine = [i for i, (tile, _) in enumerate(PE_TAPS) if tile == c]
                for i in mine:
                    t = PE_TAPS[i][1]
                    pe.wait_ge(diag_ready, i + 1)
                    d_hi, d_lo = diag_hi[:, i % DIAGS, :], diag_lo[:, i % DIAGS, :]
                    x_hi, x_lo = ci_hi[:, c - 2, t:t + TOK], ci_lo[:, c - 2, t:t + TOK]
                    for m, (l, r) in enumerate(((d_hi, x_lo), (d_hi, x_hi), (d_lo, x_hi))):
                        for col, a, b in parts(FULL):
                            last = mm(ps[:, n % NS, col:col + b - a], l, r[:, a:b],
                                      start=(i == mine[0] and m == 0), stop=(i == mine[-1] and m == 2))
                    last.then_inc(filled_n if i == mine[-1] else diag_used, 1)

            conv_taps(2)
            for g in range(PG):
                project(SLOT["p", g], 2 * B_POOL + g, FULL)
            conv_taps(3)
            pe.wait_ge(small_lo, 2)
            for g in range(PG):
                exact(SLOT["mix", g], lambda k: (pw_hi[:, g, :], pw_lo[:, g, :]),
                      lambda k: (a_hi[:, g, :], a_lo[:, g, :]), 1, FULL,
                      lambda k: pe.wait_ge(pd_lo_ready, g + 1))

            def project_out0(stage, b, k, first, before):
                w = 2 * b + k // 2
                pe.wait_ge(w_lo_ready, w + 1)
                hi, lo = half_view(w_hi, w), half_view(w_lo, w)
                cols = slice(P * (k % 2), P * (k % 2 + 1))
                exact(SLOT[stage, k], lambda j: (hi[:, j, cols], lo[:, j, cols]),
                      lambda j: (a_hi[:, first + j, :], a_lo[:, first + j, :]), KD // 2, FULL,
                      before if k == 0 else None)

            def average(n, tiles, before):
                start_slot(n)
                for c in range(CT):
                    before(c)
                    for col, a, b in parts(FULL):
                        last = mm(ps[:, n % NS, col:col + b - a], ones_c[:, :], tiles[c][:, a:b],
                                  start=(c == 0), stop=(c == CT - 1))
                last.then_inc(filled_n, 1)

            def conv_done(c):
                mine = sum(tile == c for tile, _ in PE_TAPS)
                if mine:
                    evacuated(pe, SLOT["conv", c])
                if mine < TAPS:
                    pe.wait_ge(tap_done[c], TAPS - mine)

            for k in range(KD):
                if k == OUT_MEAN:
                    average(SLOT["mean",], [conv[:, c, :] for c in range(CT)], conv_done)
                if k == OUT_VAR:
                    average(SLOT["var",], work,
                            lambda c: pe.wait_ge(ln_sq_ready, c + 1))
                project_out0("outp", B_OUTP, k, PG, lambda j: evacuated(pe, SLOT["mix", j]))
            for k in range(KD):
                project_out0("outc", B_OUTC, k, 0, lambda j: pe.wait_ge(c_lo_ready, j + 1))

            def ffn(layer, fb, tokens, it=0):
                for i in range(2 * KD):
                    n = SLOT["ffn", layer, fb, i]
                    w = 2 * (B_F1 if layer else B_F0) + 16 * fb + i
                    t = KD * FBLK * layer + KD * fb
                    pe.wait_ge(w_lo_ready, w + 1 + 16 * it)
                    if i < KD:
                        exact(n, whalf(w), u, KD, tokens, u_wait(2 * layer + 1) if fb == i == 0 else None, it)
                    else:
                        exact(n, whalf(w), acts, KD, tokens,
                              (lambda k: pe.wait_ge(a_lo_ready, t + k + 1 + 8 * it)) if i == KD else None, it)
                    if fb == 0 and i == 0:
                        stat(2 * layer + 1, tokens)
                    if layer == 1 and fb == FBLK - 1 and i > KD:
                        flip_y(i - KD - 1)

            def ffn_all(layer, tokens):
                ffn(layer, 0, tokens)
                with pe.Fori(0, FBLK - 2) as it:
                    ffn(layer, 1, tokens, it)
                ffn(layer, FBLK - 1, tokens)

            def flip_y(k):
                n = SLOT["y", k]
                start_slot(n)
                pe.wait_ge(hg_ready, k + 1)
                for j in range(TT):
                    last = flip(ps[:, n % NS, P * j:P * (j + 1)], relu[:, k % 2, META + P * j:META + P * (j + 1)])
                last.then_inc(filled_n, 1)

            ffn_all(0, FULL)
            pe.wait_ge(small_lo, 3)
            exact(SLOT["r",], lambda k: (rw_hi[:, RANK * k:RANK * k + P], rw_lo[:, RANK * k:RANK * k + P]),
                  u, KD, FULL, u_wait(2))
            tstat(2)
            stat(2, FULL)

            def project_v(b):
                pe.wait_ge(w_lo_ready, 2 * (B_V + b) + 2)
                whole = [t[:, (B_V + b) % 2, :].rearrange("p (k n) -> p k n", k=KD) for t in (w_hi, w_lo)]
                for t in range(TT + 1):
                    n = SLOT["v", b, t]
                    a = META + P * t if t < TT else 0
                    start_slot(n)
                    for k in range(KD):
                        hi, lo = u_hi[:, k, a:a + P], u_lo[:, k, a:a + P]
                        for i, (l, r) in enumerate(((hi, whole[1]), (hi, whole[0]), (lo, whole[0]))):
                            last = mm(ps[:, n % NS, 0:256], l, r[:, k, :], start=(k == 0 and i == 0),
                                      stop=(k == KD - 1 and i == 2))
                    last.then_inc(filled_n, 1)

            project_v(0)
            evacuated(pe, SLOT["r",])
            pe.wait_ge(small_loaded, 48)
            for hd in range(HEADS):
                start_slot(SLOT["gate", hd])
                plain(SLOT["gate", hd], [(gw2[:, HK * hd:HK * (hd + 1)], r_sb)], FULL)
            for b in range(1, 4):
                project_v(b)

            def flip_k(hd):
                n = SLOT["kt", hd]
                start_slot(n)
                evacuated(pe, SLOT["k", hd])
                kd = relu[:, hd % 2, :]
                for j in range(TT):
                    flip(ps[:, n % NS, P * j:P * (j + 1)], kd[:, META + P * j:META + P * (j + 1)])
                flip(ps[:, n % NS, BANK:BANK + P], kd[:, 0:P]).then_inc(filled_n, 1)

            def project_k(hd):
                project(SLOT["k", hd], 2 * B_K + hd, FULL)

            def project_q(hd):
                project(SLOT["q", hd], 2 * B_Q + hd, FRAMES)

            def chunk_kv(c):
                n = SLOT["kv", c]
                start_slot(n)
                if c == 0:
                    for hd in range(HEADS):
                        evacuated(pe, SLOT["kt", hd])
                    for t in range(TT + 1):
                        evacuated(pe, SLOT["v", 3, t])
                    kc, vc = k_meta[:, :], v_meta[:, :]
                else:
                    j, r = (c - 1) // 2, CHUNK * ((c - 1) % 2)
                    kc, vc = k_tok[r:r + CHUNK, j, :], v_tok[r:r + CHUNK, j, :]
                for hd in range(HEADS):
                    last = mm(ps[:, n % NS, HV * hd:HV * (hd + 1)], kc[:, HK * hd:HK * (hd + 1)],
                              vc[:, HV * hd:HV * (hd + 1)], start=True, stop=True)
                last.then_inc(filled_n, 1)

            def chunk_o(c):
                n = SLOT["o", c]
                start_slot(n)
                evacuated(pe, SLOT["kv", c])
                if c == 1:
                    for hd in range(HEADS):
                        evacuated(pe, SLOT["q", hd])
                for hd in range(HEADS):
                    for m in range(HV // P):
                        k = hd * (HV // P) + m
                        last = mm(ps[:, n % NS, CHUNK * k:CHUNK * (k + 1)],
                                  state[:, c % 2, hd, P * m:P * (m + 1)],
                                  q[:, hd, CHUNK * (c - 1):CHUNK * c], start=True, stop=True)
                last.then_inc(filled_n, 1)

            def head_square_sum(j):
                n = SLOT["hn", j]
                start_slot(n)
                pe.wait_ge(o_sq_ready, j + 1)
                for hd in range(HEADS):
                    for m in range(HV // P):
                        last = mm(ps[:, n % NS, hd:hd + 1], o_sq[:, m, hd, :], ones_v[:, 0:1],
                                  start=(m == 0), stop=(m == HV // P - 1))
                last.then_inc(filled_n, 1)

            def head_spread(j):
                n = SLOT["hb", j]
                start_slot(n)
                pe.wait_ge(diag_set, j + 1)
                mm(ps[:, n % NS, 0:SEQ], ones_1[:, :], head_diag.rearrange("p h t -> p (h t)"),
                   start=True, stop=True).then_inc(filled_n, 1)

            for hd in range(HEADS):
                project_k(hd)
                if hd:
                    flip_k(hd - 1)
            project_q(0)
            flip_k(HEADS - 1)
            for c in range(3):
                project_q(c + 1)
                chunk_kv(c)
            chunk_o(1)
            for i in range(KD - 2):
                project(SLOT["g", i], 2 * B_G + i, FRAMES,
                        middle=(lambda: head_square_sum(i // 2)) if i % 2 else None)
                chunk_o(i + 2)
                chunk_kv(i + 3)
                if i % 2:
                    head_spread(i // 2)
            project(SLOT["g", KD - 2], 2 * B_G + KD - 2, FRAMES, middle=lambda: chunk_o(NCH - 1), at=2)
            head_square_sum(TT - 1)
            project(SLOT["g", KD - 1], 2 * B_G + KD - 1, FRAMES, middle=lambda: head_spread(TT - 1), at=3)

            def gated_wait(k):
                pe.wait_ge(o_lo_ready, max(n for n, part in enumerate(GATE_PARTS)
                                           if part[0] <= k < part[1]) + 1)

            for k in range(KD):
                w = 2 * B_OUT1 + k
                pe.wait_ge(w_lo_ready, w + 1)
                exact(SLOT["out1", k], whalf(w), lambda j: (gated_hi[:, j, :], gated_lo[:, j, :]), KD,
                      FRAMES, gated_wait if k == 0 else None, origin=META)
            ffn_all(1, FRAMES)
            tstat(4)
            flip_y(KD - 1)


_INS = ["x", "meta_tokens", "mix_norm_g", "ffn_norm_g", "ffn_w1", "ffn_w2", "cp_w_in", "cp_conv_w",
        "cp_conv_b", "cp_ln_g", "cp_ln_b", "cp_pool_w", "cp_pool_scale", "cp_w_out", "gla_w_in",
        "gla_gate_w2", "gla_gate_b", "gla_head_g", "gla_w_out", "final_norm_g"]


def kernel(**inputs):
    import numpy as _np
    import concourse.bacc as _bacc
    from concourse import mybir as _mybir
    from concourse.bass_utils import run_bass_kernel_spmd as _run

    nc = _bacc.Bacc("TRN2", target_bir_lowering=False, num_devices=1)
    arrays, args = {}, []
    for name in _INS:
        a = _np.ascontiguousarray(inputs[name])
        arrays[f"in_{name}_dram"] = a
        args.append(nc.dram_tensor(f"in_{name}_dram", a.shape, _mybir.dt.from_np(a.dtype),
                                   kind="ExternalInput").ap())
    shape = inputs["x"].shape
    args.append(nc.dram_tensor("out_dram", shape, _mybir.dt.float32, kind="ExternalOutput").ap())
    build_trunk(nc, *args)
    r = _run(nc, [arrays], core_ids=[0])
    return r.results[0]["out_dram"]
```

```python
from contextlib import ExitStack

import concourse.bass as bass
from concourse import mybir

F32 = mybir.dt.float32
F32R = mybir.dt.float32r
ALU = mybir.AluOpType
ACT = mybir.ActivationFunctionType

P = 128
EPS = 1e-5
META = 16
SEQ = 512
TOK = META + SEQ
D = 1024
KD = D // P
FF = 4 * D
FBLK = FF // D
CONV = 512
CT = CONV // P
TAPS = 31
PG = 4
WMAX = 16
HEADS = 4
DK = 512
HK = DK // HEADS
DV = 1024
HV = DV // HEADS
RANK = 16
GATE_NORM = 16.0
CHUNK = 64
NCH = SEQ // CHUNK + 1
TT = SEQ // P
NS = 4
BANK = 512
SPLIT = META + 2 * P
C0 = BANK - SPLIT
PE_TAPS = [(2, t) for t in range(12)] + [(3, t) for t in range(31)]
DIAGS = 8
MIX_BEFORE = 10
OUT_MEAN, OUT_VAR = 3, 5
CONV_STEP, POOL_STEP, PD_STEP, MIX_STEP, OUT_STEP = 20, 2, 2, (2, 2, 1, 0), 4
V_MIX, V_FFN, V_FIN = 0, 2 * KD, 4 * KD
V_CB = V_FIN + KD
V_LG, V_LB, V_PS, V_GB = V_CB + CT, V_CB + 2 * CT, V_CB + 3 * CT, V_CB + 4 * CT
V_HG = V_GB + DK // P
NV = V_HG + HV // P
B_GLU, B_POOL = 0, CT
B_OUTP = B_POOL + 2
B_OUTC = B_OUTP + 2
B_F0 = B_OUTC + 2
B_V = B_F0 + 8 * FBLK
B_K, B_Q, B_G = B_V + 4, B_V + 6, B_V + 8
B_OUT1 = B_G + 4
B_F1 = B_OUT1 + 4
NB = B_F1 + 8 * FBLK


def plan_slots():
    order = [("gain",), ("xm",)] + [("x", i) for i in range(KD // 2)]
    for c in range(CT):
        order += [("glu", 2 * c)] + [("vec",)] * (c == 0)
        order += [("glu", 2 * c + 1), ("h", 2 * c), ("h", 2 * c + 1)]
    order += [("conv", 2)] + [("p", g) for g in range(PG)]
    order += [("mix", 0), ("mix", 1), ("conv", 3), ("mix", 2), ("mix", 3)]
    order += [("outp", k) for k in range(OUT_MEAN)] + [("mean",)]
    order += [("outp", k) for k in range(OUT_MEAN, OUT_VAR)] + [("var",)]
    order += [("outp", k) for k in range(OUT_VAR, KD)] + [("outc", k) for k in range(KD)]
    slot = {}

    def add(names):
        for n in names:
            slot[n] = len(slot)

    def ffn(layer, norm):
        for fb in range(FBLK):
            for i in range(2 * KD):
                if layer == 1 and fb == FBLK - 1 and i >= 2 * KD - 2:
                    break
                yield ("ffn", layer, fb, i)
                if fb == 0 and i == 0:
                    yield ("stat", norm)
                if layer == 1 and fb == FBLK - 1 and i > KD:
                    yield ("y", i - KD - 1)
        if layer == 1:
            yield from (("end", 0, KD - 2), ("y", KD - 3), ("end", 0, KD - 1), ("y", KD - 2, 0),
                        ("end", 1, KD - 2), ("tstat", 4, 0), ("y", KD - 1, 0), ("end", 1, KD - 1),
                        ("y", KD - 2, 1), ("tstat", 4, 1), ("y", KD - 1, 1))

    add(order)
    add(ffn(0, 1))
    add([("r",), ("tstat", 2), ("stat", 2)])
    for b in range(4):
        add(("v", b, t) for t in range(TT + 1))
        if b == 0:
            add(("gate", n) for n in range(HEADS))
    for h in range(HEADS):
        add([("k", h)] + ([("kt", h - 1)] if h else []))
    add([("q", 0), ("kt", HEADS - 1), ("q", 1), ("kv", 0), ("q", 2), ("kv", 1), ("q", 3), ("kv", 2),
         ("o", 1)])
    for i in range(KD - 2):
        add([("hn", i // 2)] * (i % 2) + [("g", i), ("o", i + 2), ("kv", i + 3)] + [("hb", i // 2)] * (i % 2))
    add([("o", NCH - 1), ("g", KD - 2), ("hn", TT - 1), ("hb", TT - 1), ("g", KD - 1)])
    add(("out1", k) for k in range(KD))
    add(ffn(1, 3))
    return slot


SLOT = plan_slots()


def half_reader(n):
    b, j = divmod(n, 2)
    if b < B_POOL:
        return SLOT["glu", n]
    if b < B_OUTP:
        return SLOT["p", n - 2 * B_POOL]
    if b < B_OUTC:
        return SLOT["outp", 2 * (n - 2 * B_OUTP) + 1]
    if b < B_F0:
        return SLOT["outc", 2 * (n - 2 * B_OUTC) + 1]
    if b < B_V:
        return SLOT["ffn", 0, (b - B_F0) // 8, (n - 2 * B_F0) % 16]
    if b < B_K:
        return SLOT["v", b - B_V, TT]
    if b < B_Q:
        return SLOT["k", n - 2 * B_K]
    if b < B_G:
        return SLOT["q", n - 2 * B_Q]
    if b < B_OUT1:
        return SLOT["g", n - 2 * B_G]
    if b < B_F1:
        return SLOT["out1", n - 2 * B_OUT1]
    return SLOT["ffn", 1, (b - B_F1) // 8, (n - 2 * B_F1) % 16]


def half_freed(n):
    changed = n // 2 in (B_OUTP, B_OUTP + 1, B_F0, B_F0 + 1)
    return half_reader(n - 4 + (1 - n % 2 if changed else 0))


def raw_count(b):
    return 16 * (b // 2 + 1 + min(b // 2 + 1, B_POOL // 2))


def build_trunk(nc, x, meta_tokens, mix_norm_g, ffn_norm_g, ffn_w1, ffn_w2, cp_w_in, cp_conv_w,
                cp_conv_b, cp_ln_g, cp_ln_b, cp_pool_w, cp_pool_scale, cp_w_out, gla_w_in,
                gla_gate_w2, gla_gate_b, gla_head_g, gla_w_out, final_norm_g, out):
    with ExitStack() as ctx:
        def sb(name, shape, dt=F32, stack=ctx):
            return stack.enter_context(nc.sbuf_tensor(name, shape, dt))

        def sem(name):
            return ctx.enter_context(nc.semaphore(name))

        ps = ctx.enter_context(nc.psum_tensor("ps", [P, NS, 2 * BANK], F32))

        h = sb("h", [P, KD, TOK])
        u_hi = sb("u_hi", [P, KD, TOK], F32R)
        u_lo = sb("u_lo", [P, KD, TOK], F32R)
        h_sq = sb("h_sq", [P, 2, TOK])
        sq_sum = sb("sq_sum", [P, TOK])
        std = sb("std", [P, TOK])
        rstd = sb("rstd", [P, TOK])
        ms_tok = sb("ms_tok", [P, TT + 1])
        std_tok = sb("std_tok", [P, TT + 1])
        rstd_tok = sb("rstd_tok", [P, TT + 1])
        std_head = sb("std_head", [P, HEADS])
        rstd_head = sb("rstd_head", [P, HEADS])
        raw = sb("raw", [P, 2, 2 * KD * P])
        w_hi = sb("w_hi", [P, 2, 2 * KD * P], F32R)
        w_lo = sb("w_lo", [P, 2, 2 * KD * P], F32R)
        ident = sb("ident", [P, P])
        ones_d = sb("ones_d", [P, P])
        ones_c = sb("ones_c", [P, P])
        ones_v = sb("ones_v", [P, P])
        ones_1 = sb("ones_1", [P, P])
        eps = sb("eps", [P, 1])
        gain_rows = sb("gain_rows", [2 * KD, P])
        vec_rows = sb("vec_rows", [NV - 2 * KD, P])
        cw_rows = sb("cw_rows", [TAPS * CT, P])
        vec = sb("vec", [P, NV])
        cw = sb("cw", [P, TAPS * CT])
        gw2 = sb("gw2", [RANK, DK])
        rw = sb("rw", [P, KD * RANK])
        rw_hi = sb("rw_hi", [P, (KD - 1) * RANK + P], F32R)
        rw_lo = sb("rw_lo", [P, (KD - 1) * RANK + P], F32R)
        relu = sb("relu", [P, 2, TOK])
        act2 = sb("act2", [P, 2, TOK])

        with ExitStack() as part:
            with ExitStack() as start:
                xin = sb("xin", [P, TT, D], F32, start)
                xmeta = sb("xmeta", [META, D], F32, start)
            a_hi = sb("a_hi", [P, KD, TOK], F32R, part)
            with ExitStack() as early:
                sb("below_pin", [P, PG, TOK], F32, early)
                pin = sb("pin", [P, PG, WMAX + TOK], F32, early)
            a_lo = sb("a_lo", [P, KD, TOK], F32R, part)
            sb("pin_end", [P, PG, WMAX], F32, part)
            with ExitStack() as mixer0:
                win = sb("win", [P, 2, WMAX + TOK], F32, mixer0)
                rcount = sb("rcount", [P, WMAX], F32, mixer0)
                pw = sb("pw", [P, PG, P], F32, mixer0)
                pw_hi = sb("pw_hi", [P, PG, P], F32R, mixer0)
                pw_lo = sb("pw_lo", [P, PG, P], F32R, mixer0)
                conv_in = sb("conv_in", [P, CT, TAPS - 1 + TOK], F32, mixer0)
                conv = sb("conv", [P, CT, TOK], F32, mixer0)
                ci_hi = sb("ci_hi", [P, 2, TAPS - 1 + TOK], F32R, mixer0)
                ci_lo = sb("ci_lo", [P, 2, TAPS - 1 + TOK], F32R, mixer0)
                cw_hi = sb("cw_hi", [P, TAPS * CT], F32R, mixer0)
                cw_lo = sb("cw_lo", [P, TAPS * CT], F32, mixer0)
                diag_hi = sb("diag_hi", [P, DIAGS, P], F32R, mixer0)
                diag_lo = sb("diag_lo", [P, DIAGS, P], F32R, mixer0)
            with ExitStack() as last:
                y_tok = sb("y_tok", [P, TT, D], F32, last)
        with ExitStack() as gla:
            v_tok = sb("v_tok", [P, TT, DV], F32, gla)
            v_meta = sb("v_meta", [META, DV], F32, gla)
            k_tok = sb("k_tok", [P, TT, DK], F32, gla)
            k_meta = sb("k_meta", [META, DK], F32, gla)
            decay = sb("decay", [P, HEADS, TOK], F32, gla)
            with ExitStack() as gated_parts:
                gated_lo = sb("gated_lo", [P, KD, SEQ], F32R, gated_parts)
                gated_hi = sb("gated_hi", [P, KD, SEQ], F32R, gated_parts)
            gate = sb("gate", [P, KD, SEQ], F32, gla)
            o = sb("o", [P, KD, SEQ], F32, gla)
            state = sb("state", [P, 2, HEADS, HV], F32, gla)
            etot = sb("etot", [P, HEADS, NCH], F32, gla)
        q = decay[:, :, META:]
        mask = state[:, 0, :, :].rearrange("p h v -> p (h v)")[:, 0:TOK]
        logd = o[:, :, :].rearrange("p k t -> p (k t)")[:, 0:HEADS * TOK].rearrange(
            "p (h t) -> p h t", h=HEADS)
        o_sq = relu[:, :, :].rearrange("p a t -> p (a t)")[:, 0:KD * P].rearrange(
            "p (m h t) -> p m h t", m=HV // P, h=HEADS)
        r_raw, r_sb = relu[0:RANK, 1, :], relu[0:RANK, 0, :]
        work = [relu[:, 0, :], relu[:, 1, :], act2[:, 0, :], act2[:, 1, :]]
        conv_sum, centred_sq_sum = h_sq[:, 0, :], h_sq[:, 1, :]
        x_normed = h[:, :, :].rearrange("p k t -> p (k t)")[:, 0:TT * D].rearrange(
            "p (j d) -> p j d", d=D)
        meta_normed = relu[0:META, :, :].rearrange("p a t -> p (a t)")[:, 0:D]
        squares = conv[:, :, :].rearrange("p c t -> p (c t)")[:, 0:D]
        u_meta = sq_sum[:, 0:KD * META].rearrange("p (k t) -> p k t", t=META)
        head_diag = act2[:, 0, 0:SEQ].rearrange("p (h t) -> p h t", h=HEADS)

        x_loaded = [sem(f"x_loaded{i}") for i in range(TT)]
        x_squared = sem("x_squared")
        x_std = sem("x_std")
        x_normed_ready = sem("x_normed_ready")
        u_meta_lo_ready = sem("u_meta_lo_ready")
        u_meta_hi_ready = sem("u_meta_hi_ready")
        gain_loaded = sem("gain_loaded")
        meta_loaded = sem("meta_loaded")
        vec_loaded = sem("vec_loaded")
        small_loaded = sem("small_loaded")
        raw_loaded = [sem(f"raw_loaded{i}") for i in range(2)]
        consts = sem("consts")
        filled_n = sem("filled")
        evac = [sem(f"evac{i}") for i in range(NS)]
        w_hi_ready = sem("w_hi_ready")
        w_lo_ready = sem("w_lo_ready")
        small_hi = sem("small_hi")
        small_lo = sem("small_lo")
        h_sq_ready = sem("h_sq_ready")
        u_hi_ready = sem("u_hi_ready")
        u_lo_ready = sem("u_lo_ready")
        sq_sum_ready = sem("sq_sum_ready")
        rstd_ready = sem("rstd_ready")
        rstd_tok_ready = sem("rstd_tok_ready")
        tap_done = [sem(f"tap_done{c}") for c in range(CT)]
        ci_hi_ready = sem("ci_hi_ready")
        ci_lo_ready = sem("ci_lo_ready")
        diag_ready = sem("diag_ready")
        diag_used = sem("diag_used")
        dve_step = sem("dve_step")
        pin_zeroed = sem("pin_zeroed")
        pd_ready = sem("pd_ready")
        pd_hi_ready = sem("pd_hi_ready")
        pd_lo_ready = sem("pd_lo_ready")
        mix_hi_ready = sem("mix_hi_ready")
        centred = sem("centred")
        ln_sq_ready = sem("ln_sq_ready")
        conv_summed = sem("conv_summed")
        ln_sq_summed = sem("ln_sq_summed")
        normed = sem("normed")
        silu_ready = sem("silu_ready")
        sq_ready = sem("sq_ready")
        a_hi_ready = sem("a_hi_ready")
        a_lo_ready = sem("a_lo_ready")
        c_hi_ready = sem("c_hi_ready")
        c_lo_ready = sem("c_lo_ready")
        abs_ready = sem("abs_ready")
        gexp_ready = sem("gexp_ready")
        softplus_ready = sem("softplus_ready")
        suffix_ready = sem("suffix_ready")
        decay_ready = sem("decay_ready")
        kscale_ready = sem("kscale_ready")
        r_ready = sem("r_ready")
        gate_ready = sem("gate_ready")
        o_sq_ready = sem("o_sq_ready")
        o_sq_summed = sem("o_sq_summed")
        diag_set = sem("diag_set")
        gated = sem("gated")
        o_hi_ready = sem("o_hi_ready")
        o_lo_ready = sem("o_lo_ready")
        hg_ready = sem("hg_ready")
        act_out = sem("act_out")
        dve_out = sem("dve_out")
        stored = sem("stored")
        N_CONST = 14

        def units(layer, fb):
            return 2 * KD - (2 if layer == 1 and fb == FBLK - 1 else 0)

        def filled(eng, n, it=0):
            eng.wait_ge(filled_n, n + 1 + 16 * it)

        def evacuated(eng, n, it=0):
            eng.wait_ge(evac[n % NS], n // NS + 1 + 4 * it)

        GATE_PARTS = [(0, 2, 0, P), (2, 4, 0, P), (0, 4, P, 2 * P), (4, 6, 0, 2 * P), (0, 6, 2 * P, 3 * P),
                      (6, 7, 0, 3 * P), (0, 4, 3 * P, SEQ), (4, 7, 3 * P, SEQ), (7, 8, 0, SEQ)]
        GATE_AT = {2: (0,), 4: (1, 2), 6: (3, 4), 7: (5, 6, 7)}

        def diag_free(eng, i):
            c = PE_TAPS[i][0]
            if i + 1 == len(PE_TAPS) or PE_TAPS[i + 1][0] != c:
                filled(eng, SLOT["conv", c])
            else:
                eng.wait_ge(diag_used, i + 1 - (c - 2))

        FULL = (0, TOK)
        FRAMES = (META, TOK)

        HALVES = [(META + SEQ // 2 * i, META + SEQ // 2 * (i + 1)) for i in range(2)]

        def pcols(tokens):
            return (C0, C0 + TOK) if tokens == FULL else (0, tokens[1] - tokens[0])

        def slot_ap(n, tokens=FULL, rows=P):
            a, b = pcols(tokens)
            return ps[0:rows, n % NS, a:b]

        def half_view(t, n):
            b, j = divmod(n, 2)
            if B_OUTP <= b < B_F0:
                return t[:, b % 2, :].rearrange("p (k n) -> p k n", k=KD // 2)[:, :, 2 * P * j:2 * P * (j + 1)]
            return t[:, b % 2, :].rearrange("p (k n) -> p k n", k=KD)[:, :, P * j:P * (j + 1)]

        def split_hi(n, it=0):
            act = nc.scalar
            act.wait_ge(raw_loaded[n // 2 % 2], raw_count(n // 2) + 64 * it)
            if n >= 4:
                filled(act, half_freed(n), it)
            act.activation(half_view(w_hi, n), half_view(raw, n), ACT.Copy).then_inc(w_hi_ready, 1)

        def split_lo(n, it=0):
            dve = nc.vector
            if n >= 4:
                filled(dve, half_freed(n), it)
            dve.wait_ge(w_hi_ready, n + 1 + 16 * it)
            dve.tensor_tensor(half_view(w_lo, n), half_view(raw, n), half_view(w_hi, n).bitcast(F32),
                              ALU.subtract).then_inc(w_lo_ready, 1)

        block = ctx.enter_context(nc.Block())

        @block.sync
        def _(sp):
            x_v = x[0].rearrange("(j p) d -> p j d", p=P)

            def load_x(j):
                sp.dma_start(xin[:, j, :], x_v[:, j, :]).then_inc(x_loaded[j], 16)

            def reusable(b, fb=0):
                if b >= 2:
                    sp.wait_ge(w_lo_ready, 2 * (b - 1) + 16 * fb)

            def load(b, src, fb=0):
                reusable(b, fb)
                sp.dma_start(raw[:, b % 2, :].rearrange("p (k n) -> p k n", n=src.shape[2]), src)\
                  .then_inc(raw_loaded[b % 2], 16)

            cp_in = cp_w_in[0].rearrange("(k p) n -> p k n", p=P)
            cp_out = cp_w_out[0].rearrange("(k p) n -> p k n", p=P)
            gla_in = gla_w_in[0].rearrange("(k p) n -> p k n", p=P)
            gla_out = gla_w_out[0].rearrange("(k p) n -> p k n", p=P)

            def load_glu(c):
                reusable(B_GLU + c)
                for j in range(2):
                    n = 2 * (B_GLU + c) + j
                    at = CONV * (1 - j) + P * c
                    sp.dma_start(half_view(raw, n), cp_in[:, :, at:at + P])\
                      .then_inc(raw_loaded[c % 2], 16)

            def load_ffn(layer, first):
                w1 = ffn_w1[layer].rearrange("(k p) n -> p k n", p=P)
                w2 = ffn_w2[layer].rearrange("(k p) n -> p k n", p=P)
                with sp.Fori(0, FBLK) as fb:
                    for j in range(4):
                        load(first + j, w1[:, :, bass.ds(fb * D + 256 * j, 256)], fb)
                    for j in range(4):
                        load(first + 4 + j, w2[:, bass.ds(fb * KD, KD), 256 * j:256 * (j + 1)], fb)

            load_x(0)
            for j in range(1, TT):
                load_x(j)
            load_glu(0)
            sp.dma_start(vec_rows[0:2 * KD, :], ffn_norm_g.rearrange("l (k p) -> (l k) p", p=P))\
               .then_inc(vec_loaded, 16)
            at = V_FIN - 2 * KD
            sp.dma_start(vec_rows[at:at + KD, :], final_norm_g.rearrange("(k p) -> k p", p=P))\
               .then_inc(vec_loaded, 16)
            for v, row in ((cp_conv_b, V_CB), (cp_ln_g, V_LG), (cp_ln_b, V_LB), (cp_pool_scale, V_PS),
                           (gla_gate_b, V_GB), (gla_head_g, V_HG)):
                n, row = v.shape[1] // P, row - 2 * KD
                sp.dma_start(vec_rows[row:row + n, :], v[0].rearrange("(k p) -> k p", p=P))\
                   .then_inc(vec_loaded, 16)
            sp.dma_start(cw_rows[:, :], cp_conv_w[0].rearrange("t (c p) -> (t c) p", p=P))\
               .then_inc(vec_loaded, 16)
            sp.dma_start(pw[:, :, :], cp_pool_w[0].rearrange("g c d -> c g d")).then_inc(small_loaded, 16)
            sp.dma_start(rw[:, :].rearrange("p (k r) -> p k r", r=RANK),
                          gla_w_in[0].rearrange("(k p) n -> p k n", p=P)[:, :, 2 * DK + 2 * DV:])\
               .then_inc(small_loaded, 16)
            sp.dma_start(gw2[:, :], gla_gate_w2[0]).then_inc(small_loaded, 16)
            for c in range(1, CT):
                load_glu(c)
            for j in range(2):
                load(B_POOL + j, cp_in[:, :, 2 * CONV + 256 * j:2 * CONV + 256 * (j + 1)])
            for j in range(2):
                load(B_OUTP + j, cp_out[:, KD // 2:, 512 * j:512 * (j + 1)])
            for j in range(2):
                load(B_OUTC + j, cp_out[:, :KD // 2, 512 * j:512 * (j + 1)])
            load_ffn(0, B_F0)
            for b, at, n in ((B_V, 2 * DK, 4), (B_K, DK, 2), (B_Q, 0, 2), (B_G, 2 * DK + DV, 4)):
                for j in range(n):
                    load(b + j, gla_in[:, :, at + 256 * j:at + 256 * (j + 1)])
            for j in range(4):
                load(B_OUT1 + j, gla_out[:, :, 256 * j:256 * (j + 1)])
            load_ffn(1, B_F1)
            out_v = out[0].rearrange("(j p) d -> j p d", p=P)
            for j in range(TT):
                sp.wait_ge((act_out, dve_out)[j % 2], j // 2 + 1)
                sp.dma_start(out_v[j], y_tok[:, j, :]).then_inc(stored, 16)
            sp.wait_ge(stored, 16 * TT)

        @block.gpsimd
        def _(pool):
            pool.memset(ident[:, :], 0.0).then_inc(consts, 1)
            pool.wait_ge(consts, 1)
            pool.affine_select(out=ident[:, :], in_=ident[:, :], compare_op=ALU.not_equal, fill=1.0,
                               base=0, pattern=[[-1, P]], channel_multiplier=1).then_inc(consts, 1)
            pool.memset(ones_d[:, :], 1.0 / D).then_inc(consts, 1)
            pool.memset(ones_c[:, :], 1.0 / CONV).then_inc(consts, 1)
            pool.memset(ones_v[:, :], 1.0 / HV).then_inc(consts, 1)
            pool.memset(ones_1[:, :], 1.0).then_inc(consts, 1)
            pool.memset(eps[:, :], EPS).then_inc(consts, 1)
            pool.memset(conv_in[:, :, 0:TAPS - 1], 0.0).then_inc(consts, 1)
            pool.memset(win[:, :, 0:WMAX], 0.0).then_inc(consts, 1)
            pool.memset(rw_hi[:, KD * RANK:].bitcast(F32), 0.0).then_inc(consts, 1)
            pool.memset(rw_lo[:, KD * RANK:].bitcast(F32), 0.0).then_inc(consts, 1)
            for t in range(WMAX - 1):
                last = pool.memset(rcount[:, t:t + 1], 1.0 / (t + 1))
            last.then_inc(consts, 3)

        @block.scalar
        def _(act):
            def prep(norm, k, n, tokens):
                a, b = tokens
                evacuated(act, n)
                if norm < 4:
                    g = (V_MIX, V_FFN, V_MIX + KD, V_FFN + KD)[norm] + k
                    act.activation(u_hi[:, k, a:b], h[:, k, a:b], ACT.Copy, scale=vec[:, g:g + 1])\
                       .then_inc(u_hi_ready, 1)
                t = KD * (norm - 1) + k
                if t >= 2:
                    act.wait_ge(sq_sum_ready, t - 1)
                act.activation(h_sq[:, k % 2, a:b], h[:, k, a:b], ACT.Square).then_inc(h_sq_ready, 1)

            def stat(norm, tokens):
                n = SLOT["stat", norm]
                filled(act, n)
                act.activation(std[:, tokens[0]:tokens[1]], slot_ap(n, tokens), ACT.Sqrt,
                               bias=eps[:, :]).then_inc(evac[n % NS], 1)

            def tstat():
                n = SLOT["tstat", 2]
                filled(act, n)
                act.activation(std_tok[:, 0:TT], ps[:, n % NS, 0:TT], ACT.Sqrt, bias=eps[:, :])
                act.activation(std_tok[0:META, TT:TT + 1], ps[0:META, n % NS, TT:TT + 1],
                               ACT.Sqrt, bias=eps[0:META, :]).then_inc(evac[n % NS], 1)

            act.dma_start(xmeta[:, :], meta_tokens).then_inc(meta_loaded, 16)
            act.dma_start(gain_rows[:, :], mix_norm_g.rearrange("l (k p) -> (l k) p", p=P))\
               .then_inc(gain_loaded, 16)
            act.wait_ge(consts, N_CONST)
            act.activation(std_head[:, 0:1], eps[:, :], ACT.Sqrt)
            act.wait_ge(meta_loaded, 16)
            act.activation(meta_normed, xmeta[:, :], ACT.Square, accum_out=ms_tok[0:META, TT:TT + 1])\
               .then_inc(x_squared, 1)
            act.wait_ge(x_squared, 1)
            act.activation(std_tok[0:META, TT:TT + 1], ms_tok[0:META, TT:TT + 1], ACT.Sqrt,
                           bias=eps[0:META, :], scale=1.0 / D).then_inc(x_std, 1)
            for j in range(TT):
                act.wait_ge(x_loaded[j], 16)
                act.activation(squares, xin[:, j, :], ACT.Square, accum_out=ms_tok[:, j:j + 1])\
                   .then_inc(x_squared, 1)
                act.wait_ge(x_squared, j + 2)
                act.activation(std_tok[:, j:j + 1], ms_tok[:, j:j + 1], ACT.Sqrt, bias=eps[:, :],
                               scale=1.0 / D).then_inc(x_std, 1)
                if j == 0:
                    n = SLOT["gain",]
                    filled(act, n)
                    act.activation(vec[:, 0:2 * KD], ps[:, n % NS, 0:2 * KD], ACT.Copy)\
                       .then_inc(evac[n % NS], 1)
                if j == 1:
                    evacuated(act, SLOT["xm",])
                    act.activation(u_hi[:, :, 0:META], u_meta, ACT.Copy).then_inc(u_meta_hi_ready, 1)
            evacuated(act, SLOT["gain",])

            def x_bank(k):
                return ps[:, SLOT["x", k // 2] % NS, BANK * (k % 2):BANK * (k % 2) + SEQ]

            split_hi(0)
            for k in range(KD):
                filled(act, SLOT["x", k // 2])
                act.activation(u_hi[:, k, META:], x_bank(k), ACT.Copy, scale=vec[:, V_MIX + k:V_MIX + k + 1])\
                   .then_inc(u_hi_ready, 1)
            split_hi(1)
            n = SLOT["vec",]
            filled(act, n)
            act.activation(vec[:, 2 * KD:], ps[:, n % NS, 0:NV - 2 * KD], ACT.Copy)
            act.activation(cw[:, :], ps[:, n % NS, BANK:BANK + TAPS * CT], ACT.Copy)\
               .then_inc(evac[n % NS], 1)
            split_hi(2)
            evacuated(act, n)
            act.activation(cw_hi[:, :], cw[:, :], ACT.Copy).then_inc(small_hi, 1)
            act.wait_ge(small_loaded, 48)
            act.activation(pw_hi[:, :, :], pw[:, :, :], ACT.Copy).then_inc(small_hi, 1)
            act.activation(rw_hi[:, 0:KD * RANK], rw[:, :], ACT.Copy).then_inc(small_hi, 1)
            split_hi(3)
            built = [0]

            def build_diags(count):
                for i in range(built[0], min(built[0] + count, len(PE_TAPS))):
                    c, t = PE_TAPS[i]
                    col = t * CT + c
                    if i >= DIAGS:
                        diag_free(act, i - DIAGS)
                    act.activation(diag_hi[:, i % DIAGS, :], ident[:, :], ACT.Copy,
                                   scale=cw_hi[:, col:col + 1].bitcast(F32))
                    act.activation(diag_lo[:, i % DIAGS, :], ident[:, :], ACT.Copy,
                                   scale=cw_lo[:, col:col + 1]).then_inc(diag_ready, 1)
                    built[0] = i + 1

            def copy_h(k):
                n = SLOT["h", k]
                filled(act, n)
                act.activation(h[:, k, :], slot_ap(n), ACT.Copy).then_inc(evac[n % NS], 1)

            act.wait_ge(small_hi, 1)
            act.wait_ge(small_lo, 1)
            for c in range(CT):
                n = SLOT["glu", 2 * c]
                filled(act, n)
                if c >= 2:
                    evacuated(act, SLOT["glu", 2 * (c - 2) + 1])
                act.activation(act2[:, c % 2, :], slot_ap(n), ACT.Sigmoid).then_inc(evac[n % NS], 1)
                split_hi(4 * c // 2 + 4)
                build_diags(2)
                split_hi(4 * c // 2 + 5)
                copy_h(2 * c)
                copy_h(2 * c + 1)
                if c >= 2:
                    evacuated(act, SLOT["glu", 2 * c + 1])
                    act.activation(ci_hi[:, c - 2, :], conv_in[:, c, :], ACT.Copy).then_inc(ci_hi_ready, 1)

            def evac_conv(c):
                n = SLOT["conv", c]
                filled(act, n)
                act.activation(conv[:, c, :], slot_ap(n), ACT.Identity,
                               bias=vec[:, V_CB + c:V_CB + c + 1]).then_inc(evac[n % NS], 1)

            build_diags(sum(c == 2 for c, _ in PE_TAPS) - built[0])
            evac_conv(2)
            for g in range(PG):
                n = SLOT["p", g]
                filled(act, n)
                act.activation(pin[:, g, WMAX:], slot_ap(n), ACT.Copy).then_inc(evac[n % NS], 1)
                split_hi(2 * B_POOL + g + 4)
                build_diags(2)
            for g in range(PG):
                build_diags(4)
                act.wait_ge(pd_ready, g + 1)
                act.activation(a_hi[:, g, :], work[g], ACT.Copy).then_inc(pd_hi_ready, 1)

            def mix_hi(g):
                n = SLOT["mix", g]
                filled(act, n)
                act.activation(a_hi[:, PG + g, :], slot_ap(n), ACT.Copy,
                               scale=vec[:, V_PS + g:V_PS + g + 1]).then_inc(mix_hi_ready, 1)

            build_diags(len(PE_TAPS) - MIX_BEFORE + 4 - built[0])
            for g in range(2):
                mix_hi(g)
                build_diags(1)
            build_diags(len(PE_TAPS))
            evac_conv(3)
            mix_hi(2)
            mix_hi(3)
            for k in range(1, OUT_MEAN, 2):
                split_hi(2 * B_OUTC + k // 2)
            for c in range(CT):
                if c < CT - 1:
                    act.wait_ge(centred, c + 1)
                else:
                    evacuated(act, SLOT["mean",])
                act.activation(work[c], conv[:, c, :], ACT.Square).then_inc(ln_sq_ready, 1)
            for k in range(OUT_MEAN, OUT_VAR):
                if k % 2:
                    split_hi(2 * B_OUTC + k // 2)
            n = SLOT["var",]
            filled(act, n)
            act.activation(std[:, :], slot_ap(n), ACT.Sqrt, bias=eps[:, :]).then_inc(evac[n % NS], 1)
            for c in range(CT):
                act.wait_ge(normed, c + 1)
                act.activation(work[c], conv[:, c, :], ACT.Silu, bias=vec[:, V_LB + c:V_LB + c + 1],
                               scale=vec[:, V_LG + c:V_LG + c + 1]).then_inc(silu_ready, 1)
                if c == 0:
                    act.wait_ge(silu_ready, 1)
                    act.activation(a_hi[:, c, :], work[c], ACT.Copy).then_inc(c_hi_ready, 1)
            for k in range(OUT_VAR, KD):
                if k % 2:
                    split_hi(2 * B_OUTC + k // 2)
            for k in range(KD):
                prep(1, k, SLOT["outc", k], FULL)
                if k % 2:
                    split_hi(2 * B_F0 + k // 2)

            def ffn(layer, fb, tokens, it=0):
                a, b = tokens
                for i in range(units(layer, fb)):
                    n = SLOT["ffn", layer, fb, i]
                    w = 2 * (B_F1 if layer else B_F0) + 16 * fb + i + 4
                    if fb == 0 and i == 0:
                        stat(2 * layer + 1, tokens)
                    if i < KD:
                        t = KD * FBLK * layer + KD * fb + i
                        evacuated(act, n, it)
                        if t >= 2:
                            act.wait_ge(a_lo_ready, t - 1 + 8 * it)
                        act.activation(act2[:, i % 2, a:b], relu[:, i % 2, a:b], ACT.Square)\
                           .then_inc(sq_ready, 1)
                        act.wait_ge(sq_ready, t + 1 + 8 * it)
                        act.activation(a_hi[:, i, a:b], act2[:, i % 2, a:b], ACT.Copy)\
                           .then_inc(a_hi_ready, 1)
                    if w < 2 * NB:
                        split_hi(w, it)
                    if i >= KD and fb == FBLK - 1:
                        k = i - KD
                        if layer == 0:
                            prep(2, k, n, FULL)
                            continue
                        result(k, n, FRAMES, 4 * KD - KD + k)

            def result(k, n, tokens, t):
                a, b = tokens
                evacuated(act, n)
                act.wait_ge(sq_sum_ready, t - 1)
                act.activation(h_sq[:, k % 2, a:b], h[:, k, a:b], ACT.Square).then_inc(h_sq_ready, 1)
                if k >= 2:
                    filled(act, SLOT["y", k - 2])
                act.activation(relu[:, k % 2, a:b], h[:, k, a:b], ACT.Copy,
                               scale=vec[:, V_FIN + k:V_FIN + k + 1]).then_inc(hg_ready, 1)

            def ffn_all(layer, tokens):
                ffn(layer, 0, tokens)
                with act.Fori(0, FBLK - 2) as it:
                    ffn(layer, 1, tokens, it)
                ffn(layer, FBLK - 1, tokens)

            ffn_all(0, FULL)

            def evac_v(b):
                cols = slice(256 * b, 256 * (b + 1))
                for t in range(TT + 1):
                    n = SLOT["v", b, t]
                    filled(act, n)
                    if t < TT:
                        dst, src, r = v_tok[:, t, cols], ps[:, n % NS, 0:256], rstd_tok[:, t:t + 1]
                    else:
                        dst, src, r = v_meta[:, cols], ps[0:META, n % NS, 0:256], rstd_tok[0:META, TT:TT + 1]
                    act.activation(dst, src, ACT.Copy, scale=r).then_inc(evac[n % NS], 1)

            def split_v(b):
                for j in range(2):
                    split_hi(2 * (B_V + b) + 4 + j)

            n = SLOT["r",]
            filled(act, n)
            act.activation(r_raw, slot_ap(n, FULL, RANK), ACT.Copy).then_inc(evac[n % NS], 1)
            tstat()
            stat(2, FULL)
            act.wait_ge(rstd_tok_ready, TT + 2)
            evac_v(0)
            for hd in range(HEADS):
                n = SLOT["gate", hd]
                filled(act, n)
                act.activation(decay[:, hd, :], slot_ap(n), ACT.Abs,
                               bias=vec[:, V_GB + hd:V_GB + hd + 1]).then_inc(abs_ready, 1)
            split_v(0)
            act.wait_ge(abs_ready, HEADS)
            act.activation(decay[:, :, :], decay[:, :, :], ACT.Exp, scale=-1.0).then_inc(gexp_ready, 1)
            act.wait_ge(gexp_ready, 1)
            act.activation(decay[:, :, :], decay[:, :, :], ACT.Ln, bias=1.0).then_inc(softplus_ready, 1)
            evac_v(1)
            split_v(1)
            evac_v(2)
            split_v(2)
            for hd in range(HEADS):
                act.wait_ge(suffix_ready, hd + 1)
                act.activation(etot[:, hd, :], decay[:, hd, META - 1::CHUNK], ACT.Exp, scale=1.0 / GATE_NORM)
                act.activation(logd[:, hd, :], logd[:, hd, :], ACT.Exp, scale=1.0 / GATE_NORM)\
                   .then_inc(decay_ready, 1)
            evac_v(3)
            split_v(3)

            def evac_kt(hd):
                n = SLOT["kt", hd]
                filled(act, n)
                cols = slice(HK * hd, HK * (hd + 1))
                act.activation(k_tok[:, :, cols], ps[:, n % NS, 0:SEQ].rearrange("p (j d) -> p j d", d=HK),
                               ACT.Copy)
                act.activation(k_meta[:, cols], ps[0:META, n % NS, BANK:BANK + HK], ACT.Copy)\
                   .then_inc(evac[n % NS], 1)

            for hd in range(HEADS):
                split_hi(2 * B_K + hd + 4)
                if hd:
                    evac_kt(hd - 1)
            evac_kt(HEADS - 1)
            for hd in range(HEADS):
                split_hi(2 * B_Q + hd + 4)

            def evac_o(c):
                n = SLOT["o", c]
                filled(act, n)
                act.activation(o[:, :, CHUNK * (c - 1):CHUNK * c],
                               ps[:, n % NS, 0:KD * CHUNK].rearrange("p (k t) -> p k t", t=CHUNK),
                               ACT.Copy).then_inc(evac[n % NS], 1)

            def square_o(j):
                evacuated(act, SLOT["o", 2 * j + 2])
                evacuated(act, SLOT["o", 2 * j + 1])
                if j:
                    filled(act, SLOT["hn", j - 1])
                act.activation(o_sq, o[:, :, P * j:P * (j + 1)].rearrange("p (h m) t -> p m h t", m=HV // P),
                               ACT.Square).then_inc(o_sq_ready, 1)

            def head_std(j):
                n = SLOT["hn", j]
                filled(act, n)
                act.activation(std_head[:, :], ps[:, n % NS, 0:HEADS], ACT.Sqrt, bias=eps[:, :])\
                   .then_inc(evac[n % NS], 1)

            def silu_gate(i):
                evacuated(act, SLOT["g", i])
                act.activation(gate[:, i, :], gate[:, i, :], ACT.Silu).then_inc(gate_ready, 1)

            def round_o(n):
                k0, k1, a, b = GATE_PARTS[n]
                act.wait_ge(gated, n + 1)
                act.activation(gated_hi[:, k0:k1, a:b], gate[:, k0:k1, a:b], ACT.Copy).then_inc(o_hi_ready, 1)

            evac_o(1)
            for i in range(KD - 2):
                if i % 2:
                    head_std(i // 2)
                silu_gate(i)
                split_hi(2 * B_G + i + 4)
                evac_o(i + 2)
                if i % 2 == 0:
                    square_o(i // 2)
                for n in GATE_AT.get(i, ()):
                    round_o(n)
            evac_o(NCH - 1)
            square_o(TT - 1)
            for n in GATE_AT[KD - 2]:
                round_o(n)
            head_std(TT - 1)
            silu_gate(KD - 2)
            split_hi(2 * B_G + KD - 2 + 4)
            for n in GATE_AT[KD - 1]:
                round_o(n)
            silu_gate(KD - 1)
            round_o(len(GATE_PARTS) - 1)
            split_hi(2 * B_G + KD - 1 + 4)
            for k in range(KD):
                split_hi(2 * B_OUT1 + k + 4)
                prep(3, k, SLOT["out1", k], FRAMES)
            ffn_all(1, FRAMES)

            def std_half(i):
                n = SLOT["tstat", 4, i]
                filled(act, n)
                act.activation(std_tok[:, 2 * i:2 * i + 2], ps[:, n % NS, 0:2], ACT.Sqrt, bias=eps[:, :])\
                   .then_inc(evac[n % NS], 1)

            def scale_result(i):
                act.wait_ge(rstd_tok_ready, TT + 3 + i)
                for k in range(KD - 2):
                    evacuated(act, SLOT["y", k])
                evacuated(act, SLOT["y", KD - 2, i])
                evacuated(act, SLOT["y", KD - 1, i])
                act.activation(y_tok[:, 2 * i, :], y_tok[:, 2 * i, :], ACT.Copy,
                               scale=rstd_tok[:, 2 * i:2 * i + 1]).then_inc(act_out, 1)

            t = 3 * KD + KD - 2
            result(KD - 2, SLOT["end", 0, KD - 2], HALVES[0], t)
            result(KD - 1, SLOT["end", 0, KD - 1], HALVES[0], t + 1)
            result(KD - 2, SLOT["end", 1, KD - 2], HALVES[1], t + 2)
            std_half(0)
            scale_result(0)
            result(KD - 1, SLOT["end", 1, KD - 1], HALVES[1], t + 3)
            std_half(1)
            scale_result(1)

        @block.vector
        def _(dve):
            V = nc.vector
            steps = [0]

            def step(ins):
                ins.then_inc(dve_step, 1)
                steps[0] += 1
                dve.wait_ge(dve_step, steps[0])

            def rest_of_u(norm, k, tokens):
                a, b = tokens
                g = (V_MIX, V_FFN, V_MIX + KD, V_FFN + KD)[norm] + k
                dve.wait_ge(u_hi_ready, KD * norm + k + 1)
                V.scalar_tensor_tensor(out=u_lo[:, k, a:b], in0=h[:, k, a:b], scalar=vec[:, g:g + 1],
                                       in1=u_hi[:, k, a:b].bitcast(F32), op0=ALU.mult,
                                       op1=ALU.subtract).then_inc(u_lo_ready, 1)

            def add_squares(norm, k, tokens, extra=0):
                a, b = tokens
                t = KD * (norm - 1) + k + 1 + extra
                dve.wait_ge(h_sq_ready, t)
                if k == 0:
                    V.tensor_copy(sq_sum[:, a:b], h_sq[:, 0, a:b]).then_inc(sq_sum_ready, 1)
                else:
                    dve.wait_ge(sq_sum_ready, t - 1)
                    V.tensor_tensor(sq_sum[:, a:b], sq_sum[:, a:b], h_sq[:, k % 2, a:b], ALU.add)\
                     .then_inc(sq_sum_ready, 1)

            def prep(norm, k, tokens):
                if norm < 4:
                    rest_of_u(norm, k, tokens)
                add_squares(norm, k, tokens)

            uses = [0]

            def recip(n, tokens):
                evacuated(dve, n)
                V.reciprocal(rstd[:, tokens[0]:tokens[1]], std[:, tokens[0]:tokens[1]])\
                 .then_inc(rstd_ready, 1)
                uses[0] += 1
                dve.wait_ge(rstd_ready, uses[0])

            def scale_out(dst, n, tokens):
                filled(dve, n)
                V.tensor_tensor(dst, slot_ap(n, tokens), rstd[:, tokens[0]:tokens[1]], ALU.mult)\
                 .then_inc(evac[n % NS], 1)

            def add_to_h(k, n, tokens, it=0):
                a, b = tokens
                filled(dve, n, it)
                V.tensor_tensor(h[:, k, a:b], h[:, k, a:b], slot_ap(n, tokens), ALU.add)\
                 .then_inc(evac[n % NS], 1)

            dve.wait_ge(consts, N_CONST)
            V.memset(pin[:, :, 0:WMAX], 0.0).then_inc(pin_zeroed, 1)
            for i in range(TT + 1):
                rows, t = (META, TT) if i == 0 else (P, i - 1)
                dve.wait_ge(x_std, i + 1)
                V.reciprocal(rstd_tok[0:rows, t:t + 1], std_tok[0:rows, t:t + 1]).then_inc(rstd_tok_ready, 1)
                dve.wait_ge(rstd_tok_ready, i + 1)
                src, dst = (xmeta[:, :], meta_normed) if i == 0 else (xin[:, t, :], x_normed[:, t, :])
                V.tensor_scalar(dst, src, rstd_tok[0:rows, t:t + 1], None, ALU.mult).then_inc(x_normed_ready, 1)
                if i == 1:
                    n = SLOT["xm",]
                    evacuated(dve, SLOT["gain",])
                    filled(dve, n)
                    V.tensor_tensor(u_meta, ps[:, n % NS, 0:KD * META].rearrange("p (k t) -> p k t", t=META),
                                    vec[:, V_MIX:V_MIX + KD, None].to_broadcast([P, KD, META]), ALU.mult)\
                     .then_inc(evac[n % NS], 1)
            evacuated(dve, SLOT["xm",])
            dve.wait_ge(u_meta_hi_ready, 1)
            V.tensor_tensor(u_lo[:, :, 0:META], u_meta, u_hi[:, :, 0:META].bitcast(F32), ALU.subtract)\
             .then_inc(u_meta_lo_ready, 1)
            split_lo(0)
            for k in range(KD):
                n = SLOT["x", k // 2]
                dve.wait_ge(u_hi_ready, k + 1)
                ins = V.scalar_tensor_tensor(out=u_lo[:, k, META:],
                                             in0=ps[:, n % NS, BANK * (k % 2):BANK * (k % 2) + SEQ],
                                             scalar=vec[:, V_MIX + k:V_MIX + k + 1],
                                             in1=u_hi[:, k, META:].bitcast(F32), op0=ALU.mult,
                                             op1=ALU.subtract)
                if k % 2:
                    ins.then_inc(evac[n % NS], 1)
            split_lo(1)
            split_lo(2)
            evacuated(dve, SLOT["vec",])
            dve.wait_ge(small_hi, 3)
            V.tensor_tensor(cw_lo[:, :], cw[:, :], cw_hi[:, :].bitcast(F32), ALU.subtract)\
             .then_inc(small_lo, 1)
            V.tensor_tensor(pw_lo[:, :, :], pw[:, :, :], pw_hi[:, :, :].bitcast(F32), ALU.subtract)\
             .then_inc(small_lo, 1)
            V.tensor_tensor(rw_lo[:, 0:KD * RANK], rw[:, :], rw_hi[:, 0:KD * RANK].bitcast(F32),
                            ALU.subtract).then_inc(small_lo, 1)
            split_lo(3)

            taps = {c: [t for t in range(TAPS) if (c, t) not in PE_TAPS] for c in range(CT)}
            last_tile = [0]

            def run_taps(count, tiles):
                while count and any(taps[c] for c in tiles):
                    live = [c for c in tiles if taps[c]][:2]
                    c = live[-1] if last_tile[0] == live[0] else live[0]
                    last_tile[0] = c
                    t = taps[c].pop(0)
                    count -= 1
                    src, wt = conv_in[:, c, t:t + TOK], cw[:, t * CT + c:t * CT + c + 1]
                    done = sum((c, i) not in PE_TAPS for i in range(t))
                    if t == 0:
                        evacuated(dve, SLOT["glu", 2 * c + 1])
                        V.tensor_scalar(conv[:, c, :], src, wt, vec[:, V_CB + c:V_CB + c + 1],
                                        ALU.mult, ALU.add).then_inc(tap_done[c], 1)
                        continue
                    if done:
                        dve.wait_ge(tap_done[c], done)
                    else:
                        evacuated(dve, SLOT["glu", 2 * c + 1])
                        evacuated(dve, SLOT["conv", c])
                    V.scalar_tensor_tensor(out=conv[:, c, :], in0=src, scalar=wt, in1=conv[:, c, :],
                                           op0=ALU.mult, op1=ALU.add).then_inc(tap_done[c], 1)

            for c in range(CT):
                n = SLOT["glu", 2 * c + 1]
                evacuated(dve, SLOT["glu", 2 * c])
                split_lo(2 * c + 4)
                run_taps(5, (0, 1)[:c])
                filled(dve, n)
                V.tensor_tensor(conv_in[:, c, TAPS - 1:], slot_ap(n), act2[:, c % 2, :], ALU.mult)\
                 .then_inc(evac[n % NS], 1)
                split_lo(2 * c + 5)
                if c >= 2:
                    dve.wait_ge(ci_hi_ready, c - 1)
                    V.tensor_tensor(ci_lo[:, c - 2, :], conv_in[:, c, :], ci_hi[:, c - 2, :].bitcast(F32),
                                    ALU.subtract).then_inc(ci_lo_ready, 1)
                run_taps(6, (0, 1)[:c + 1])
            run_taps(CONV_STEP, (0, 1))
            dve.wait_ge(pin_zeroed, 1)
            for g in range(PG):
                n = SLOT["p", g]
                run_taps(POOL_STEP, (0, 1))
                split_lo(2 * B_POOL + g + 4)
                evacuated(dve, n)
                src = p_in = pin[:, g, :]
                for j in range(g + 1):
                    back = 1 << j
                    V.tensor_tensor(win[:, j % 2, WMAX:], src[:, WMAX:], src[:, WMAX - back:-back],
                                    ALU.add).then_inc(dve_step, 1)
                    steps[0] += 1
                    run_taps(1, (0, 1))
                    dve.wait_ge(dve_step, steps[0])
                    src = win[:, j % 2, :]
                short, pd = (2 << g) - 1, work[g]
                V.scalar_tensor_tensor(out=pd[:, short:], in0=src[:, WMAX + short:], scalar=1.0 / (short + 1),
                                       in1=p_in[:, WMAX + short:], op0=ALU.mult, op1=ALU.subtract)
                step(V.tensor_tensor(pd[:, 0:short], src[:, WMAX:WMAX + short], rcount[:, 0:short], ALU.mult))
                V.tensor_tensor(pd[:, 0:short], pd[:, 0:short], p_in[:, WMAX:WMAX + short], ALU.subtract)\
                 .then_inc(pd_ready, 1)
            for g in range(PG):
                run_taps(PD_STEP, (0, 1, 2))
                dve.wait_ge(pd_hi_ready, g + 1)
                V.tensor_tensor(a_lo[:, g, :], work[g], a_hi[:, g, :].bitcast(F32), ALU.subtract)\
                 .then_inc(pd_lo_ready, 1)
            for g in range(PG):
                n = SLOT["mix", g]
                if g == 0:
                    run_taps(2 * TAPS, (0, 1))
                    dve.wait_ge(tap_done[0], TAPS)
                    dve.wait_ge(tap_done[1], TAPS)
                    V.tensor_tensor(conv_sum, conv[:, 0, :], conv[:, 1, :], ALU.add).then_inc(conv_summed, 1)
                run_taps(MIX_STEP[g], (0, 1, 2))
                dve.wait_ge(mix_hi_ready, g + 1)
                V.scalar_tensor_tensor(out=a_lo[:, PG + g, :], in0=slot_ap(n),
                                       scalar=vec[:, V_PS + g:V_PS + g + 1],
                                       in1=a_hi[:, PG + g, :].bitcast(F32), op0=ALU.mult,
                                       op1=ALU.subtract).then_inc(evac[n % NS], 1)

            dve.wait_ge(conv_summed, 1)
            evacuated(dve, SLOT["conv", 3])
            V.tensor_tensor(conv_sum, conv_sum, conv[:, 3, :], ALU.add).then_inc(conv_summed, 1)

            def out_pool(k):
                add_to_h(k, SLOT["outp", k], FULL)
                if k % 2:
                    split_lo(2 * B_OUTC + k // 2)

            for k in range(OUT_MEAN):
                out_pool(k)
                run_taps(OUT_STEP, (0, 1, 2))
            run_taps(len(PE_TAPS) + 2 * TAPS, (0, 1, 2))
            n = SLOT["mean",]
            filled(dve, n)
            for c in range(CT):
                V.tensor_tensor(conv[:, c, :], conv[:, c, :], slot_ap(n), ALU.subtract)\
                 .then_inc(centred if c < CT - 1 else evac[n % NS], 1)
            dve.wait_ge(ln_sq_ready, 2)
            V.tensor_tensor(centred_sq_sum, work[0], work[1], ALU.add).then_inc(ln_sq_summed, 1)
            for c in range(2, CT):
                dve.wait_ge(ln_sq_ready, c + 1)
                dve.wait_ge(ln_sq_summed, c - 1)
                V.tensor_tensor(centred_sq_sum, centred_sq_sum, work[c], ALU.add).then_inc(ln_sq_summed, 1)
            for k in range(OUT_MEAN, OUT_VAR):
                out_pool(k)
            recip(SLOT["var",], FULL)
            for c in range(CT):
                V.tensor_tensor(conv[:, c, :], conv[:, c, :], rstd[:, :], ALU.mult).then_inc(normed, 1)
            for c in range(CT):
                if c:
                    dve.wait_ge(silu_ready, c + 1)
                    V.tensor_copy(a_hi[:, c, :], work[c]).then_inc(c_hi_ready, 1)
                dve.wait_ge(c_hi_ready, c + 1)
                V.tensor_tensor(a_lo[:, c, :], work[c], a_hi[:, c, :].bitcast(F32), ALU.subtract)\
                 .then_inc(c_lo_ready, 1)
            for k in range(OUT_VAR, KD):
                out_pool(k)
            for k in range(KD):
                add_to_h(k, SLOT["outc", k], FULL)
                if k:
                    rest_of_u(1, k - 1, FULL)
                if k == KD - 1:
                    rest_of_u(1, k, FULL)
                if k:
                    add_squares(1, k - 1, FULL)
                if k and k % 2 == 0:
                    split_lo(2 * B_F0 + k // 2 - 1)
            add_squares(1, KD - 1, FULL)
            split_lo(2 * B_F0 + KD // 2 - 1)

            def ffn(layer, fb, tokens, it=0):
                a, b = tokens
                for i in range(units(layer, fb)):
                    n = SLOT["ffn", layer, fb, i]
                    w = 2 * (B_F1 if layer else B_F0) + 16 * fb + i + 4
                    if fb == 0 and i == 0:
                        recip(SLOT["stat", 2 * layer + 1], tokens)
                    if i < KD:
                        t = KD * FBLK * layer + KD * fb + i
                        filled(dve, n, it)
                        if t >= 2:
                            dve.wait_ge(sq_ready, t - 1 + 8 * it)
                        V.scalar_tensor_tensor(out=relu[:, i % 2, a:b], in0=slot_ap(n, tokens), scalar=0.0,
                                               in1=rstd[:, a:b], op0=ALU.max, op1=ALU.mult)\
                         .then_inc(evac[n % NS], 1)
                        dve.wait_ge(a_hi_ready, t + 1 + 8 * it)
                        V.tensor_tensor(a_lo[:, i, a:b], act2[:, i % 2, a:b], a_hi[:, i, a:b].bitcast(F32),
                                        ALU.subtract).then_inc(a_lo_ready, 1)
                    else:
                        add_to_h(i - KD, n, tokens, it)
                    if w < 2 * NB:
                        split_lo(w, it)
                    if i >= KD and fb == FBLK - 1:
                        k = i - KD
                        prep(2 if layer == 0 else 4, k, tokens)
                        if layer and k:
                            copy_y(k - 1)

            def ffn_all(layer, tokens):
                ffn(layer, 0, tokens)
                with dve.Fori(0, FBLK - 2) as it:
                    ffn(layer, 1, tokens, it)
                ffn(layer, FBLK - 1, tokens)

            def copy_y(k):
                n = SLOT["y", k]
                filled(dve, n)
                V.tensor_copy(y_tok[:, :, P * k:P * (k + 1)],
                              ps[:, n % NS, 0:SEQ].rearrange("p (j d) -> p j d", d=P)).then_inc(evac[n % NS], 1)

            ffn_all(0, FULL)
            evacuated(dve, SLOT["tstat", 2])
            V.reciprocal(rstd_tok[:, 0:TT], std_tok[:, 0:TT])
            V.reciprocal(rstd_tok[0:META, TT:TT + 1], std_tok[0:META, TT:TT + 1]).then_inc(rstd_tok_ready, 1)
            recip(SLOT["stat", 2], FULL)
            evacuated(dve, SLOT["r",])
            V.tensor_tensor(r_sb, r_raw, rstd[0:RANK, :], ALU.mult).then_inc(r_ready, 1)
            step(V.memset(mask, 1.0))
            V.memset(mask[:, META::CHUNK], 0.0).then_inc(dve_step, 1)
            steps[0] += 1

            def split_v(b):
                for j in range(2):
                    split_lo(2 * (B_V + b) + 4 + j)

            for hd in range(HEADS):
                n = SLOT["gate", hd]
                dve.wait_ge(abs_ready, hd + 1)
                V.tensor_scalar(logd[:, hd, :], slot_ap(n), vec[:, V_GB + hd:V_GB + hd + 1], 0.0,
                                ALU.add, ALU.min).then_inc(evac[n % NS], 1)
            split_v(0)
            split_v(1)
            dve.wait_ge(softplus_ready, 1)
            dve.wait_ge(dve_step, steps[0])
            for hd in range(HEADS):
                evacuated(dve, SLOT["gate", hd])
                ld, cum = logd[:, hd, :], decay[:, hd, :]
                step(V.tensor_tensor(ld, ld, cum, ALU.subtract))
                step(V.tensor_tensor_scan(cum, mask, ld, 0.0, ALU.mult, ALU.add))
                V.tensor_tensor(ld[:, 0:META], cum[:, META - 1:META].to_broadcast([P, META]),
                                cum[:, 0:META], ALU.subtract)
                cf = cum[:, META:].rearrange("p (c t) -> p c t", t=CHUNK)
                V.tensor_tensor(ld[:, META:].rearrange("p (c t) -> p c t", t=CHUNK),
                                cf[:, :, CHUNK - 1:CHUNK].to_broadcast([P, NCH - 1, CHUNK]), cf,
                                ALU.subtract).then_inc(suffix_ready, 1)
            split_v(2)
            for hd in range(HEADS):
                dve.wait_ge(decay_ready, hd + 1)
                V.tensor_tensor(decay[:, hd, :], logd[:, hd, :], rstd[:, :], ALU.mult).then_inc(kscale_ready, 1)
            split_v(3)
            dve.wait_ge(kscale_ready, HEADS)
            for hd in range(HEADS):
                n = SLOT["k", hd]
                filled(dve, n)
                if hd >= 2:
                    filled(dve, SLOT["kt", hd - 2])
                V.tensor_tensor(relu[:, hd % 2, :], slot_ap(n), decay[:, hd, :], ALU.mult)\
                 .then_inc(evac[n % NS], 1)
                split_lo(2 * B_K + hd + 4)

            def update_state(c):
                n = SLOT["kv", c]
                filled(dve, n)
                kv = ps[:, n % NS, :].rearrange("p (h v) -> p h v", h=HEADS)
                if c == 0:
                    V.tensor_copy(state[:, 0, :, :], kv).then_inc(evac[n % NS], 1)
                    return
                evacuated(dve, SLOT["kv", c - 1])
                for hd in range(HEADS):
                    last = V.scalar_tensor_tensor(out=state[:, c % 2, hd, :], in0=state[:, (c - 1) % 2, hd, :],
                                                  scalar=etot[:, hd, c:c + 1], in1=kv[:, hd, :],
                                                  op0=ALU.mult, op1=ALU.add)
                last.then_inc(evac[n % NS], 1)

            for hd in range(HEADS):
                n = SLOT["q", hd]
                filled(dve, n)
                V.scalar_tensor_tensor(out=q[:, hd, :], in0=slot_ap(n, FRAMES), scalar=HK ** -0.5,
                                       in1=rstd[:, META:], op0=ALU.mult, op1=ALU.mult)\
                 .then_inc(evac[n % NS], 1)
                split_lo(2 * B_Q + hd + 4)
                if hd:
                    update_state(hd - 1)

            def sum_squares(j):
                dve.wait_ge(o_sq_ready, j + 1)
                V.tensor_tensor(o_sq[:, 0, :, :], o_sq[:, 0, :, :], o_sq[:, 1, :, :], ALU.add)\
                 .then_inc(o_sq_summed, 1)

            def head_factors(j):
                evacuated(dve, SLOT["hn", j])
                step(V.reciprocal(rstd_head[:, :], std_head[:, :]))
                if j:
                    filled(dve, SLOT["hb", j - 1])
                V.tensor_tensor(head_diag, ident[:, None, :].to_broadcast([P, HEADS, P]),
                                rstd_head[:, :, None].to_broadcast([P, HEADS, P]), ALU.mult)\
                 .then_inc(diag_set, 1)

            def head_norm(j):
                n = SLOT["hb", j]
                filled(dve, n)
                r = ps[:, n % NS, 0:SEQ].rearrange("p (h t) -> p h t", h=HEADS)
                evacuated(dve, SLOT["o", 2 * j + 2])
                for m in range(HV // P):
                    part = o[:, m::HV // P, P * j:P * (j + 1)]
                    last = V.scalar_tensor_tensor(out=part, in0=part, scalar=vec[:, V_HG + m:V_HG + m + 1],
                                                  in1=r, op0=ALU.mult, op1=ALU.mult)
                last.then_inc(evac[n % NS], 1)

            def gate_o(n):
                k0, k1, a, b = GATE_PARTS[n]
                dve.wait_ge(gate_ready, k1)
                evacuated(dve, SLOT["hb", (b - 1) // P])
                V.tensor_tensor(gate[:, k0:k1, a:b], gate[:, k0:k1, a:b], o[:, k0:k1, a:b], ALU.mult)\
                 .then_inc(gated, 1)

            def rest_of_o(n):
                k0, k1, a, b = GATE_PARTS[n]
                dve.wait_ge(o_hi_ready, n + 1)
                V.tensor_tensor(gated_lo[:, k0:k1, a:b], gate[:, k0:k1, a:b],
                                gated_hi[:, k0:k1, a:b].bitcast(F32), ALU.subtract).then_inc(o_lo_ready, 1)

            for i in range(KD - 2):
                for n in GATE_AT.get(i, ()):
                    gate_o(n)
                if i % 2:
                    head_factors(i // 2)
                scale_out(gate[:, i, :], SLOT["g", i], FRAMES)
                split_lo(2 * B_G + i + 4)
                update_state(i + 3)
                if i % 2:
                    head_norm(i // 2)
                else:
                    sum_squares(i // 2)
                for n in GATE_AT.get(i, ()):
                    rest_of_o(n)
            for n in GATE_AT[KD - 2]:
                gate_o(n)
            sum_squares(TT - 1)
            scale_out(gate[:, KD - 2, :], SLOT["g", KD - 2], FRAMES)
            head_factors(TT - 1)
            rest_of_o(3)
            gate_o(5)
            head_norm(TT - 1)
            gate_o(6)
            gate_o(7)
            rest_of_o(4)
            rest_of_o(5)
            rest_of_o(6)
            scale_out(gate[:, KD - 1, :], SLOT["g", KD - 1], FRAMES)
            rest_of_o(7)
            gate_o(8)
            rest_of_o(8)
            split_lo(2 * B_G + KD - 2 + 4)
            split_lo(2 * B_G + KD - 1 + 4)
            for k in range(KD):
                add_to_h(k, SLOT["out1", k], FRAMES)
                split_lo(2 * B_OUT1 + k + 4)
                prep(3, k, FRAMES)
            ffn_all(1, FRAMES)

            def end(i, k):
                add_to_h(k, SLOT["end", i, k], HALVES[i])
                add_squares(4, k, HALVES[i], 2 * i)

            def copy_half(k, i):
                n = SLOT["y", k, i]
                filled(dve, n)
                V.tensor_copy(y_tok[:, 2 * i:2 * i + 2, P * k:P * (k + 1)],
                              ps[:, n % NS, 0:SEQ // 2].rearrange("p (j d) -> p j d", d=P))\
                 .then_inc(evac[n % NS], 1)

            def recip_half(i):
                evacuated(dve, SLOT["tstat", 4, i])
                V.reciprocal(rstd_tok[:, 2 * i:2 * i + 2], std_tok[:, 2 * i:2 * i + 2])\
                 .then_inc(rstd_tok_ready, 1)

            def scale_result(i):
                t = 2 * i + 1
                dve.wait_ge(rstd_tok_ready, TT + 3 + i)
                for k in range(KD - 2):
                    evacuated(dve, SLOT["y", k])
                evacuated(dve, SLOT["y", KD - 2, i])
                evacuated(dve, SLOT["y", KD - 1, i])
                V.tensor_scalar(y_tok[:, t, :], y_tok[:, t, :], rstd_tok[:, t:t + 1], None, ALU.mult)\
                 .then_inc(dve_out, 1)

            end(0, KD - 2)
            copy_y(KD - 3)
            end(0, KD - 1)
            copy_half(KD - 2, 0)
            end(1, KD - 2)
            recip_half(0)
            copy_half(KD - 1, 0)
            scale_result(0)
            end(1, KD - 1)
            copy_half(KD - 2, 1)
            recip_half(1)
            copy_half(KD - 1, 1)
            scale_result(1)

        @block.tensor
        def _(pe):
            mm = nc.tensor.matmul

            def start_slot(n, it=0):
                if n >= NS:
                    evacuated(pe, n - NS, it)

            def parts(tokens):
                if tokens == FULL:
                    return ((C0, 0, SPLIT), (BANK, SPLIT, TOK))
                return ((0, *tokens),)

            def exact(n, lhs, rhs, count, tokens, before=None, it=0, middle=None, at=KD // 2, origin=0):
                start_slot(n, it)
                for k in range(count):
                    if middle and k == at:
                        middle()
                    if before:
                        before(k)
                    (l_hi, l_lo), (r_hi, r_lo) = lhs(k), rhs(k)
                    for i, (l, r) in enumerate(((l_hi, r_lo), (l_hi, r_hi), (l_lo, r_hi))):
                        for c, a, b in parts(tokens):
                            last = mm(ps[:, n % NS, c:c + b - a], l, r[:, a - origin:b - origin],
                                      start=(k == 0 and i == 0), stop=(k == count - 1 and i == 2))
                last.then_inc(filled_n, 1)

            def plain(n, pairs, tokens):
                for i, (l, r) in enumerate(pairs):
                    for c, a, b in parts(tokens):
                        last = mm(ps[:, n % NS, c:c + b - a], l, r[:, a:b], start=(i == 0),
                                  stop=(i == len(pairs) - 1))
                last.then_inc(filled_n, 1)

            def whalf(w):
                hi, lo = half_view(w_hi, w), half_view(w_lo, w)
                return lambda k: (hi[:, k, 0:P], lo[:, k, 0:P])

            def u(k):
                return u_hi[:, k, :], u_lo[:, k, :]

            def acts(k):
                return a_hi[:, k, :], a_lo[:, k, :]

            def u_wait(norm):
                return lambda k: pe.wait_ge(u_lo_ready, KD * (norm - 1) + k + 1)

            def project(n, w, tokens, before=None, middle=None, at=KD // 2):
                pe.wait_ge(w_lo_ready, w + 1)
                exact(n, whalf(w), u, KD, tokens, before, middle=middle, at=at)

            def stat(norm, tokens):
                n = SLOT["stat", norm]
                start_slot(n)
                pe.wait_ge(sq_sum_ready, KD * norm)
                plain(n, [(ones_d[:, :], sq_sum)], tokens)

            def tstat():
                n = SLOT["tstat", 2]
                start_slot(n)
                pe.wait_ge(sq_sum_ready, KD * 2)
                for t in range(TT):
                    mm(ps[:, n % NS, t:t + 1], sq_sum[:, META + P * t:META + P * (t + 1)],
                       ones_d[:, 0:1], start=True, stop=True)
                mm(ps[0:META, n % NS, TT:TT + 1], sq_sum[:, 0:META], ones_d[:, 0:1],
                   start=True, stop=True).then_inc(filled_n, 1)

            def flip(dst, src, rows=P):
                return nc.tensor.transpose(dst, src, ident[0:rows, 0:rows])

            pe.wait_ge(consts, N_CONST)
            pe.wait_ge(gain_loaded, 16)
            n = SLOT["gain",]
            flip(ps[:, n % NS, 0:2 * KD], gain_rows[:, :], 2 * KD).then_inc(filled_n, 1)
            pe.wait_ge(x_normed_ready, 1)
            n = SLOT["xm",]
            for k in range(KD):
                last = flip(ps[:, n % NS, META * k:META * (k + 1)], meta_normed[:, P * k:P * (k + 1)], META)
            last.then_inc(filled_n, 1)
            for j in range(TT):
                pe.wait_ge(x_normed_ready, j + 2)
                for k in range(KD):
                    n = SLOT["x", k // 2]
                    if j == 0 and k % 2 == 0:
                        start_slot(n)
                    c = BANK * (k % 2) + P * j
                    last = flip(ps[:, n % NS, c:c + P], x_normed[:, j, P * k:P * (k + 1)])
                    if j == TT - 1 and k % 2:
                        last.then_inc(filled_n, 1)

            def flip_x(n, k):
                start_slot(n)
                flip(ps[:, n % NS, C0:C0 + META], xmeta[:, P * k:P * (k + 1)], META)
                for j in range(TT):
                    c = C0 + META + P * j
                    last = flip(ps[:, n % NS, c:c + P], xin[:, j, P * k:P * (k + 1)])
                last.then_inc(filled_n, 1)

            def input_wait(k):
                if k == 0:
                    pe.wait_ge(u_meta_lo_ready, 1)
                evacuated(pe, SLOT["x", k // 2])

            for c in range(CT):
                project(SLOT["glu", 2 * c], 2 * B_GLU + 2 * c, FULL,
                        input_wait if c == 0 else None)
                if c == 0:
                    n = SLOT["vec",]
                    start_slot(n)
                    pe.wait_ge(vec_loaded, 144)
                    flip(ps[:, n % NS, 0:NV - 2 * KD], vec_rows[:, :], NV - 2 * KD)
                    flip(ps[:, n % NS, BANK:BANK + TAPS * CT], cw_rows[:, :], TAPS * CT)\
                        .then_inc(filled_n, 1)
                project(SLOT["glu", 2 * c + 1], 2 * B_GLU + 2 * c + 1, FULL)
                flip_x(SLOT["h", 2 * c], 2 * c)
                flip_x(SLOT["h", 2 * c + 1], 2 * c + 1)

            def conv_taps(c):
                n = SLOT["conv", c]
                start_slot(n)
                pe.wait_ge(ci_lo_ready, c - 1)
                mine = [i for i, (tile, _) in enumerate(PE_TAPS) if tile == c]
                for i in mine:
                    if i == len(PE_TAPS) - MIX_BEFORE:
                        mix(0)
                        mix(1)
                    t = PE_TAPS[i][1]
                    pe.wait_ge(diag_ready, i + 1)
                    d_hi, d_lo = diag_hi[:, i % DIAGS, :], diag_lo[:, i % DIAGS, :]
                    x_hi, x_lo = ci_hi[:, c - 2, t:t + TOK], ci_lo[:, c - 2, t:t + TOK]
                    for m, (l, r) in enumerate(((d_hi, x_lo), (d_hi, x_hi), (d_lo, x_hi))):
                        for col, a, b in parts(FULL):
                            last = mm(ps[:, n % NS, col:col + b - a], l, r[:, a:b],
                                      start=(i == mine[0] and m == 0), stop=(i == mine[-1] and m == 2))
                    last.then_inc(filled_n if i == mine[-1] else diag_used, 1)

            def mix(g):
                if g == 0:
                    pe.wait_ge(small_lo, 2)
                exact(SLOT["mix", g], lambda k: (pw_hi[:, g, :], pw_lo[:, g, :]),
                      lambda k: (a_hi[:, g, :], a_lo[:, g, :]), 1, FULL,
                      lambda k: pe.wait_ge(pd_lo_ready, g + 1))

            conv_taps(2)
            for g in range(PG):
                project(SLOT["p", g], 2 * B_POOL + g, FULL)
            conv_taps(3)
            mix(2)
            mix(3)

            def project_out0(stage, b, k, first, before):
                w = 2 * b + k // 2
                pe.wait_ge(w_lo_ready, w + 1)
                hi, lo = half_view(w_hi, w), half_view(w_lo, w)
                cols = slice(P * (k % 2), P * (k % 2 + 1))
                exact(SLOT[stage, k], lambda j: (hi[:, j, cols], lo[:, j, cols]),
                      lambda j: (a_hi[:, first + j, :], a_lo[:, first + j, :]), KD // 2, FULL,
                      before if k == 0 else None)

            for k in range(KD):
                if k == OUT_MEAN:
                    n = SLOT["mean",]
                    start_slot(n)
                    pe.wait_ge(conv_summed, 2)
                    evacuated(pe, SLOT["conv", 2])
                    pe.wait_ge(tap_done[2], sum((2, t) not in PE_TAPS for t in range(TAPS)))
                    plain(n, [(ones_c[:, :], conv_sum), (ones_c[:, :], conv[:, 2, :])], FULL)
                if k == OUT_VAR:
                    n = SLOT["var",]
                    start_slot(n)
                    pe.wait_ge(ln_sq_summed, CT - 1)
                    plain(n, [(ones_c[:, :], centred_sq_sum)], FULL)
                project_out0("outp", B_OUTP, k, PG, lambda j: evacuated(pe, SLOT["mix", j]))
            for k in range(KD):
                project_out0("outc", B_OUTC, k, 0, lambda j: pe.wait_ge(c_lo_ready, j + 1))

            def ffn(layer, fb, tokens, it=0):
                for i in range(units(layer, fb)):
                    n = SLOT["ffn", layer, fb, i]
                    w = 2 * (B_F1 if layer else B_F0) + 16 * fb + i
                    t = KD * FBLK * layer + KD * fb
                    pe.wait_ge(w_lo_ready, w + 1 + 16 * it)
                    if i < KD:
                        exact(n, whalf(w), u, KD, tokens, u_wait(2 * layer + 1) if fb == i == 0 else None, it)
                    else:
                        exact(n, whalf(w), acts, KD, tokens,
                              (lambda k: pe.wait_ge(a_lo_ready, t + k + 1 + 8 * it)) if i == KD else None, it)
                    if fb == 0 and i == 0:
                        stat(2 * layer + 1, tokens)
                    if layer == 1 and fb == FBLK - 1 and i > KD:
                        flip_y(i - KD - 1)

            def ffn_all(layer, tokens):
                ffn(layer, 0, tokens)
                with pe.Fori(0, FBLK - 2) as it:
                    ffn(layer, 1, tokens, it)
                ffn(layer, FBLK - 1, tokens)

            def flip_y(k):
                n = SLOT["y", k]
                start_slot(n)
                pe.wait_ge(hg_ready, k + 1)
                for j in range(TT):
                    last = flip(ps[:, n % NS, P * j:P * (j + 1)], relu[:, k % 2, META + P * j:META + P * (j + 1)])
                last.then_inc(filled_n, 1)

            ffn_all(0, FULL)
            pe.wait_ge(small_lo, 3)
            exact(SLOT["r",], lambda k: (rw_hi[:, RANK * k:RANK * k + P], rw_lo[:, RANK * k:RANK * k + P]),
                  u, KD, FULL, u_wait(2))
            tstat()
            stat(2, FULL)

            def project_v(b):
                pe.wait_ge(w_lo_ready, 2 * (B_V + b) + 2)
                whole = [t[:, (B_V + b) % 2, :].rearrange("p (k n) -> p k n", k=KD) for t in (w_hi, w_lo)]
                for t in range(TT + 1):
                    n = SLOT["v", b, t]
                    a = META + P * t if t < TT else 0
                    start_slot(n)
                    for k in range(KD):
                        hi, lo = u_hi[:, k, a:a + P], u_lo[:, k, a:a + P]
                        for i, (l, r) in enumerate(((hi, whole[1]), (hi, whole[0]), (lo, whole[0]))):
                            last = mm(ps[:, n % NS, 0:256], l, r[:, k, :], start=(k == 0 and i == 0),
                                      stop=(k == KD - 1 and i == 2))
                    last.then_inc(filled_n, 1)

            project_v(0)
            pe.wait_ge(r_ready, 1)
            pe.wait_ge(small_loaded, 48)
            for hd in range(HEADS):
                start_slot(SLOT["gate", hd])
                plain(SLOT["gate", hd], [(gw2[:, HK * hd:HK * (hd + 1)], r_sb)], FULL)
            for b in range(1, 4):
                project_v(b)

            def flip_k(hd):
                n = SLOT["kt", hd]
                start_slot(n)
                evacuated(pe, SLOT["k", hd])
                kd = relu[:, hd % 2, :]
                for j in range(TT):
                    flip(ps[:, n % NS, P * j:P * (j + 1)], kd[:, META + P * j:META + P * (j + 1)])
                flip(ps[:, n % NS, BANK:BANK + P], kd[:, 0:P]).then_inc(filled_n, 1)

            def project_k(hd):
                project(SLOT["k", hd], 2 * B_K + hd, FULL)

            def project_q(hd):
                project(SLOT["q", hd], 2 * B_Q + hd, FRAMES)

            def chunk_kv(c):
                n = SLOT["kv", c]
                start_slot(n)
                if c == 0:
                    for hd in range(HEADS):
                        evacuated(pe, SLOT["kt", hd])
                    for t in range(TT + 1):
                        evacuated(pe, SLOT["v", 3, t])
                    kc, vc = k_meta[:, :], v_meta[:, :]
                else:
                    j, r = (c - 1) // 2, CHUNK * ((c - 1) % 2)
                    kc, vc = k_tok[r:r + CHUNK, j, :], v_tok[r:r + CHUNK, j, :]
                for hd in range(HEADS):
                    last = mm(ps[:, n % NS, HV * hd:HV * (hd + 1)], kc[:, HK * hd:HK * (hd + 1)],
                              vc[:, HV * hd:HV * (hd + 1)], start=True, stop=True)
                last.then_inc(filled_n, 1)

            def chunk_o(c):
                n = SLOT["o", c]
                start_slot(n)
                evacuated(pe, SLOT["kv", c])
                if c == 1:
                    for hd in range(HEADS):
                        evacuated(pe, SLOT["q", hd])
                for hd in range(HEADS):
                    for m in range(HV // P):
                        k = hd * (HV // P) + m
                        last = mm(ps[:, n % NS, CHUNK * k:CHUNK * (k + 1)],
                                  state[:, c % 2, hd, P * m:P * (m + 1)],
                                  q[:, hd, CHUNK * (c - 1):CHUNK * c], start=True, stop=True)
                last.then_inc(filled_n, 1)

            def head_square_sum(j):
                n = SLOT["hn", j]
                start_slot(n)
                pe.wait_ge(o_sq_summed, j + 1)
                for hd in range(HEADS):
                    last = mm(ps[:, n % NS, hd:hd + 1], o_sq[:, 0, hd, :], ones_v[:, 0:1], start=True,
                              stop=True)
                last.then_inc(filled_n, 1)

            def head_spread(j):
                n = SLOT["hb", j]
                start_slot(n)
                pe.wait_ge(diag_set, j + 1)
                mm(ps[:, n % NS, 0:SEQ], ones_1[:, :], head_diag.rearrange("p h t -> p (h t)"),
                   start=True, stop=True).then_inc(filled_n, 1)

            for hd in range(HEADS):
                project_k(hd)
                if hd:
                    flip_k(hd - 1)
            project_q(0)
            flip_k(HEADS - 1)
            for c in range(3):
                project_q(c + 1)
                chunk_kv(c)
            chunk_o(1)
            for i in range(KD - 2):
                project(SLOT["g", i], 2 * B_G + i, FRAMES,
                        middle=(lambda: head_square_sum(i // 2)) if i % 2 else None)
                chunk_o(i + 2)
                chunk_kv(i + 3)
                if i % 2:
                    head_spread(i // 2)
            project(SLOT["g", KD - 2], 2 * B_G + KD - 2, FRAMES, middle=lambda: chunk_o(NCH - 1), at=2)
            head_square_sum(TT - 1)
            project(SLOT["g", KD - 1], 2 * B_G + KD - 1, FRAMES, middle=lambda: head_spread(TT - 1), at=2)

            def gated_wait(k):
                pe.wait_ge(o_lo_ready, max(n for n, part in enumerate(GATE_PARTS)
                                           if part[0] <= k < part[1]) + 1)

            for k in range(KD):
                w = 2 * B_OUT1 + k
                pe.wait_ge(w_lo_ready, w + 1)
                exact(SLOT["out1", k], whalf(w), lambda j: (gated_hi[:, j, :], gated_lo[:, j, :]), KD,
                      FRAMES, gated_wait if k == 0 else None, origin=META)
            ffn_all(1, FRAMES)

            def end(i, k):
                w = 2 * NB - KD + k
                pe.wait_ge(w_lo_ready, w + 1)
                exact(SLOT["end", i, k], whalf(w), acts, KD, HALVES[i])

            def flip_half(k, i):
                n = SLOT["y", k, i]
                start_slot(n)
                pe.wait_ge(hg_ready, k + 1 + 2 * i)
                for j in range(2):
                    at = HALVES[i][0] + P * j
                    last = flip(ps[:, n % NS, P * j:P * (j + 1)], relu[:, k % 2, at:at + P])
                last.then_inc(filled_n, 1)

            def tstat_half(i):
                n = SLOT["tstat", 4, i]
                start_slot(n)
                pe.wait_ge(sq_sum_ready, 4 * KD + 2 * i)
                for j in range(2):
                    at = HALVES[i][0] + P * j
                    last = mm(ps[:, n % NS, j:j + 1], sq_sum[:, at:at + P], ones_d[:, 0:1], start=True,
                              stop=True)
                last.then_inc(filled_n, 1)

            end(0, KD - 2)
            flip_y(KD - 3)
            end(0, KD - 1)
            flip_half(KD - 2, 0)
            end(1, KD - 2)
            tstat_half(0)
            flip_half(KD - 1, 0)
            end(1, KD - 1)
            flip_half(KD - 2, 1)
            tstat_half(1)
            flip_half(KD - 1, 1)


_INS = ["x", "meta_tokens", "mix_norm_g", "ffn_norm_g", "ffn_w1", "ffn_w2", "cp_w_in", "cp_conv_w",
        "cp_conv_b", "cp_ln_g", "cp_ln_b", "cp_pool_w", "cp_pool_scale", "cp_w_out", "gla_w_in",
        "gla_gate_w2", "gla_gate_b", "gla_head_g", "gla_w_out", "final_norm_g"]


def kernel(**inputs):
    import numpy as _np
    import concourse.bacc as _bacc
    from concourse import mybir as _mybir
    from concourse.bass_utils import run_bass_kernel_spmd as _run

    nc = _bacc.Bacc("TRN2", target_bir_lowering=False, num_devices=1)
    arrays, args = {}, []
    for name in _INS:
        a = _np.ascontiguousarray(inputs[name])
        arrays[f"in_{name}_dram"] = a
        args.append(nc.dram_tensor(f"in_{name}_dram", a.shape, _mybir.dt.from_np(a.dtype),
                                   kind="ExternalInput").ap())
    shape = inputs["x"].shape
    args.append(nc.dram_tensor("out_dram", shape, _mybir.dt.float32, kind="ExternalOutput").ap())
    build_trunk(nc, *args)
    r = _run(nc, [arrays], core_ids=[0])
    return r.results[0]["out_dram"]
```
